# Optimizing a Trainium2 kernel written in Bass

```python
import math
import jax, jax.numpy as jnp
from jax import lax
import numpy as np

D_MODEL = 1024
BATCH = 1
SEQ = 256
DEPTH = 2
DEC_BATCH = 8
DEC_SEQ = 4
PAST_LEN = 2048
PAGE_SIZE = 128

DN_HEADS = 6
DN_DK = 64
DN_DV = 64
DN_QK = DN_HEADS * DN_DK
DN_W = DN_HEADS * DN_DV
DN_CONV = 2 * DN_QK + DN_W
CONV_W = 4
RW_HEADS = 6
RW_N = 64
RW_W = RW_HEADS * RW_N
RW_DECAY_R = 64
RW_AAA_R = 64
RW_GATE_R = 160
RT_HEADS = 4
RT_DK = 32
RT_DV = 64
RT_QK = RT_HEADS * RT_DK
RT_W = RT_HEADS * RT_DV
MIX_W = DN_W + RW_W + RT_W
CHUNK = 64
ROPE_BASE = 10000.0
D_FF = 2816
N_EXP = 8
TOP_K = 2
D_EXP = 3584
N_DENSE = (DEPTH + 1) // 2
N_MOE = DEPTH // 2
NORM_EPS = 1e-6
RW_GN_EPS = 64e-5
RT_GN_EPS = 1e-5

DN_SIZES = (DN_CONV, DN_W, DN_HEADS, DN_HEADS)
RW_SIZES = (RW_W, RW_W, RW_W, RW_DECAY_R, RW_AAA_R, RW_GATE_R)
RT_SIZES = (RT_QK, RT_QK, RT_W, RT_W)
DN_P = sum(DN_SIZES)
RW_P = sum(RW_SIZES)
RT_P = sum(RT_SIZES)
P_IN = DN_P + RW_P + RT_P

kernel_name = 'hybrid_deltanet_rwkv7_retention_step'

def _split(z, sizes):
    idx = [int(i) for i in np.cumsum(sizes)[:-1]]
    return jnp.split(z, idx, axis=-1)

def _rmsnorm(x, g):
    xf = x.astype(jnp.float32)
    y = xf * lax.rsqrt(jnp.mean(xf * xf, axis=-1, keepdims=True) + NORM_EPS)
    return (y * g.astype(jnp.float32)).astype(x.dtype)

def _l2norm(x):
    return x * lax.rsqrt(jnp.sum(x * x, axis=-1, keepdims=True) + 1e-6)

def _head_groupnorm(y, eps):
    d = y - jnp.mean(y, axis=-1, keepdims=True)
    return d * lax.rsqrt(jnp.mean(d * d, axis=-1, keepdims=True) + eps)

def _to_chunks(t, n, c):
    return jnp.moveaxis(t.reshape((t.shape[0], n, c) + t.shape[2:]), 3, 1)

def _from_chunks(t):
    b, h, n, c = t.shape[:4]
    return jnp.transpose(t, (0, 2, 3, 1, 4)).reshape(b, n * c, h, t.shape[-1])

def _rotary(x, pos0):
    t_len, d = x.shape[1], x.shape[-1]
    half = d // 2
    inv = ROPE_BASE ** (-jnp.arange(half, dtype=jnp.float32) / half)
    ang = (pos0 + jnp.arange(t_len, dtype=jnp.float32))[:, None] * inv[None, :]
    cos = jnp.cos(ang)[None, :, None, :]
    sin = jnp.sin(ang)[None, :, None, :]
    x1, x2 = x[..., :half], x[..., half:]
    return jnp.concatenate([x1 * cos - x2 * sin, x1 * sin + x2 * cos], axis=-1)

def _chunk_gated_delta(q, k, v, g, beta, s0):
    t_len = q.shape[1]
    c = math.gcd(CHUNK, t_len)
    n = t_len // c
    q, k, v, g, beta = (_to_chunks(t, n, c) for t in (q, k, v, g, beta))
    gc = jnp.cumsum(g, axis=-1)
    causal = jnp.tril(jnp.ones((c, c), dtype=bool))
    strict = jnp.tril(jnp.ones((c, c), dtype=bool), -1)
    dmask = jnp.exp(jnp.where(causal, gc[..., :, None] - gc[..., None, :], -jnp.inf))
    kb = k * beta[..., None]
    amat = jnp.where(strict, jnp.einsum('bhnid,bhnjd->bhnij', kb, k) * dmask, 0.0)
    eye = jnp.eye(c, dtype=amat.dtype)
    tmat = lax.linalg.triangular_solve(amat + eye, jnp.broadcast_to(eye, amat.shape),
                                       left_side=True, lower=True, unit_diagonal=True)
    u0 = jnp.einsum('bhnij,bhnje->bhnie', tmat, v * beta[..., None])
    kcd = jnp.einsum('bhnij,bhnjd->bhnid', tmat, kb * jnp.exp(gc)[..., None])
    qk = jnp.einsum('bhnid,bhnjd->bhnij', q, k) * dmask
    q_dec = q * jnp.exp(gc)[..., None]
    k_dec = k * jnp.exp(gc[..., -1:] - gc)[..., None]
    g_last = jnp.exp(gc[..., -1])

    def step(s, xs):
        u0_n, kcd_n, qk_n, qd_n, kd_n, gl_n = xs
        u = u0_n - jnp.einsum('bhcd,bhde->bhce', kcd_n, s)
        o = jnp.einsum('bhcd,bhde->bhce', qd_n, s) + jnp.einsum('bhij,bhje->bhie', qk_n, u)
        s = s * gl_n[..., None, None] + jnp.einsum('bhcd,bhce->bhde', kd_n, u)
        return s, o

    xs = tuple(jnp.moveaxis(t, 2, 0) for t in (u0, kcd, qk, q_dec, k_dec, g_last))
    s, o = lax.scan(step, s0, xs)
    return _from_chunks(jnp.moveaxis(o, 0, 2)), s

def _delta_group(zdn, conv_buf, s0, conv_w, a_log, dt_bias, norm_w):
    b, t_len, _ = zdn.shape
    qkv, zg, a_in, b_in = _split(zdn, DN_SIZES)
    xpad = jnp.concatenate([conv_buf.astype(qkv.dtype), qkv], axis=1)
    conv = jax.nn.silu(sum(xpad[:, j:j + t_len] * conv_w[j] for j in range(CONV_W)))
    new_buf = xpad[:, t_len:]
    q, k, v = _split(conv.astype(jnp.float32), (DN_QK, DN_QK, DN_W))
    q = _l2norm(q.reshape(b, t_len, DN_HEADS, DN_DK)) * DN_DK ** -0.5
    k = _l2norm(k.reshape(b, t_len, DN_HEADS, DN_DK))
    v = v.reshape(b, t_len, DN_HEADS, DN_DV)
    beta = jax.nn.sigmoid(b_in.astype(jnp.float32))
    g = -jnp.exp(a_log.astype(jnp.float32)) * jax.nn.softplus(a_in.astype(jnp.float32) + dt_bias)
    o, s = _chunk_gated_delta(q, k, v, g, beta, s0.astype(jnp.float32))
    o = o * lax.rsqrt(jnp.mean(o * o, axis=-1, keepdims=True) + NORM_EPS) * norm_w
    o = o * jax.nn.silu(zg.astype(jnp.float32).reshape(b, t_len, DN_HEADS, DN_DV))
    return o.reshape(b, t_len, DN_W).astype(zdn.dtype), new_buf, s.astype(zdn.dtype)

def _rwkv7_scan(r, w, k, v, a, bb, s0):
    def step(s, xs):
        r_t, w_t, k_t, v_t, a_t, b_t = xs
        sa = jnp.einsum('bhvk,bhk->bhv', s, a_t)
        s = s * w_t[:, :, None, :] + sa[..., None] * b_t[:, :, None, :] + v_t[..., None] * k_t[:, :, None, :]
        return s, jnp.einsum('bhvk,bhk->bhv', s, r_t)

    xs = tuple(jnp.moveaxis(t, 1, 0) for t in (r, w, k, v, a, bb))
    s, y = lax.scan(step, s0, xs)
    return jnp.moveaxis(y, 0, 1), s

def _rwkv_group(zrw, shift_prev, s0, mu, w0, w2, a0, a2, g2, k_k, k_a, r_k, ln_g, ln_b):
    b, t_len, _ = zrw.shape
    prev = jnp.concatenate([shift_prev[:, None].astype(zrw.dtype), zrw[:, :-1]], axis=1)
    zs = zrw + (prev - zrw) * mu
    new_shift = zrw[:, -1]
    r, k, v, wl, al, gl = (t.astype(jnp.float32) for t in _split(zs, RW_SIZES))
    w = -jax.nn.softplus(-(w0 + jnp.tanh(wl) @ w2)) - 0.5
    a = jax.nn.sigmoid(a0 + al @ a2)
    g = jax.nn.sigmoid(gl) @ g2
    hd = lambda t: t.reshape(b, t_len, RW_HEADS, RW_N)
    kk = _l2norm(hd(k * k_k))
    k = k * (1.0 + (a - 1.0) * k_a)
    r_h, k_h, v_h, a_h = hd(r), hd(k), hd(v), hd(a)
    decay = jnp.exp(-jnp.exp(hd(w)))
    y, s = _rwkv7_scan(r_h, decay, k_h, v_h, -kk, kk * a_h, s0.astype(jnp.float32))
    y = _head_groupnorm(y, RW_GN_EPS).reshape(b, t_len, RW_W) * ln_g + ln_b
    bonus = jnp.sum(r_h * k_h * r_k, axis=-1, keepdims=True) * v_h
    y = (y + bonus.reshape(b, t_len, RW_W)) * g
    return y.astype(zrw.dtype), new_shift, s.astype(zrw.dtype)

def _chunk_retention(q, k, v, r0):
    t_len, n_heads = q.shape[1], q.shape[2]
    c = math.gcd(CHUNK, t_len)
    n = t_len // c
    q, k, v = (_to_chunks(t, n, c) for t in (q, k, v))
    lg = jnp.log1p(-jnp.exp2(-5.0 - jnp.arange(n_heads, dtype=jnp.float32)))
    idx = jnp.arange(c, dtype=jnp.float32)
    causal = jnp.tril(jnp.ones((c, c), dtype=bool))
    dmask = jnp.exp(jnp.where(causal, (idx[:, None] - idx[None, :]) * lg[:, None, None], -jnp.inf))
    inner = jnp.einsum('bhnij,bhnje->bhnie',
                       jnp.einsum('bhnid,bhnjd->bhnij', q, k) * dmask[None, :, None], v)
    q_dec = q * jnp.exp((idx + 1.0) * lg[:, None])[None, :, None, :, None]
    k_dec = k * jnp.exp((c - 1.0 - idx) * lg[:, None])[None, :, None, :, None]
    kv = jnp.einsum('bhncd,bhnce->bhnde', k_dec, v)
    g_chunk = jnp.exp(c * lg)[None, :, None, None]

    def step(rs, xs):
        qd_n, kv_n = xs
        return rs * g_chunk + kv_n, jnp.einsum('bhcd,bhde->bhce', qd_n, rs)

    rs, cross = lax.scan(step, r0, (jnp.moveaxis(q_dec, 2, 0), jnp.moveaxis(kv, 2, 0)))
    return _from_chunks(inner + jnp.moveaxis(cross, 0, 2)), rs

def _retention_group(zrt, s0, ln_g, pos0):
    b, t_len, _ = zrt.shape
    q, k, v, gate = (t.astype(jnp.float32) for t in _split(zrt, RT_SIZES))
    q = _rotary(q.reshape(b, t_len, RT_HEADS, RT_DK), pos0)
    k = _rotary(k.reshape(b, t_len, RT_HEADS, RT_DK), pos0) * RT_DK ** -0.5
    v = v.reshape(b, t_len, RT_HEADS, RT_DV)
    o, s = _chunk_retention(q, k, v, s0.astype(jnp.float32))
    o = _head_groupnorm(o, RT_GN_EPS).reshape(b, t_len, RT_W) * ln_g * jax.nn.silu(gate)
    return o.astype(zrt.dtype), s.astype(zrt.dtype)

def _swiglu(h, w1, w3, w2):
    return (jax.nn.silu(h @ w1) * (h @ w3)) @ w2

def _moe(h, router, w1, w3, w2):
    logits = jnp.einsum('btd,de->bte', h, router).astype(jnp.float32)
    top_v, top_i = lax.top_k(logits, TOP_K)
    gates = jax.nn.softmax(top_v, axis=-1)
    combine = jnp.einsum('btk,btke->bte', gates,
                         jax.nn.one_hot(top_i, N_EXP, dtype=jnp.float32)).astype(h.dtype)
    y = jnp.zeros_like(h)
    for e in range(N_EXP):
        y = y + combine[..., e:e + 1] * _swiglu(h, w1[e], w3[e], w2[e])
    return y

def _trunk(x, conv_buf, s_dn, shift, s_rw, s_rt, pos0, W):
    convs, dns, shifts, rws, rts = [], [], [], [], []
    for l in range(DEPTH):
        h = _rmsnorm(x, W['ln_mix'][l])
        z = h @ W['w_in'][l]
        zdn, zrw, zrt = _split(z, (DN_P, RW_P, RT_P))
        o_dn, nb, nsd = _delta_group(zdn, conv_buf[l], s_dn[l], W['dn_conv'][l], W['dn_a_log'][l],
                                     W['dn_dt_bias'][l], W['dn_norm'][l])
        o_rw, nsh, nsr = _rwkv_group(zrw, shift[l], s_rw[l], W['rw_mu'][l], W['rw_w0'][l], W['rw_w2'][l],
                                     W['rw_a0'][l], W['rw_a2'][l], W['rw_g2'][l], W['rw_kk'][l],
                                     W['rw_ka'][l], W['rw_rk'][l], W['rw_ln_g'][l], W['rw_ln_b'][l])
        o_rt, nst = _retention_group(zrt, s_rt[l], W['rt_ln'][l], pos0)
        x = x + jnp.concatenate([o_dn, o_rw, o_rt], axis=-1) @ W['w_out'][l]
        h = _rmsnorm(x, W['ln_ffn'][l])
        if l % 2 == 0:
            x = x + _swiglu(h, W['ffn_w1'][l // 2], W['ffn_w3'][l // 2], W['ffn_w2'][l // 2])
        else:
            x = x + _moe(h, W['moe_router'][l // 2], W['moe_w1'][l // 2], W['moe_w3'][l // 2], W['moe_w2'][l // 2])
        convs.append(nb)
        dns.append(nsd)
        shifts.append(nsh)
        rws.append(nsr)
        rts.append(nst)
    y = _rmsnorm(x, W['ln_final'])
    return (y, jnp.stack(convs), jnp.stack(dns), jnp.stack(shifts), jnp.stack(rws), jnp.stack(rts))

def setup_inputs(seed: int = 0) -> dict:
    key = jax.random.key(seed)
    ks = iter(jax.random.split(key, 48))
    nrm = lambda shape, s: s * jax.random.normal(next(ks), shape, jnp.float32)
    unif = lambda shape, lo, hi: jax.random.uniform(next(ks), shape, jnp.float32, lo, hi)
    dt = jnp.exp(unif((DEPTH, DN_HEADS), math.log(1e-3), math.log(1e-1)))
    return {
        'x_prompt': nrm((BATCH, SEQ, D_MODEL), 1.0),
        'x_sample': nrm((DEC_BATCH, DEC_SEQ, D_MODEL), 1.0),
        'state_dn_conv': nrm((DEPTH, DEC_BATCH, CONV_W - 1, DN_CONV), 1.0),
        'state_dn': nrm((DEPTH, DEC_BATCH, DN_HEADS, DN_DK, DN_DV), 0.3),
        'state_rw_shift': nrm((DEPTH, DEC_BATCH, RW_P), 1.0),
        'state_rw': nrm((DEPTH, DEC_BATCH, RW_HEADS, RW_N, RW_N), 0.3),
        'state_rt': nrm((DEPTH, DEC_BATCH, RT_HEADS, RT_DK, RT_DV), 0.3),
        'ln_mix': 1.0 + nrm((DEPTH, D_MODEL), 0.02),
        'w_in': nrm((DEPTH, D_MODEL, P_IN), D_MODEL ** -0.5),
        'dn_conv': nrm((DEPTH, CONV_W, DN_CONV), CONV_W ** -0.5),
        'dn_a_log': jnp.log(unif((DEPTH, DN_HEADS), 1.0, 16.0)),
        'dn_dt_bias': dt + jnp.log(-jnp.expm1(-dt)),
        'dn_norm': 1.0 + nrm((DEPTH, DN_DV), 0.02),
        'rw_mu': unif((DEPTH, RW_P), 0.0, 1.0),
        'rw_w0': jnp.linspace(-6.0, -1.0, RW_W, dtype=jnp.float32)[None, :] + nrm((DEPTH, RW_W), 0.1),
        'rw_w2': nrm((DEPTH, RW_DECAY_R, RW_W), 0.5 * RW_DECAY_R ** -0.5),
        'rw_a0': nrm((DEPTH, RW_W), 0.1),
        'rw_a2': nrm((DEPTH, RW_AAA_R, RW_W), 0.5 * RW_AAA_R ** -0.5),
        'rw_g2': nrm((DEPTH, RW_GATE_R, RW_W), RW_GATE_R ** -0.5),
        'rw_kk': 0.85 + nrm((DEPTH, RW_W), 0.02),
        'rw_ka': 1.0 + nrm((DEPTH, RW_W), 0.02),
        'rw_rk': nrm((DEPTH, RW_HEADS, RW_N), 0.1),
        'rw_ln_g': 1.0 + nrm((DEPTH, RW_W), 0.02),
        'rw_ln_b': nrm((DEPTH, RW_W), 0.02),
        'rt_ln': 1.0 + nrm((DEPTH, RT_W), 0.02),
        'w_out': nrm((DEPTH, MIX_W, D_MODEL), MIX_W ** -0.5),
        'ln_ffn': 1.0 + nrm((DEPTH, D_MODEL), 0.02),
        'ffn_w1': nrm((N_DENSE, D_MODEL, D_FF), D_MODEL ** -0.5),
        'ffn_w3': nrm((N_DENSE, D_MODEL, D_FF), D_MODEL ** -0.5),
        'ffn_w2': nrm((N_DENSE, D_FF, D_MODEL), D_FF ** -0.5),
        'moe_router': nrm((N_MOE, D_MODEL, N_EXP), D_MODEL ** -0.5),
        'moe_w1': nrm((N_MOE, N_EXP, D_MODEL, D_EXP), D_MODEL ** -0.5),
        'moe_w3': nrm((N_MOE, N_EXP, D_MODEL, D_EXP), D_MODEL ** -0.5),
        'moe_w2': nrm((N_MOE, N_EXP, D_EXP, D_MODEL), D_EXP ** -0.5),
        'ln_final': 1.0 + nrm((D_MODEL,), 0.02),
    }

def reference(x_prompt, x_sample, state_dn_conv, state_dn, state_rw_shift, state_rw, state_rt,
              ln_mix, w_in, dn_conv, dn_a_log, dn_dt_bias, dn_norm,
              rw_mu, rw_w0, rw_w2, rw_a0, rw_a2, rw_g2, rw_kk, rw_ka, rw_rk, rw_ln_g, rw_ln_b,
              rt_ln, w_out, ln_ffn, ffn_w1, ffn_w3, ffn_w2,
              moe_router, moe_w1, moe_w3, moe_w2, ln_final):
    W = dict(ln_mix=ln_mix, w_in=w_in, dn_conv=dn_conv, dn_a_log=dn_a_log, dn_dt_bias=dn_dt_bias,
             dn_norm=dn_norm, rw_mu=rw_mu, rw_w0=rw_w0, rw_w2=rw_w2, rw_a0=rw_a0, rw_a2=rw_a2,
             rw_g2=rw_g2, rw_kk=rw_kk, rw_ka=rw_ka, rw_rk=rw_rk, rw_ln_g=rw_ln_g, rw_ln_b=rw_ln_b,
             rt_ln=rt_ln, w_out=w_out, ln_ffn=ln_ffn, ffn_w1=ffn_w1, ffn_w3=ffn_w3, ffn_w2=ffn_w2,
             moe_router=moe_router, moe_w1=moe_w1, moe_w3=moe_w3, moe_w2=moe_w2, ln_final=ln_final)
    bp, dt = x_prompt.shape[0], x_prompt.dtype
    z_conv = jnp.zeros((DEPTH, bp, CONV_W - 1, DN_CONV), dt)
    z_dn = jnp.zeros((DEPTH, bp, DN_HEADS, DN_DK, DN_DV), dt)
    z_shift = jnp.zeros((DEPTH, bp, RW_P), dt)
    z_rw = jnp.zeros((DEPTH, bp, RW_HEADS, RW_N, RW_N), dt)
    z_rt = jnp.zeros((DEPTH, bp, RT_HEADS, RT_DK, RT_DV), dt)
    y_prompt, p_conv, p_dn, p_shift, p_rw, p_rt = _trunk(x_prompt, z_conv, z_dn, z_shift, z_rw, z_rt, 0, W)
    y_sample, s_conv, s_dn, s_shift, s_rw, s_rt = _trunk(x_sample, state_dn_conv, state_dn, state_rw_shift,
                                                         state_rw, state_rt, PAST_LEN, W)
    return (y_prompt, y_sample, p_conv, p_dn, p_shift, p_rw, p_rt, s_conv, s_dn, s_shift, s_rw, s_rt)


_drawn_inputs = setup_inputs


def setup_inputs(seed=0):
    import zlib

    import numpy as np

    out = dict(_drawn_inputs(seed))
    spreads = {}
    factors = {}
    for name, (base, spread) in spreads.items():
        noise = np.random.default_rng([zlib.crc32(name.encode()), seed]).standard_normal(out[name].shape)
        drawn = base * np.exp(spread * noise) if base else spread * noise
        out[name] = __import__('jax').numpy.asarray(drawn.astype(out[name].dtype))
    for name, factor in factors.items():
        out[name] = (out[name] * factor).astype(out[name].dtype)
    return out
```

```python
import math
from contextlib import ExitStack

import numpy as np

import concourse.bass as bass
from concourse import mybir

F32 = mybir.dt.float32
ALU = mybir.AluOpType
ACT = mybir.ActivationFunctionType
AX = mybir.AxisListType
MUL, ADD, SUB = ALU.mult, ALU.add, ALU.subtract

P = 128
D = 1024
KD = D // P
SEQ, NB, DS = 256, 8, 4
NT = SEQ + NB * DS
DEPTH = 2
TILES = [(0, 128), (128, 128), (256, 32)]
CHUNK = 64
H = 6
HD = 64
CONV_W = 4
DN_QKV = 9
P_IN = 3756
RT_H, RT_K = 4, 32
D_FF, N_EXP, D_EXP = 2816, 8, 3584
FB = 256
FT = FB // P
FFN_BLOCKS = D_FF // FB
EXP_BLOCKS = D_EXP // FB
MOE_BLOCKS = N_EXP * EXP_BLOCKS
SLOT = 3 * KD * FB
SLOTS = 4
UNROLL = 4
PADC = CONV_W - 1
ZC = PADC + SEQ + NB * (PADC + DS)
ZR = 1 + SEQ + NB * (1 + DS)
RW_DECAY = math.exp(-0.5)
NORM_EPS, RW_GN_EPS, RT_GN_EPS, L2_EPS = 1e-6, 64e-5, 1e-5, 1e-6
PAST_LEN = 2048
NEG = -1e30

DN0, RW0, RT0 = 0, 1548, 2988
ZTILES = [("conv", m, DN0 + P * m, P) for m in range(9)] + [("zg", m, 1152 + P * m, P) for m in range(3)]
ZTILES += [("rw", m, RW0 + P * m, P) for m in range(11)] + [("rw", 11, RW0 + 11 * P, 32)]
ZTILES += [("rt", m, RT0 + P * m, P) for m in range(6)]
WSLOT = KD * 384
WIN_LOADS = [(0, 384), (384, 768), (768, 1152), (1152, 1536), (1536, 1804), (1804, 2188), (2188, 2572), (2572, 2956),
             (2956, 3244), (3244, 3628), (3628, 3756)]
WOUT_LOADS = [(0, 384), (384, 768), (768, 1024)]
AB_LOAD = 4
MIX_LOADS = len(WIN_LOADS) + len(WOUT_LOADS)

PCOLS = [("ln_mix", 8), ("ln_ffn", 8), ("conv", 36), ("dn_norm", 1), ("mu", 12), ("a0", 3), ("kk", 3),
         ("ka", 3), ("rk", 3), ("ln_g", 3), ("ln_b", 3), ("rt_ln", 2), ("a_log", 6), ("dt", 6)]
CCOLS = [("ident", 128), ("tri", 384), ("tri_s", 96), ("neg", 128), ("neg_s", 32), ("level", 6 * 128),
         ("level0_t", 128), ("ones64", 128), ("mean64", 128), ("bmask", 8), ("rot", 128), ("cos", 2 * NT), ("qdec", 32), ("kdec", NT),
         ("g4", 1), ("rt_mask", 4 * SEQ), ("rt_mask_s", 128), ("rank", 8), ("ones", 128)]


def columns(cols):
    at, out = 0, {}
    for name, n in cols:
        out[name] = (at, n)
        at += n
    return out, at


PAT, PN = columns(PCOLS)
CAT, CN = columns(CCOLS)


def constants():
    c = np.zeros((P, CN), np.float64)

    def put(name, a, rows=P):
        at, n = CAT[name]
        c[:rows, at:at + n] = np.asarray(a).reshape(rows, n)

    i = np.arange(P)
    put("ident", np.eye(P))
    for name, size, n in (("tri", CHUNK, P), ("tri_s", DS, 32)):
        j, k = i[:n, None], i[None, :n]
        same = j // size == k // size
        put(name, np.concatenate([same & (j <= k), same & (j < k), same & (j > k)], 1), n)
        put("neg" + name[3:], np.where(same & (j <= k), 0.0, NEG), n)
    levels = []
    for s in (1, 2, 4, 8, 16, 32):
        a, b = i[:, None], i[None, :]
        levels.append(-1.0 * ((a // (2 * s) == b // (2 * s)) & (a % (2 * s) >= s) & (b % (2 * s) < s)))
    put("level", np.concatenate(levels, 1))
    put("level0_t", levels[0].T)
    blocks = (i[:, None] // HD == i[None, :] // HD) * 1.0
    put("ones64", blocks)
    put("mean64", blocks / HD)
    put("bmask", i[:32, None] // DS == np.arange(NB)[None], 32)
    rot = np.zeros((P, P))
    half = RT_K // 2
    for x in range(P):
        if x % RT_K < half:
            rot[x + half, x] = -1.0
        else:
            rot[x - half, x] = 1.0
    put("rot", rot)
    inv = (np.float32(10000.0) ** (-np.arange(half, dtype=np.float32) / np.float32(half))).astype(np.float32)
    pos = np.concatenate([np.arange(SEQ), np.tile(PAST_LEN + np.arange(DS), NB)]).astype(np.float32)
    ang = (pos[None, :] * inv[i % half][:, None]).astype(np.float32).astype(np.float64)
    put("cos", np.concatenate([np.cos(ang), np.sin(ang)], 1))
    lg = np.log1p(-np.exp2(-5.0 - np.arange(RT_H)))
    lgp = lg[i // RT_K][:, None]
    tok = np.tile(np.arange(DS), NB)[None]
    put("qdec", np.exp((tok + 1) * lgp))
    put("kdec", RT_K ** -0.5 * np.exp(np.concatenate([SEQ - 1 - np.arange(SEQ)[None] + 0 * lgp, DS - 1 - tok + 0 * lgp], 1) * lgp))
    put("g4", np.exp(DS * lgp))
    m = []
    for h in range(RT_H):
        d = np.arange(SEQ)[None] - i[:, None]
        m.append(RT_K ** -0.5 * np.where(d >= 0, np.exp(np.maximum(d, 0) * lg[h]), 0.0))
    put("rt_mask", np.concatenate(m, 1))
    j, k = i[:32, None], i[None, :32]
    put("rt_mask_s", RT_K ** -0.5 * np.concatenate([np.where((j // DS == k // DS) & (j <= k), np.exp(np.maximum(k - j, 0) * lg[h]), 0.0)
                                     for h in range(RT_H)], 1), 32)
    put("rank", np.tile(N_EXP - np.arange(N_EXP), (P, 1)))
    put("ones", np.ones((P, P)))
    return c.astype(np.float32)


def trunk(nc, x_in, consts, pcol, rw_w2a2, rw_g2, rw_w0, ln_final, router, w_in, w_out, ffn, moe,
          conv_state, shift_state, dn_state, rw_state, rt_state,
          y_out, conv_out, shift_out, p_dn, p_rw, p_rt, s_dn, s_rw, s_rt):
    with ExitStack() as ctx:
        def sb(name, *free, rows=P):
            return ctx.enter_context(nc.sbuf_tensor(name, [rows, *free], F32))

        class Signal:

            def __init__(self, name, per, step=1):
                self.sem, self.per, self.step = ctx.enter_context(nc.semaphore(name)), per, step

            def at(self, layer, unit):
                assert 0 <= unit < self.per, (self.sem, unit)
                return self.step * (layer * self.per + unit + 1)

        def wait(eng, signal, layer, unit):
            eng.wait_ge(signal.sem, signal.at(layer, unit))

        ring = sb("ring", SLOTS * SLOT)
        wslot = [ring[:, s * WSLOT:(s + 1) * WSLOT] for s in range(2)]
        slot = [ring[:, s * SLOT:(s + 1) * SLOT] for s in range(SLOTS)]
        mix_at = [2 * WSLOT]

        def in_ring(*free, at=None):
            n = int(np.prod(free))
            a = mix_at[0] if at is None else at
            if at is None:
                mix_at[0] += n
            assert a + n <= SLOTS * SLOT, (a, n)
            names = "abcd"[:len(free)]
            if len(free) == 1:
                return ring[:, a:a + n]
            return ring[:, a:a + n].rearrange(f"p ({' '.join(names)}) -> p {' '.join(names)}", **dict(zip(names, free)))

        zc_at = mix_at[0]
        zc = in_ring(9, ZC)
        zr = in_ring(12, ZR)
        Q = in_ring(3, 4, NT, at=zc_at)
        UX = in_ring(4, NB, HD, at=zc_at + 12 * NT)
        assert 12 * NT + 4 * NB * HD <= 9 * ZC + 11 * ZR
        rtz = in_ring(6, NT)
        tmp3 = in_ring(3, ZC)
        R = in_ring(H, 4, P)
        nat = in_ring(4, H, HD)
        E3 = in_ring(3, 3, P)
        keys = in_ring(2, 3, P)

        X = sb("X", 3, D)
        hT = sb("hT", KD, NT)
        C = sb("C", CN)
        PC = sb("PC", DEPTH, PN)
        w2a2 = sb("w2a2", 384)
        g2 = sb("g2", 2, 384)
        w0 = sb("w0", 384, rows=1)
        rt_w = sb("rt_w", KD, N_EXP)
        conv = sb("conv", 9, NT)
        zg = sb("zg", 3, NT)
        zs = sb("zs", 12, NT)
        gate = sb("gate", 3, NT)
        aT = sb("aT", 3, NT)
        bonus = sb("bonus", 3, NT)
        TM = sb("TM", 2, 3, P)
        TT = sb("TT", 2, 3, P)
        XM = sb("XM", 2, 3, P)
        DI = XM
        EI = in_ring(3, P)
        ends = in_ring(2, 3, P)
        sg = in_ring(3, 384)
        U0 = sb("U0", H, HD)
        U = sb("U", H, HD)
        S = sb("S", 2, 3, HD)
        Sr = sb("Sr", DEPTH, HD)
        SS = sb("SS", 3, NB, HD)
        SSr = sb("SSr", NB, HD)
        USO = in_ring(3, 2, 32)
        early = U0[:, :, :].rearrange("p a b -> p (a b)")
        cvs = early[:, 0:216].rearrange("p (a b) -> p a b", a=9)
        shs = early[:, 216:312].rearrange("p (a b) -> p a b", a=12)
        cvo = sb("cvo", 1, 9, 27)
        sho = sb("sho", 1, 12, 9)
        ab = sb("ab", 3, 12)
        dn = sb("dn", 12, 3, H)
        gb8 = sb("gb8", 2, NT, rows=N_EXP)
        gb = gb8[0:H, :, :]
        decay = sb("decay", 3, 12)
        stat = sb("stat", 3, 12)
        EPS = [NORM_EPS, L2_EPS, RW_GN_EPS, RT_GN_EPS, -math.log(HD) / 2]
        eps_cols = sb("eps_cols", len(EPS))
        eps = lambda k: eps_cols[:, k:k + 1]
        small = sb("small", 8, 3, N_EXP)
        hn = [conv[:, 0:4, :].rearrange("p a b -> p (a b)")[:, 0:D], conv[:, 4:8, :].rearrange("p a b -> p (a b)")[:, 0:D]]
        OT = hT
        SQ = R.rearrange("p a b c -> p (a b c)")[:, 0:6 * NT].rearrange("p (a b) -> p a b", b=NT)
        eg, KK = gate, gate
        hid = [zs[:, f, :] for f in range(2)]
        silu_h = zs[:, 2, :]
        comb = zs[:, 3:11, :]
        combT = gb8[:, 0, :]
        pair_sel = bonus[0:H, :, :].rearrange("p a b -> p (a b)")[:, 0:H * HD]
        lnf = ring[:, 0:D]
        junk = zs[:, 0:4, :].rearrange("p a b -> p (a b)")[:, 0:D]
        rt_qd = EI[:, 0, 0:32]
        omka = stat[:, 0, 9:12]

        banks = [ctx.enter_context(nc.psum_tensor(f"bank{b}", [P, 512], F32)) for b in range(8)]

        def cst(name, a=0, n=None, rows=P):
            at, size = CAT[name]
            return C[0:rows, at + a:at + a + (size - a if n is None else n)]

        def par(layer, name, k=0, n=1):
            at = PAT[name][0] + k
            return PC[:, layer, at:at + n]

        def over(a, n, at=1):
            shape = list(a.shape)
            shape.insert(at, n)
            return a.unsqueeze(at).to_broadcast(shape)

        ident = cst("ident")
        tri = [cst("tri"), cst("tri"), cst("tri_s", rows=32)]
        neg = [cst("neg"), cst("neg"), cst("neg_s", rows=32)]
        LEVELS = [6, 6, 2]
        seqs = lambda a: a.rearrange("p m (b s) -> p m b s", b=NB)

        def sig(name, per, step=1):
            return Signal(name, per, step)

        loaded = [sig(f"wslot{s}_loaded", MIX_LOADS // 2, 16) for s in range(2)]
        out_ok = sig("out_columns_added", len(WOUT_LOADS))
        block_loaded = [ctx.enter_context(nc.semaphore(f"block_slot{s}_loaded")) for s in range(SLOTS)]
        bank_full = [ctx.enter_context(nc.semaphore(f"bank{b}_full")) for b in range(8)]
        bank_free = [ctx.enter_context(nc.semaphore(f"bank{b}_free")) for b in range(8)]
        inputs = ctx.enter_context(nc.semaphore("inputs_loaded"))
        stored = sig("outputs_stored", 5, 16)
        lora_loaded = sig("lora_loaded", 3, 16)
        seq_states = sig("conv_shift_states_loaded", 2, 16)
        rt_state_in = sig("rt_state_loaded", 1, 16)
        rt_state_out = sig("rt_state_stored", 1, 16)
        ss_in = sig("sample_state_loaded", 2, 16)
        ss_out = sig("sample_state_stored", 2, 16)
        dve_seq = ctx.enter_context(nc.semaphore("vector_steps"))
        act_seq = ctx.enter_context(nc.semaphore("scalar_steps"))
        ssq_ok = sig("squares_summed", 6)
        rstd_ok = sig("rstd_ready", 6)
        hn_ok = sig("normed", 6)
        hT_ok = sig("hT_ready", 12)
        ab_ok = sig("ab_ready", 1)
        zeroed = sig("pads_zeroed", 1)
        z_ok = sig("z_ready", 30)
        pads_ok = sig("pads_ready", 1)
        conv_ok = sig("conv_summed", 3)
        qkv_ok = sig("qkv_ready", 3)
        cvo_ok = sig("conv_tail_ready", 1)
        sho_ok = sig("shift_tail_ready", 1)
        zs_ok = sig("shifted", 1)
        lora_ok = sig("lora_inputs_ready", 1)
        sg_ok = sig("decay_sigmoid_ready", 3)
        aT_ok = sig("a_ready", 3)
        gT_ok = sig("g_ready", 1)
        beta_ok = sig("beta_ready", 1)
        negA_ok = sig("neg_A_ready", 1)
        dtb_ok = sig("dt_biased", 1)
        sp_ok = sig("softplus_log_ready", 1)
        g_ok = sig("g_log_decay_ready", 1)
        cum_ok = sig("cum_ready", 1)
        gb_ok = sig("g_beta_rows_ready", 1)
        egn_ok = sig("cum_exp_ready", 1)
        sq_ok = sig("qk_squares", 1)
        rn_ok = sig("qk_rnorm", 6)
        eg_ok = sig("eg_ready", 3)
        Q_ok = sig("queries_ready", 1)
        nat_ok = sig("naturals_ready", 3)
        natb_ok = sig("naturals_copied", 3)
        DI_ok = sig("pair_decays", 6)
        R_ok = sig("products_ready", 36)
        T_ok = sig("inverse_ready", 2 * 2 * (6 + 6 + 2))
        XM_ok = sig("masked_ready", 2 * 2 * (6 + 6 + 2))
        XV_ok = sig("av_ready", 3)
        U0_ok = sig("u0_ready", 6)
        W_ok = sig("w_ready", 6)
        U_ok = sig("u_ready", 10)
        O_ok = sig("o_ready", 8)
        Os_ok = sig("sample_o_ready", 2)
        S_ok = sig("state_ready", 8)
        USO_ok = sig("sample_state_read", 2)
        UX_ok = sig("spread_ready", 6)
        SS_ok = sig("sample_state_updated", 2)
        kk_sq = sig("kk_squares", 1)
        kk_rn = sig("kk_rnorm", 3)
        kk_ok = sig("kk_ready", 1)
        rk_ok = sig("rk_products", 1)
        E_ok = sig("rw_decays", 3)
        keys_ok = sig("rw_keys_ready", 3)
        rot_ok = sig("rotated", 1)
        rtk_ok = sig("rt_natural_ready", 3)
        rtR_ok = sig("rt_products", 8)
        rtO_ok = sig("rt_o_ready", 2)
        rtC_ok = sig("rt_cross_ready", 2)
        rtX_ok = sig("rt_spread_ready", 4)
        rtS_ok = sig("rt_state_updated", 1)
        rtSp_ok = sig("rt_prompt_state_ready", 1)
        dev_ok = sig("deviations_ready", 2)
        osq_ok = sig("o_squares_ready", 3)
        orn_ok = sig("o_rnorm_ready", 8)
        cat_ok = sig("mixed_ready", 1)
        X_ok = sig("x_mixed", 1)
        logit_ok = sig("combine_ready", 1)
        cT_ok = sig("combine_rows_ready", 1)
        comb_ok = sig("combine_spread", 1)
        h1_full = ctx.enter_context(nc.semaphore("h1_full"))
        h3_full = ctx.enter_context(nc.semaphore("h3_full"))
        silu_done = ctx.enter_context(nc.semaphore("silu_done"))
        hid_ok = ctx.enter_context(nc.semaphore("hidden_ready"))
        hid_used = ctx.enter_context(nc.semaphore("hidden_used"))
        final_ok = sig("y_ready", 3)
        fss_ok = sig("last_squares_summed", 3)
        frs_ok = sig("last_rstd_ready", 3)
        diff_ok = sig("logit_difference", 1)
        odds_ok = sig("odds_ready", 1)
        weighted = ctx.enter_context(nc.semaphore("silu_weighted"))
        lnf_in = ctx.enter_context(nc.semaphore("last_norm_weights_loaded"))
        y_stored = ctx.enter_context(nc.semaphore("y_stored"))
        eps_ok = ctx.enter_context(nc.semaphore("eps_ready"))

        fills = {}

        def fill(pe, *key):
            b, turn = len(fills) % 8, len(fills) // 8
            assert key not in fills, key
            fills[key] = (b, turn)
            if turn:
                pe.wait_ge(bank_free[b], turn)
            return banks[b], bank_full[b]

        def take(eng, *key):
            b, turn = fills[key]
            eng.wait_ge(bank_full[b], turn + 1)
            return banks[b], bank_free[b]

        def mm(pe, out, lhsT, rhs, start=True, stop=True):
            return nc.tensor.matmul(out, lhsT, rhs, start=start, stop=stop, skip_group_check=True)

        def tr(pe, out, in_):
            n = in_.shape[0]
            return nc.tensor.transpose(out, in_, ident[0:n, 0:n])

        def half(h):
            return slice(64 * (h % 2), 64 * (h % 2) + 64), h // 2

        block = ctx.enter_context(nc.Block())
        N_IN = 5
        FFN_USES = [[len(range(s, FFN_BLOCKS, SLOTS)) for s in range(SLOTS)]]

        @block.tensor
        def _(pe):
            def norm_transposes(l, use):
                for t, (t0, n) in enumerate(TILES):
                    u = use * 3 + t
                    wait(pe, hn_ok, l, u)
                    for part in range(2):
                        b, full = fill(pe, l, "hT", u, part)
                        for q in range(4):
                            k = part * 4 + q
                            i = tr(pe, b[:, q * P:q * P + n], hn[t % 2][0:n, k * P:(k + 1) * P])
                        i.then_inc(full, 1)

            def project(l):
                wait(pe, hT_ok, l, 5)
                tiles = list(enumerate(ZTILES))
                for i, (c0, c1) in enumerate(WIN_LOADS):
                    wait(pe, loaded[i % 2], l, i // 2)
                    w = wslot[i % 2][:, 0:KD * (c1 - c0)].rearrange("p (k c) -> p k c", k=KD)
                    last = None
                    if i == AB_LOAD:
                        b, full = fill(pe, l, "ab")
                        for t, (t0, n) in enumerate(TILES):
                            for k in range(KD):
                                last = mm(pe, b[0:n, t * 12:t * 12 + 12], hT[:, k, t0:t0 + n], w[:, k, 0:12],
                                          start=k == 0, stop=k == KD - 1)
                        last.then_inc(full, 1)
                    while tiles and tiles[0][1][2] < c1:
                        m, (_, _, c, n) = tiles.pop(0)
                        b, full = fill(pe, l, "z", m)
                        for k in range(KD):
                            last = mm(pe, b[0:n, 0:NT], w[:, k, c - c0:c - c0 + n], hT[:, k, :],
                                      start=k == 0, stop=k == KD - 1)
                        last.then_inc(full, 1)

            def lora(l):
                wait(pe, lora_loaded, l, 2)
                wait(pe, lora_ok, l, 0)
                for t, (t0, n) in enumerate(TILES):
                    b, full = fill(pe, l, "y", t)
                    mm(pe, b[0:n, 0:384], cst("ones", 0, n, rows=1), w0[:, :], stop=False)
                    mm(pe, b[0:n, 0:384], zs[0:64, 9, t0:t0 + n], w2a2[0:64, :], start=False).then_inc(full, 1)
                for f in range(3):
                    b, full = fill(pe, l, "a", f)
                    mm(pe, b[:, 0:NT], w2a2[64:128, f * P:(f + 1) * P], zs[64:128, 9, :]).then_inc(full, 1)
                for f in range(3):
                    b, full = fill(pe, l, "g", f)
                    mm(pe, b[:, 0:NT], g2[:, 0, f * P:(f + 1) * P], zs[:, 10, :], stop=False)
                    mm(pe, b[:, 0:NT], g2[0:32, 1, f * P:(f + 1) * P], zs[0:32, 11, :], start=False).then_inc(full, 1)

            def dn_prepare(l):
                wait(pe, sq_ok, l, 0)
                for i in range(6):
                    b, full = fill(pe, l, "dnss", i)
                    mm(pe, b[:, 0:NT], cst("ones64"), SQ[:, i, :]).then_inc(full, 1)
                wait(pe, g_ok, l, 0)
                wait(pe, beta_ok, l, 0)
                b, full = fill(pe, l, "cum")
                for t, (t0, n) in enumerate(TILES):
                    mm(pe, b[0:n, t * 12:t * 12 + 6], tri[t][:, 0:n], dn[0:n, 0, t, :])
                    i = mm(pe, b[0:n, t * 12 + 6:t * 12 + 12], tri[t][:, 2 * n:3 * n], dn[0:n, 0, t, :])
                i.then_inc(full, 1)
                b, full = fill(pe, l, "rows_g")
                for t, (t0, n) in enumerate(TILES):
                    i = mm(pe, b[0:H, t0:t0 + n], dn[0:n, 0, t, :], tri[t][:, 0:n])
                i.then_inc(full, 1)
                b, full = fill(pe, l, "rows_b")
                for t, (t0, n) in enumerate(TILES):
                    i = mm(pe, b[0:H, t0:t0 + n], dn[0:n, 1, t, :], ident[0:n, 0:n])
                i.then_inc(full, 1)
                wait(pe, gb_ok, l, 0)
                for p in range(3):
                    sel = pair_sel[:, p * P:(p + 1) * P]
                    b, full = fill(pe, l, "bc_g", p)
                    mm(pe, b[:, 0:NT], sel, gb[:, 0, :]).then_inc(full, 1)
                    b, full = fill(pe, l, "bc_b", p)
                    mm(pe, b[:, 0:NT], sel, gb[:, 1, :]).then_inc(full, 1)

            def dn_tile(l, t):
                t0, n = TILES[t]
                wait(pe, Q_ok, l, 0)
                for name, m in (("k", 3), ("v", 6)):
                    b, full = fill(pe, l, "dn" + name, t)
                    for p in range(3):
                        i = tr(pe, b[0:n, p * P:(p + 1) * P], conv[:, m + p, t0:t0 + n])
                    i.then_inc(full, 1)
                for g in range(2):
                    b, full = fill(pe, l, "E", t, g)
                    for x in range(3):
                        h = 3 * g + x
                        mm(pe, b[0:n, x * n:(x + 1) * n], ident[0:H, h:h + 1].to_broadcast([H, n]), gb[:, 0, t0:t0 + n], stop=False)
                        i = mm(pe, b[0:n, x * n:(x + 1) * n], ident[0:n, 0:n], neg[t][:, 0:n], start=False)
                    i.then_inc(full, 1)
                    for x in range(3):
                        s, p = half(3 * g + x)
                        b, full = fill(pe, l, 0, "products", t, 3 * g + x)
                        mm(pe, b[0:n, 0:2 * n].rearrange("p (a b) -> p a b", a=2), conv[s, 3 + p, t0:t0 + n],
                           Q[s, p, 0:2, t0:t0 + n]).then_inc(full, 1)

            def rw_prepare(l):
                wait(pe, kk_sq, l, 0)
                for f in range(3):
                    b, full = fill(pe, l, "kss", f)
                    mm(pe, b[:, 0:NT], cst("ones64"), SQ[:, f, :]).then_inc(full, 1)
                wait(pe, rk_ok, l, 0)
                for f in range(3):
                    b, full = fill(pe, l, "bonus", f)
                    mm(pe, b[:, 0:NT], cst("ones64"), SQ[:, 3 + f, :]).then_inc(full, 1)

            def rw_tile(l, t):
                t0, n = TILES[t]
                wait(pe, sg_ok, l, t)
                for f in range(3):
                    b, full = fill(pe, l, "cumw", t, f)
                    mm(pe, b[:, 0:3 * n], sg[0:n, t, f * P:(f + 1) * P], tri[t]).then_inc(full, 1)
                wait(pe, keys_ok, l, t)
                srcs = [Q[:, :, 1, t0:t0 + n], ends[:, 0, :, 0:n], zs[:, 6:9, t0:t0 + n], ends[:, 1, :, 0:n]]
                for k, src in enumerate(srcs):
                    b, full = fill(pe, l, "rwnat", t, k)
                    for p in range(3):
                        i = tr(pe, b[0:n, p * P:(p + 1) * P], src[:, p, :])
                    i.then_inc(full, 1)
                for h in range(H):
                    s, p = half(h)
                    b, full = fill(pe, l, 1, "products", t, h)
                    for k in range(2):
                        i = mm(pe, b[0:n, 2 * k * n:2 * (k + 1) * n].rearrange("p (a b) -> p a b", a=2),
                               keys[s, k, p, 0:n], Q[s, p, 0:2, t0:t0 + n])
                    i.then_inc(full, 1)

            def inverses(l, y, t):
                n = TILES[t][1]
                done = (y * 14 + sum(LEVELS[:t])) * 2
                for g in range(2):
                    wait(pe, R_ok, l, y * 18 + t * 6 + 3 * g + 2)
                    b, full = fill(pe, l, y, "L0", t, g)
                    for x in range(3):
                        i = tr(pe, b[0:n, x * n:(x + 1) * n], R[0:n, 3 * g + x, 1, 0:n])
                    i.then_inc(full, 1)
                for lev in range(1, LEVELS[t]):
                    for g in range(2):
                        wait(pe, T_ok, l, done + (lev - 1) * 2 + g)
                        b, full = fill(pe, l, y, "AT", t, lev, g)
                        for x in range(3):
                            i = mm(pe, b[0:n, x * n:(x + 1) * n], R[0:n, 3 * g + x, 1, 0:n], TM[0:n, g, x, 0:n])
                        i.then_inc(full, 1)
                    for g in range(2):
                        wait(pe, XM_ok, l, done + lev * 2 + g)
                        b, full = fill(pe, l, y, "TX", t, lev, g)
                        for x in range(3):
                            i = mm(pe, b[0:n, x * n:(x + 1) * n], TT[0:n, g, x, 0:n], XM[0:n, g, x, 0:n])
                        i.then_inc(full, 1)
                        b, full = fill(pe, l, y, "XT", t, lev, g)
                        for x in range(3):
                            i = mm(pe, b[0:n, x * n:(x + 1) * n], XM[0:n, g, x, 0:n], TT[0:n, g, x, 0:n])
                        i.then_inc(full, 1)
                for g in range(2):
                    wait(pe, T_ok, l, done + (LEVELS[t] - 1) * 2 + g)

            def chunk_inputs(l, y, t):
                n = TILES[t][1]
                wait(pe, natb_ok if y else nat_ok, l, t)
                if y:
                    b, full = fill(pe, l, "XV", t)
                    for h in range(H):
                        i = mm(pe, b[0:n, h * HD:(h + 1) * HD], R[0:n, h, 3, 0:n], nat[0:n, 2, h, :])
                    i.then_inc(full, 1)
                b, full = fill(pe, l, y, "W", t)
                for h in range(H):
                    s, p = half(h)
                    i = mm(pe, b[s, p * n:(p + 1) * n], nat[0:n, 0, h, :], TT[0:n, h // 3, h % 3, 0:n])
                i.then_inc(full, 1)
                if y:
                    wait(pe, XV_ok, l, t)
                v = U if y else nat[:, 2, :, :]
                b, full = fill(pe, l, y, "U0", t)
                for h in range(H):
                    i = mm(pe, b[0:n, h * HD:(h + 1) * HD], TT[0:n, h // 3, h % 3, 0:n], v[0:n, h, :])
                i.then_inc(full, 1)

            def prompt_chunk(l, y, c):
                t, cc = c // 2, c % 2
                rows = slice(64 * cc, 64 * cc + 64)
                cols = slice(CHUNK * c, CHUNK * (c + 1))
                st = S[:, y, :, :]
                if c:
                    wait(pe, W_ok, l, y * 3 + t)
                    wait(pe, S_ok, l, y * 4 + c - 1)
                    for odd in range(2):
                        b, full = fill(pe, l, y, "WS", c, odd)
                        for p in range(3):
                            s = slice(64 * odd, 64 * odd + 64)
                            i = mm(pe, b[rows, p * HD:(p + 1) * HD], Q[s, p, 3, cols], st[s, p, :])
                        i.then_inc(full, 1)
                wait(pe, U_ok, l, y * 5 + c)
                b, full = fill(pe, l, y, "O", c)
                for h in range(H):
                    s, p = half(h)
                    out = b[s, p * CHUNK:(p + 1) * CHUNK]
                    inner = slice(64 * cc, 64 * cc + 64)
                    if c:
                        mm(pe, out, st[s, p, :], Q[s, p, 0 if y else 2, cols], stop=False)
                    if y:
                        mm(pe, out, nat[:, 2, h, :], R[:, h, 2, inner], start=c == 0, stop=False)
                    i = mm(pe, out, U[:, h, :], R[:, h, 0, inner], start=c == 0 and not y)
                i.then_inc(full, 1)
                b, full = fill(pe, l, y, "S", c)
                for h in range(H):
                    s, p = half(h)
                    out = b[s, p * HD:(p + 1) * HD]
                    if y:
                        mm(pe, out, nat[rows, 3, h, :], nat[rows, 2, h, :], stop=False)
                    i = mm(pe, out, nat[rows, 1, h, :], U[rows, h, :], start=not y)
                i.then_inc(full, 1)

            def sample_chunks(l, y):
                wait(pe, W_ok, l, y * 3 + 2)
                wait(pe, ss_in, l, y)
                b, full = fill(pe, l, y, "SU")
                for h in range(H):
                    s, p = half(h)
                    for q in range(NB):
                        cols = slice(SEQ + DS * q, SEQ + DS * (q + 1))
                        both = Q[s, p, 0:4:3, cols] if y else Q[s, p, 2:4, cols]
                        out = b[s, p * 64:(p + 1) * 64].rearrange("p (a b) -> p a b", a=2)[:, :, DS * q:DS * (q + 1)]
                        i = mm(pe, out, SS[s, p, q, :], both)
                i.then_inc(full, 1)
                wait(pe, USO_ok, l, y)
                b, full = fill(pe, l, y, "SUT")
                for p in range(3):
                    i = tr(pe, b[0:32, p * P:(p + 1) * P], USO[:, p, 1, :])
                i.then_inc(full, 1)
                wait(pe, U_ok, l, y * 5 + 4)
                b, full = fill(pe, l, y, "O", 4)
                for h in range(H):
                    s, p = half(h)
                    out = b[s, p * 32:(p + 1) * 32]
                    if y:
                        mm(pe, out, nat[0:32, 2, h, :], R[0:32, h, 2, 0:32], stop=False)
                    i = mm(pe, out, U[0:32, h, :], R[0:32, h, 0, 0:32], start=not y)
                i.then_inc(full, 1)
                for p in range(3):
                    wait(pe, UX_ok, l, y * 3 + p)
                    b, full = fill(pe, l, y, "SS", p)
                    for q in range(2):
                        h = 2 * p + q
                        s = half(h)[0]
                        flat = lambda k: UX[0:32, k, :, :].rearrange("p a b -> p (a b)")
                        if y:
                            mm(pe, b[s, :], nat[0:32, 3, h, :], flat(2 + q), stop=False)
                        i = mm(pe, b[s, :], nat[0:32, 1, h, :], flat(q), start=not y)
                    i.then_inc(full, 1)

            def retention(l):
                wait(pe, z_ok, l, 29)
                for k in range(2):
                    b, full = fill(pe, l, "rot", k)
                    mm(pe, b[:, 0:NT], cst("rot"), rtz[:, k, :]).then_inc(full, 1)
                wait(pe, rot_ok, l, 0)
                for t, (t0, n) in enumerate(TILES):
                    b, full = fill(pe, l, "rtn", t)
                    for k, src in enumerate([aT[:, 2, t0:t0 + n], rtz[:, 2, t0:t0 + n], rtz[:, 3, t0:t0 + n]]):
                        i = tr(pe, b[0:n, k * P:(k + 1) * P], src)
                    i.then_inc(full, 1)
                q, k = aT[:, 0, :], aT[:, 1, :]
                for h in range(RT_H):
                    s = slice(32 * h, 32 * h + 32)
                    b, full = fill(pe, l, "rtp", h)
                    mm(pe, b[:, 0:SEQ], k[s, 0:P], q[s, 0:SEQ])
                    mm(pe, b[:, SEQ:SEQ + P], k[s, P:SEQ], q[s, P:SEQ]).then_inc(full, 1)
                for h in range(RT_H):
                    s = slice(32 * h, 32 * h + 32)
                    b, full = fill(pe, l, "rtp", 4 + h)
                    mm(pe, b[0:32, 0:32], k[s, SEQ:NT], q[s, SEQ:NT]).then_inc(full, 1)
                wait(pe, rtR_ok, l, 7)
                wait(pe, rtk_ok, l, 2)
                wait(pe, rt_state_in, l, 0)
                rp = R.rearrange("p a b c -> p (a b c)")
                rs = keys.rearrange("p a b c -> p (a b c)")
                nat_rt = lambda t: sg[:, t, :]
                V = lambda t, h: nat_rt(t)[:, P + h * HD:P + (h + 1) * HD]
                Kn = lambda t, h: nat_rt(t)[:, 32 * h:32 * h + 32]
                for p in range(2):
                    b, full = fill(pe, l, "rto", p)
                    for hh in range(2):
                        h, s = 2 * p + hh, slice(64 * hh, 64 * hh + 64)
                        m = rp[:, h * 384:(h + 1) * 384]
                        mm(pe, b[s, 0:P], V(0, h), m[:, 0:P])
                        mm(pe, b[s, P:SEQ], V(0, h), m[:, P:SEQ], stop=False)
                        mm(pe, b[s, P:SEQ], V(1, h), m[:, SEQ:SEQ + P], start=False)
                        i = mm(pe, b[s, SEQ:NT], V(2, h)[0:32, :], rs[0:32, 32 * h:32 * h + 32])
                    i.then_inc(full, 1)
                    b, full = fill(pe, l, "rtc", p)
                    for hh in range(2):
                        h, s = 2 * p + hh, slice(64 * hh, 64 * hh + 64)
                        k4 = slice(32 * h, 32 * h + 32)
                        for x in range(NB):
                            i = mm(pe, b[s, DS * x:DS * (x + 1)], SSr[k4, x, :], rt_qd[k4, DS * x:DS * (x + 1)])
                    i.then_inc(full, 1)
                b, full = fill(pe, l, "rts")
                for h in range(RT_H):
                    s = slice(32 * h, 32 * h + 32)
                    mm(pe, b[s, 0:HD], Kn(0, h), V(0, h), stop=False)
                    i = mm(pe, b[s, 0:HD], Kn(1, h), V(1, h), start=False)
                i.then_inc(full, 1)
                b, full = fill(pe, l, "rtss")
                for h in range(RT_H):
                    wait(pe, rtX_ok, l, h)
                    i = mm(pe, b[32 * h:32 * h + 32, :], Kn(2, h)[0:32, :], UX[0:32, h, :, :].rearrange("p a b -> p (a b)"))
                i.then_inc(full, 1)

            def out_norms(l):
                for y, (a, n) in enumerate(((3, 3), (6, 2))):
                    if y == 0:
                        wait(pe, O_ok, l, 7)
                        wait(pe, Os_ok, l, 1)
                    else:
                        wait(pe, rtO_ok, l, 1)
                    for p in range(a, a + n):
                        b, full = fill(pe, l, "mean", p)
                        mm(pe, b[:, 0:NT], cst("mean64"), OT[:, p, :]).then_inc(full, 1)
                for y, (a, n) in enumerate(((0, 3), (3, 3), (6, 2))):
                    wait(pe, osq_ok, l, y)
                    for p in range(a, a + n):
                        b, full = fill(pe, l, "var", p)
                        mm(pe, b[:, 0:NT], cst("mean64"), conv[:, p, :]).then_inc(full, 1)

            def out_projection(l):
                wait(pe, cat_ok, l, 0)
                for c, (c0, c1) in enumerate(WOUT_LOADS):
                    n_load = len(WIN_LOADS) + c
                    s = n_load % 2
                    wait(pe, loaded[s], l, n_load // 2)
                    w = wslot[s][:, 0:KD * (c1 - c0)].rearrange("p (k c) -> p k c", k=KD)
                    for t, (t0, n) in enumerate(TILES):
                        b, full = fill(pe, l, "out", t, c)
                        for k in range(KD):
                            i = mm(pe, b[0:n, 0:c1 - c0], OT[:, k, t0:t0 + n], w[:, k, :], start=k == 0, stop=k == KD - 1)
                        i.then_inc(full, 1)

            def routing(l):
                b, full = fill(pe, l, "logits")
                for t, (t0, n) in enumerate(TILES):
                    for k in range(KD):
                        i = mm(pe, b[0:n, t * N_EXP:(t + 1) * N_EXP], hT[:, k, t0:t0 + n], rt_w[:, k, :],
                               start=k == 0, stop=k == KD - 1)
                i.then_inc(full, 1)
                wait(pe, logit_ok, 0, 0)
                b, full = fill(pe, l, "combT")
                for t, (t0, n) in enumerate(TILES):
                    i = mm(pe, b[0:N_EXP, t0:t0 + n], small[0:n, 7, t, :], ident[0:n, 0:n])
                i.then_inc(full, 1)
                wait(pe, cT_ok, 0, 0)
                for e in range(N_EXP):
                    b, full = fill(pe, l, "comb", e)
                    mm(pe, b[:, 0:NT], ident[0:N_EXP, e:e + 1].to_broadcast([N_EXP, P]), combT[:, :]).then_inc(full, 1)

            def one_block(s, load, tile0, first, last):
                w = slot[s]
                w13 = w[:, 0:2 * KD * FB].rearrange("p (x k f) -> p x k f", x=2, k=KD)
                w2 = w[:, 2 * KD * FB:].rearrange("p (f d) -> p f d", f=FT)
                pe.wait_ge(block_loaded[s], load)
                for f in range(FT):
                    tile = tile0 + f
                    for x, (full, free) in enumerate(((h1_full, silu_done), (h3_full, hid_ok))):
                        if not (isinstance(tile, int) and tile == 0):
                            pe.wait_ge(free, tile)
                        for k in range(KD):
                            i = mm(pe, banks[6 + x][:, 0:NT], w13[:, x, k, f * P:(f + 1) * P], hT[:, k, :],
                                   start=k == 0, stop=k == KD - 1)
                        i.then_inc(full, 1)
                    yield lambda f=f, tile=tile: second(w2[:, f, :], tile, first and f == 0, last and f == FT - 1)

            def second(w2, tile, first, last):
                pe.wait_ge(hid_ok, tile + 1)
                for t, (t0, n) in enumerate(TILES):
                    for c in range(2):
                        i = mm(pe, banks[2 * t + c][0:n, :], hid_of(tile)[:, t0:t0 + n], w2[:, c * 512:(c + 1) * 512],
                               start=first, stop=last)
                i.then_inc(hid_used, 1)

            def hid_of(tile):
                return hid[parity[0]]

            parity = [0]

            def run_blocks(steps):
                pending = None
                n = 0
                for step in steps:
                    for then in one_block(*step):
                        if pending:
                            parity[0] = (n - 1) % 2
                            pending()
                        pending = then
                        n += 1
                parity[0] = (n - 1) % 2
                pending()

            def feed_forward(l, blocks, base_tile, base_load):
                for b in range(8):
                    turns = len([1 for v in fills.values() if v[0] == b])
                    pe.wait_ge(bank_free[b], turns)
                n_tiles = UNROLL * FT

                def steps(i, m, peeled, final):
                    return [(s, (base_load[s] + i + 1) * 16, base_tile + n_tiles * i + FT * s,
                             peeled and s == 0, final and s == m - 1) for s in range(m)]
                whole, rest = divmod(blocks, UNROLL)
                if not rest:
                    whole, rest = whole - 1, UNROLL
                run_blocks(steps(0, UNROLL, True, False))
                with pe.Fori(1, whole) as i:
                    run_blocks(steps(i, UNROLL, False, False))
                run_blocks(steps(whole, rest, False, True))

            pe.wait_ge(inputs, 16 * N_IN)
            for l in range(DEPTH):
                norm_transposes(l, 0)
                project(l)
                lora(l)
                dn_prepare(l)
                for y in range(2):
                    if y:
                        rw_prepare(l)
                    for t in range(3):
                        (rw_tile if y else dn_tile)(l, t)
                        inverses(l, y, t)
                        chunk_inputs(l, y, t)
                        if t < 2:
                            prompt_chunk(l, y, 2 * t)
                            prompt_chunk(l, y, 2 * t + 1)
                        else:
                            sample_chunks(l, y)
                retention(l)
                out_norms(l)
                out_projection(l)
                norm_transposes(l, 1)
                wait(pe, hT_ok, l, 11)
                if l == 0:
                    feed_forward(l, FFN_BLOCKS, 0, [0] * SLOTS)
                else:
                    routing(l)
                    wait(pe, comb_ok, 0, 0)
                    feed_forward(l, MOE_BLOCKS, FFN_BLOCKS * FT, FFN_USES[0])

        @block.vector
        def _(dve):
            V = nc.vector
            steps = [0]

            def own(ins):
                steps[0] += 1
                ins.then_inc(dve_seq, 1)
                return steps[0]

            def settle():
                dve.wait_ge(dve_seq, steps[0])

            def tt(out, a, b, op):
                return V.tensor_tensor(out, a, b, op)

            def norm(l, use):
                for t, (t0, n) in enumerate(TILES):
                    own(V.tensor_tensor_reduce(junk[0:n], X[0:n, t, :], X[0:n, t, :], 1.0, 0.0, MUL, ADD,
                                               stat[0:n, t, 0:1]))
                    settle()
                    V.nop().then_inc(ssq_ok.sem, 1)
                for t, (t0, n) in enumerate(TILES):
                    wait(dve, rstd_ok, l, use * 3 + t)
                    V.tensor_scalar(hn[t % 2][0:n], X[0:n, t, :], stat[0:n, t, 2:3], None, MUL).then_inc(hn_ok.sem, 1)
                    if t:
                        transposed(l, use, t - 1)
                transposed(l, use, 2)

            def transposed(l, use, t):
                t0, n = TILES[t]
                for part in range(2):
                    b, free = take(dve, l, "hT", use * 3 + t, part)
                    w = par(l, "ln_ffn" if use else "ln_mix", 4 * part, 4)
                    tt(hT[:, 4 * part:4 * part + 4, t0:t0 + n], b[:, :].rearrange("p (a b) -> p a b", a=4)[:, :, 0:n],
                       over(w, n, 2), MUL).then_inc(free, 1)
                    V.engine_nop().then_inc(hT_ok.sem, 1)

            def convolve(l):
                n = ZC - PADC
                for g in range(3):
                    wait(dve, z_ok, l, 3 * g + 2)
                    if g:
                        wait(dve, qkv_ok, l, g - 1)
                    for j in range(CONV_W):
                        for m in range(3):
                            w = par(l, "conv", 4 * (3 * g + m) + j)
                            src = zc[:, 3 * g + m, j:j + n]
                            if j == 0:
                                own(V.tensor_scalar(tmp3[:, m, 0:n], src, w, None, MUL))
                            elif j < CONV_W - 1 or m < 2:
                                own(V.scalar_tensor_tensor(tmp3[:, m, 0:n], src, w, tmp3[:, m, 0:n], MUL, ADD))
                            else:
                                V.scalar_tensor_tensor(tmp3[:, m, 0:n], src, w, tmp3[:, m, 0:n], MUL, ADD)\
                                    .then_inc(conv_ok.sem, 1)
                        settle()
                if l:
                    wait(dve, stored, l - 1, 4)
                own(V.tensor_copy(cvo[:, 0, :, 0:PADC], zc[:, :, SEQ:SEQ + PADC]))
                settle()
                V.tensor_copy(seqs(cvo[:, 0, :, PADC:]), seqs(zc[:, :, SEQ + PADC:])[:, :, :, DS:]).then_inc(cvo_ok.sem, 1)

            def gates(l):
                b, free = take(dve, l, "ab")
                own(V.tensor_copy(ab[:, 0:2, :], b[:, 0:24].rearrange("p (a b) -> p a b", a=2)))
                V.tensor_copy(ab[0:32, 2, :], b[0:32, 24:36]).then_inc(free, 1)
                dve.wait_ge(free, fills[(l, "ab")][1] + 1)
                settle()
                V.engine_nop().then_inc(ab_ok.sem, 1)
                tt(dn[:, 2, :, :], ab[:, :, 0:H], over(par(l, "dt", 0, H), 3), ADD).then_inc(dtb_ok.sem, 1)

            def shift(l):
                wait(dve, z_ok, l, 23)
                wait(dve, qkv_ok, l, 2)
                for g in range(4):
                    ms = slice(3 * g, 3 * g + 3)
                    own(tt(tmp3[:, :, 0:ZR - 1], zr[:, ms, 0:ZR - 1], zr[:, ms, 1:ZR], SUB))
                    settle()
                    for m in range(3 * g, 3 * g + 3):
                        x = tmp3[:, m - 3 * g, :]
                        own(V.scalar_tensor_tensor(zs[:, m, 0:SEQ], x[:, 0:SEQ], par(l, "mu", m), zr[:, m, 1:SEQ + 1], MUL, ADD))
                        own(V.scalar_tensor_tensor(zs[:, m, SEQ:].rearrange("p (b s) -> p b s", b=NB),
                                                   five(x, SEQ + 1),
                                                   par(l, "mu", m), five(zr[:, m, :], SEQ + 2), MUL, ADD))
                    settle()
                own(V.tensor_copy(sho[:, 0, :, 0:1], zr[:, :, SEQ:SEQ + 1]))
                settle()
                V.tensor_copy(sho[:, 0, :, 1:], zr[:, :, SEQ + 1:].rearrange("p m (b s) -> p m b s", s=DS + 1)[:, :, :, DS])\
                    .then_inc(sho_ok.sem, 1)
                wait(dve, sho_ok, l, 0)
                V.engine_nop().then_inc(zs_ok.sem, 1)

            def five(a, start):
                base = start - (SEQ + 1)
                return a[:, SEQ + 1:SEQ + 1 + NB * (DS + 1)].rearrange("p (b s) -> p b s", b=NB)[:, :, base:base + DS]

            def dn_prepare(l):
                tt(SQ[:, :, :], conv[:, 0:6, :], conv[:, 0:6, :], MUL).then_inc(sq_ok.sem, 1)
                wait(dve, dtb_ok, l, 0)
                own(V.tensor_scalar(dn[:, 4, :, :], dn[:, 2, :, :], 0.0, None, ALU.max))
                wait(dve, sp_ok, l, 0)
                settle()
                own(tt(dn[:, 4, :, :], dn[:, 4, :, :], dn[:, 3, :, :], ADD))
                wait(dve, negA_ok, l, 0)
                settle()
                V.scalar_tensor_tensor(dn[:, 0, :, :], dn[:, 4, :, :], -1.0, over(dn[:, 11, 0, :], 3), MUL, MUL)\
                    .then_inc(g_ok.sem, 1)
                b, free = take(dve, l, "cum")
                wait(dve, beta_ok, l, 0)
                c = b[:, 0:36].rearrange("p (t k h) -> p k t h", t=3, k=2)
                own(V.tensor_copy(dn[:, 5:7, 0:2, :], c[:, :, 0:2, :]))
                own(V.tensor_copy(dn[0:32, 5:7, 2, :], c[0:32, :, 2, :]))
                settle()
                V.tensor_scalar(dn[:, 10, :, :], dn[:, 5, :, :], -1.0, None, MUL).then_inc(cum_ok.sem, 1)
                V.engine_nop().then_inc(free, 1)
                own(V.tensor_copy(pair_sel.rearrange("p (h d) -> p h d", h=H), over(ident[0:H, 0:H], HD, 2)))
                settle()
                for k, name in enumerate(("rows_g", "rows_b")):
                    b, free = take(dve, l, name)
                    V.tensor_copy(gb[:, k, :], b[0:H, 0:NT]).then_inc(free, 1)
                    dve.wait_ge(free, fills[(l, name)][1] + 1)
                V.engine_nop().then_inc(gb_ok.sem, 1)
                wait(dve, rn_ok, l, 5)
                own(tt(Q[:, :, 0, :], conv[:, 0:3, :], SQ[:, 0:3, :], MUL))
                own(tt(conv[:, 3:6, :], conv[:, 3:6, :], SQ[:, 3:6, :], MUL))
                settle()
                for p in range(3):
                    b, free = take(dve, l, "bc_b", p)
                    tt(Q[:, p, 1, :], conv[:, 3 + p, :], b[:, 0:NT], MUL).then_inc(free, 1)
                wait(dve, eg_ok, l, 2)
                own(tt(Q[:, :, 2, :], Q[:, :, 0, :], eg[:, :, :], MUL))
                wait(dve, egn_ok, l, 0)
                own(tt(dn[:, 9, :, :], dn[:, 7, :, :], dn[:, 1, :, :], MUL))
                settle()
                V.engine_nop().then_inc(Q_ok.sem, 1)

            def dn_tile(l, t):
                n = TILES[t][1]
                heads = lambda b: b[0:n, 0:384].rearrange("p (h d) -> p h d", h=H)
                sc = lambda k: over(dn[0:n, k, t, :], HD, 2)
                b, free = take(dve, l, "dnk", t)
                own(tt(nat[0:n, 0, :, :], heads(b), sc(9), MUL))
                tt(nat[0:n, 1, :, :], heads(b), sc(8), MUL).then_inc(free, 1)
                dve.wait_ge(free, fills[(l, "dnk", t)][1] + 1)
                b, free = take(dve, l, "dnv", t)
                tt(nat[0:n, 2, :, :], heads(b), sc(1), MUL).then_inc(free, 1)
                dve.wait_ge(free, fills[(l, "dnv", t)][1] + 1)
                settle()
                V.engine_nop().then_inc(nat_ok.sem, 1)
                for h in range(H):
                    wait(dve, DI_ok, l, t * 2 + h // 3)
                    b, free = take(dve, l, 0, "products", t, h)
                    tt(R[0:n, h, 0:2, 0:n], b[0:n, 0:2 * n].rearrange("p (a b) -> p a b", a=2),
                       over(DI[0:n, h // 3, h % 3, 0:n], 2), MUL).then_inc(R_ok.sem, 1)
                    wait(dve, R_ok, l, t * 6 + h)
                    V.engine_nop().then_inc(free, 1)

            def inverses(l, y, t):
                n = TILES[t][1]
                done = (y * 14 + sum(LEVELS[:t])) * 2
                m = lambda a: over(a[0:n, 0:n], 3)
                three = lambda b: b[0:n, 0:3 * n].rearrange("p (a b) -> p a b", a=3)
                for g in range(2):
                    b, free = take(dve, l, y, "L0", t, g)
                    own(tt(TT[0:n, g, :, 0:n], R[0:n, 3 * g:3 * g + 3, 1, 0:n], m(cst("level0_t")), MUL))
                    tt(XM[0:n, g, :, 0:n], three(b), m(cst("level", 0, P)), MUL).then_inc(XM_ok.sem, 1)
                    wait(dve, XM_ok, l, done + g)
                    V.engine_nop().then_inc(free, 1)
                    settle()
                    own(tt(TM[0:n, g, :, 0:n], XM[0:n, g, :, 0:n], m(ident), ADD))
                    settle()
                    tt(TT[0:n, g, :, 0:n], TT[0:n, g, :, 0:n], m(ident), ADD).then_inc(T_ok.sem, 1)
                for lev in range(1, LEVELS[t]):
                    for g in range(2):
                        b, free = take(dve, l, y, "AT", t, lev, g)
                        tt(XM[0:n, g, :, 0:n], three(b), m(cst("level", lev * P, P)), MUL).then_inc(XM_ok.sem, 1)
                        wait(dve, XM_ok, l, done + lev * 2 + g)
                        V.engine_nop().then_inc(free, 1)
                    for g in range(2):
                        b, free = take(dve, l, y, "TX", t, lev, g)
                        tt(TM[0:n, g, :, 0:n], TM[0:n, g, :, 0:n], three(b), ADD).then_inc(free, 1)
                        dve.wait_ge(free, fills[(l, y, "TX", t, lev, g)][1] + 1)
                        b, free = take(dve, l, y, "XT", t, lev, g)
                        tt(TT[0:n, g, :, 0:n], TT[0:n, g, :, 0:n], three(b), ADD).then_inc(T_ok.sem, 1)
                        wait(dve, T_ok, l, done + lev * 2 + g)
                        V.engine_nop().then_inc(free, 1)

            def state_decay(y, p, c):
                return decay[:, p, c:c + 1] if y else eg[:, p, CHUNK * (c + 1) - 1:CHUNK * (c + 1)]

            def prompt_chunk(l, y, c):
                t, cc = c // 2, c % 2
                rows = slice(64 * cc, 64 * cc + 64)
                st = S[:, y, :, :]
                wait(dve, U0_ok, l, y * 3 + t)
                if cc == 0:
                    i = V.tensor_copy(U[:, :, :], U0[:, :, :])
                    if c:
                        own(i)
                        settle()
                    else:
                        i.then_inc(U_ok.sem, 1)
                if c:
                    for odd in range(2):
                        b, free = take(dve, l, y, "WS", c, odd)
                        heads = slice(odd, H, 2)
                        tt(U[rows, heads, :], U0[rows, heads, :], b[rows, 0:192].rearrange("p (a b) -> p a b", a=3), SUB)\
                            .then_inc(free, 1)
                        dve.wait_ge(free, fills[(l, y, "WS", c, odd)][1] + 1)
                    V.engine_nop().then_inc(U_ok.sem, 1)
                b, free = take(dve, l, y, "S", c)
                for p in range(3):
                    new = b[:, p * HD:(p + 1) * HD]
                    if c == 0:
                        i = V.tensor_copy(st[:, p, :], new)
                    else:
                        i = V.scalar_tensor_tensor(st[:, p, :], st[:, p, :], state_decay(y, p, c), new, MUL, ADD)
                    if p < 2:
                        own(i)
                settle()
                i.then_inc(S_ok.sem, 1)
                wait(dve, S_ok, l, y * 4 + c)
                V.engine_nop().then_inc(free, 1)

            def spread(out, src):
                return tt(out, over(src, NB, 1), over(cst("bmask", rows=32), HD, 2), MUL)

            def sample_chunks(l, y):
                flat = lambda a: a[0:32, :, :].rearrange("p a b -> p (a b)")
                b, free = take(dve, l, y, "SUT")
                wait(dve, U0_ok, l, y * 3 + 2)
                tt(flat(U), flat(U0), b[0:32, 0:384], SUB).then_inc(U_ok.sem, 1)
                wait(dve, U_ok, l, y * 5 + 4)
                V.engine_nop().then_inc(free, 1)
                b, free = take(dve, l, y, "O", 4)
                tt(OT[:, 3 * y:3 * y + 3, SEQ:], b[:, 0:96].rearrange("p (a b) -> p a b", a=3), USO[:, :, 0, :], ADD)\
                    .then_inc(Os_ok.sem, 1)
                wait(dve, Os_ok, l, y)
                V.engine_nop().then_inc(free, 1)
                for p in range(3):
                    own(spread(UX[0:32, 0, :, :], U[0:32, 2 * p, :]))
                    if y:
                        own(spread(UX[0:32, 2, :, :], nat[0:32, 2, 2 * p, :]))
                        own(spread(UX[0:32, 3, :, :], nat[0:32, 2, 2 * p + 1, :]))
                    own(spread(UX[0:32, 1, :, :], U[0:32, 2 * p + 1, :]))
                    settle()
                    V.engine_nop().then_inc(UX_ok.sem, 1)
                    dec = decay[:, p, 4:12] if y else eg[:, p, SEQ + DS - 1::DS]
                    own(tt(SS[:, p, :, :], SS[:, p, :, :], over(dec, HD, 2), MUL))
                    b, free = take(dve, l, y, "SS", p)
                    settle()
                    tt(SS[:, p, :, :], SS[:, p, :, :], b[:, :].rearrange("p (a b) -> p a b", a=NB), ADD).then_inc(free, 1)
                    dve.wait_ge(free, fills[(l, y, "SS", p)][1] + 1)
                V.engine_nop().then_inc(SS_ok.sem, 1)

            def rw_prepare(l):
                own(V.tensor_scalar(omka, par(l, "ka", 0, 3), -1.0, 1.0, MUL, ADD))
                for f in range(3):
                    own(V.tensor_scalar(KK[:, f, :], zs[:, 3 + f, :], par(l, "kk", f), None, MUL))
                settle()
                tt(SQ[:, 0:3, :], KK[:, :, :], KK[:, :, :], MUL).then_inc(kk_sq.sem, 1)
                wait(dve, aT_ok, l, 2)
                for f in range(3):
                    own(V.tensor_scalar(bonus[:, f, :], aT[:, f, :], par(l, "ka", f), omka[:, f:f + 1], MUL, ADD))
                settle()
                own(tt(zs[:, 3:6, :], zs[:, 3:6, :], bonus[:, :, :], MUL))
                settle()
                for f in range(3):
                    own(V.scalar_tensor_tensor(SQ[:, 3 + f, :], zs[:, f, :], par(l, "rk", f), zs[:, 3 + f, :], MUL, MUL))
                settle()
                V.engine_nop().then_inc(rk_ok.sem, 1)
                wait(dve, kk_rn, l, 2)
                own(tt(KK[:, :, :], KK[:, :, :], SQ[:, 0:3, :], MUL))
                settle()
                own(tt(aT[:, :, :], aT[:, :, :], KK[:, :, :], MUL))
                for f in range(3):
                    b, free = take(dve, l, "bonus", f)
                    tt(bonus[:, f, :], b[:, 0:NT], zs[:, 6 + f, :], MUL).then_inc(free, 1)
                    dve.wait_ge(free, fills[(l, "bonus", f)][1] + 1)
                settle()

            def rw_tile(l, t):
                t0, n = TILES[t]
                tok = slice(t0, t0 + n)
                wait(dve, E_ok, l, t)
                own(tt(Q[:, :, 0, tok], zs[:, 0:3, tok], E3[:, :, 0, 0:n], MUL))
                own(tt(Q[:, :, 1, tok], KK[:, :, tok], E3[:, :, 1, 0:n], MUL))
                own(tt(keys[:, 0, :, 0:n], aT[:, :, tok], EI[:, :, 0:n], MUL))
                own(tt(keys[:, 1, :, 0:n], zs[:, 3:6, tok], EI[:, :, 0:n], MUL))
                own(tt(ends[:, 0, :, 0:n], aT[:, :, tok], E3[:, :, 2, 0:n], MUL))
                own(tt(ends[:, 1, :, 0:n], zs[:, 3:6, tok], E3[:, :, 2, 0:n], MUL))
                if t < 2:
                    own(V.tensor_copy(decay[:, :, 2 * t:2 * t + 2], E3[:, :, 0, CHUNK - 1::CHUNK]))
                else:
                    own(V.tensor_copy(decay[:, :, 4:12], E3[:, :, 0, DS - 1:32:DS]))
                settle()
                V.engine_nop().then_inc(keys_ok.sem, 1)
                for h in range(H):
                    b, free = take(dve, l, 1, "products", t, h)
                    four = lambda a: a.rearrange("p (k a) c -> p k a c", k=2)
                    tt(four(R[0:n, h, :, :])[:, :, :, 0:n], b[0:n, 0:4 * n].rearrange("p (k a c) -> p k a c", k=2, a=2),
                       over(tri[t][:, 0:2 * n].rearrange("p (a c) -> p a c", a=2), 2), MUL).then_inc(R_ok.sem, 1)
                    wait(dve, R_ok, l, 18 + t * 6 + h)
                    V.engine_nop().then_inc(free, 1)

            def copy_av(l, t):
                n = TILES[t][1]
                b, free = take(dve, l, "XV", t)
                V.tensor_copy(U[0:n, :, :].rearrange("p a b -> p (a b)"), b[0:n, 0:384]).then_inc(XV_ok.sem, 1)
                wait(dve, XV_ok, l, t)
                V.engine_nop().then_inc(free, 1)

            def retention(l):
                for k in range(2):
                    b, free = take(dve, l, "rot", k)
                    own(tt(aT[:, k, :], rtz[:, k, :], cst("cos", 0, NT), MUL))
                    tt(gate[:, k, :], b[:, 0:NT], cst("cos", NT, NT), MUL).then_inc(free, 1)
                    dve.wait_ge(free, fills[(l, "rot", k)][1] + 1)
                    settle()
                    own(tt(aT[:, k, :], aT[:, k, :], gate[:, k, :], ADD))
                settle()
                own(tt(aT[:, 2, :], aT[:, 1, :], cst("kdec"), MUL))
                own(tt(rt_qd, aT[:, 0, SEQ:], cst("qdec"), MUL))
                settle()
                V.engine_nop().then_inc(rot_ok.sem, 1)
                rp = R.rearrange("p a b c -> p (a b c)")
                for h in range(RT_H):
                    b, free = take(dve, l, "rtp", h)
                    own(tt(rp[:, h * 384:h * 384 + SEQ], b[:, 0:SEQ], cst("rt_mask", h * SEQ, SEQ), MUL))
                    tt(rp[:, h * 384 + SEQ:(h + 1) * 384], b[:, SEQ:384], cst("rt_mask", h * SEQ, P), MUL).then_inc(free, 1)
                    dve.wait_ge(free, fills[(l, "rtp", h)][1] + 1)
                    settle()
                    V.engine_nop().then_inc(rtR_ok.sem, 1)
                for h in range(RT_H):
                    b, free = take(dve, l, "rtp", 4 + h)
                    tt(keys.rearrange("p a b c -> p (a b c)")[0:32, 32 * h:32 * h + 32], b[0:32, 0:32],
                       cst("rt_mask_s", 32 * h, 32, rows=32), MUL).then_inc(free, 1)
                    dve.wait_ge(free, fills[(l, "rtp", 4 + h)][1] + 1)
                    V.engine_nop().then_inc(rtR_ok.sem, 1)
                wait(dve, rtk_ok, l, 2)
                for h in range(RT_H):
                    spread(UX[0:32, h, :, :], sg[0:32, 2, P + h * HD:P + (h + 1) * HD]).then_inc(rtX_ok.sem, 1)
                for p in range(2):
                    b, free = take(dve, l, "rto", p)
                    own(V.tensor_copy(OT[:, 6 + p, 0:SEQ], b[:, 0:SEQ]))
                    wait(dve, rtC_ok, l, p)
                    tt(OT[:, 6 + p, SEQ:], b[:, SEQ:NT], USO[:, p, 0, :], ADD).then_inc(free, 1)
                    dve.wait_ge(free, fills[(l, "rto", p)][1] + 1)
                    settle()
                    V.engine_nop().then_inc(rtO_ok.sem, 1)
                b, free = take(dve, l, "rtss")
                x = SSr[:, :, :].rearrange("p a b -> p (a b)")
                V.scalar_tensor_tensor(x, x, cst("g4"), b[:, :], MUL, ADD).then_inc(rtS_ok.sem, 1)
                wait(dve, rtS_ok, l, 0)
                V.engine_nop().then_inc(free, 1)

            def out_norms(l):
                wait(dve, O_ok, l, 7)
                wait(dve, rtO_ok, l, 1)
                tt(conv[:, 0:3, :], OT[:, 0:3, :], OT[:, 0:3, :], MUL).then_inc(osq_ok.sem, 1)
                for a, n in ((3, 3), (6, 2)):
                    for p in range(a, a + n):
                        b, free = take(dve, l, "mean", p)
                        tt(OT[:, p, :], OT[:, p, :], b[:, 0:NT], SUB).then_inc(free, 1)
                        dve.wait_ge(free, fills[(l, "mean", p)][1] + 1)
                    tt(conv[:, a:a + n, :], OT[:, a:a + n, :], OT[:, a:a + n, :], MUL).then_inc(osq_ok.sem, 1)
                weights = [par(l, "dn_norm")] * 3 + [par(l, "ln_g", f) for f in range(3)] + [par(l, "rt_ln", f) for f in range(2)]
                for p in range(8):
                    wait(dve, orn_ok, l, p)
                    own(V.scalar_tensor_tensor(OT[:, p, :], OT[:, p, :], weights[p], conv[:, p, :], MUL, MUL))
                settle()
                for f in range(3):
                    own(V.scalar_tensor_tensor(OT[:, 3 + f, :], OT[:, 3 + f, :], par(l, "ln_b", f), bonus[:, f, :], ADD, ADD))
                own(tt(OT[:, 0:3, :], OT[:, 0:3, :], zg[:, :, :], MUL))
                own(tt(OT[:, 6:8, :], OT[:, 6:8, :], rtz[:, 4:6, :], MUL))
                wait(dve, gT_ok, l, 0)
                settle()
                tt(OT[:, 3:6, :], OT[:, 3:6, :], zs[:, 9:12, :], MUL).then_inc(cat_ok.sem, 1)

            def residual(l):
                for c, (c0, c1) in enumerate(WOUT_LOADS):
                    for t, (t0, n) in enumerate(TILES):
                        b, free = take(dve, l, "out", t, c)
                        x = X[0:n, t, c0:c1]
                        tt(x, x, b[0:n, 0:c1 - c0], ADD).then_inc(free, 1)
                        dve.wait_ge(free, fills[(l, "out", t, c)][1] + 1)
                    V.engine_nop().then_inc(out_ok.sem, 1)

            def routing(l):
                b, free = take(dve, l, "logits")
                own(V.tensor_copy(small[:, 0, 0:2, :], b[:, 0:16].rearrange("p (a b) -> p a b", a=2)))
                V.tensor_copy(small[0:32, 0, 2, :], b[0:32, 16:24]).then_inc(free, 1)
                dve.wait_ge(free, fills[(l, "logits")][1] + 1)
                settle()
                rank = over(cst("rank"), 3)
                top = lambda k: over(stat[:, :, k], N_EXP, 2)

                def pick(src, scored, hot, k):
                    own(V.tensor_reduce(stat[:, :, k], small[:, src, :, :], AX.X, ALU.max))
                    settle()
                    own(tt(small[:, scored, :, :], small[:, src, :, :], top(k), ALU.is_equal))
                    settle()
                    own(tt(small[:, scored, :, :], small[:, scored, :, :], rank, MUL))
                    settle()
                    own(V.tensor_reduce(stat[:, :, k + 1], small[:, scored, :, :], AX.X, ALU.max))
                    settle()
                    own(tt(small[:, hot, :, :], small[:, scored, :, :], top(k + 1), ALU.is_equal))
                    settle()

                pick(0, 1, 2, 3)
                own(V.scalar_tensor_tensor(small[:, 3, :, :], small[:, 2, :, :], -3e38, small[:, 0, :, :], MUL, ADD))
                settle()
                pick(3, 4, 5, 5)
                own(tt(stat[:, :, 7], stat[:, :, 5], stat[:, :, 3], SUB))
                settle()
                V.engine_nop().then_inc(diff_ok.sem, 1)
                wait(dve, odds_ok, 0, 0)
                own(V.tensor_scalar(stat[:, :, 3], stat[:, :, 8], 1.0, None, ADD))
                settle()
                own(V.reciprocal(stat[:, :, 5], stat[:, :, 3]))
                settle()
                own(tt(stat[:, :, 6], stat[:, :, 5], stat[:, :, 8], MUL))
                own(tt(small[:, 2, :, :], small[:, 2, :, :], top(5), MUL))
                settle()
                own(tt(small[:, 5, :, :], small[:, 5, :, :], top(6), MUL))
                settle()
                tt(small[:, 7, :, :], small[:, 2, :, :], small[:, 5, :, :], ADD).then_inc(logit_ok.sem, 1)

            def hidden(l, tile, f, weight):
                dve.wait_ge(silu_done, tile + 1)
                if weight is not None:
                    e, moe_tile = weight
                    V.tensor_tensor(silu_h, silu_h, comb_at(e), MUL).then_inc(weighted, 1)
                    dve.wait_ge(weighted, moe_tile + 1)
                dve.wait_ge(h3_full, tile + 1)
                if not isinstance(tile, int) or tile >= 2:
                    dve.wait_ge(hid_used, tile - 1)
                tt(hid[f % 2], silu_h, banks[7][:, 0:NT], MUL).then_inc(hid_ok, 1)

            def comb_at(e):
                if isinstance(e, int):
                    return comb[:, e, :]
                flat = zs[:, :, :].rearrange("p a b -> p (a b)")
                return flat[:, bass.ds(3 * NT + e * NT, NT)]

            def feed_forward(l, blocks, base):
                n = UNROLL * FT
                whole, rest = divmod(blocks, UNROLL)

                def body(i, m):
                    for s in range(m):
                        j = i * UNROLL + s
                        for f in range(FT):
                            w = None
                            if l:
                                w = (j // EXP_BLOCKS, i * n + s * FT + f)
                            hidden(l, base + i * n + s * FT + f, s * FT + f, w)
                body(0, UNROLL)
                with dve.Fori(1, whole if rest else whole - 1) as i:
                    body(i, UNROLL)
                body(whole if rest else whole - 1, rest or UNROLL)
                dve.wait_ge(hid_used, base + blocks * FT)
                for t, (t0, m) in enumerate(TILES):
                    for c in range(2):
                        x = X[0:m, t, c * 512:(c + 1) * 512]
                        own(tt(x, x, banks[2 * t + c][0:m, :], ADD))
                settle()

            for k, e in enumerate(EPS):
                V.memset(eps(k), e).then_inc(eps_ok, 1)
            own(V.memset(ab[:, :, :], 0.0))
            own(V.memset(dn[:, :, :, :], 0.0))
            own(V.memset(small[:, :, :, :], 0.0))
            own(V.memset(stat[:, :, :], 0.0))
            settle()
            dve.wait_ge(inputs, 16 * N_IN)
            for l in range(DEPTH):
                own(V.memset(zc[:, :, 0:PADC], 0.0))
                own(V.memset(zr[:, :, 0:1], 0.0))
                own(V.memset(zr[:, 11, 1:], 0.0))
                settle()
                V.engine_nop().then_inc(zeroed.sem, 1)
                norm(l, 0)
                wait(dve, pads_ok, l, 0)
                convolve(l)
                gates(l)
                shift(l)
                dn_prepare(l)
                for y in range(2):
                    if y:
                        rw_prepare(l)
                    for t in range(3):
                        (rw_tile if y else dn_tile)(l, t)
                        inverses(l, y, t)
                        if y:
                            copy_av(l, t)
                        if t < 2:
                            prompt_chunk(l, y, 2 * t)
                            prompt_chunk(l, y, 2 * t + 1)
                        else:
                            sample_chunks(l, y)
                retention(l)
                out_norms(l)
                residual(l)
                norm(l, 1)
                if l:
                    routing(l)
                    wait(dve, comb_ok, 0, 0)
                feed_forward(l, MOE_BLOCKS if l else FFN_BLOCKS, FFN_BLOCKS * FT if l else 0)
            dve.wait_ge(lnf_in, 16)
            for t, (t0, n) in enumerate(TILES):
                own(V.tensor_tensor_reduce(junk[0:n], X[0:n, t, :], X[0:n, t, :], 1.0, 0.0, MUL, ADD, stat[0:n, t, 0:1]))
                settle()
                V.engine_nop().then_inc(fss_ok.sem, 1)
            for t, (t0, n) in enumerate(TILES):
                wait(dve, frs_ok, 0, t)
                V.scalar_tensor_tensor(X[0:n, t, :], X[0:n, t, :], stat[0:n, t, 2:3], lnf[0:n, :], MUL, MUL)\
                    .then_inc(final_ok.sem, 1)

        @block.scalar
        def _(act):
            A = nc.scalar.activation
            steps = [0]

            def own(ins):
                steps[0] += 1
                ins.then_inc(act_seq, 1)

            def settle():
                act.wait_ge(act_seq, steps[0])

            def copy(out, in_):
                return A(out, in_, ACT.Copy)

            def rstd(l, use):
                for t, (t0, n) in enumerate(TILES):
                    if l is None:
                        wait(act, fss_ok, 0, t)
                    else:
                        wait(act, ssq_ok, l, use * 3 + t)
                    own(A(stat[0:n, t, 1:2], stat[0:n, t, 0:1], ACT.Ln, bias=eps(0)[0:n], scale=1.0 / D))
                    settle()
                    A(stat[0:n, t, 2:3], stat[0:n, t, 1:2], ACT.Exp, scale=-0.5).then_inc((frs_ok if l is None else rstd_ok).sem, 1)

            def project(l):
                for m, (kind, k, _, n) in enumerate(ZTILES):
                    if m == 12:
                        wait(act, zeroed, l, 0)
                    b, free = take(act, l, "z", m)
                    sample = b[0:n, SEQ:NT].rearrange("p (b s) -> p b s", b=NB)
                    if kind == "conv":
                        own(copy(zc[:, k, PADC:PADC + SEQ], b[:, 0:SEQ]))
                        i = copy(zc[:, k, PADC + SEQ:].rearrange("p (b s) -> p b s", b=NB)[:, :, PADC:], sample)
                    elif kind == "rw":
                        own(copy(zr[0:n, k, 1:1 + SEQ], b[0:n, 0:SEQ]))
                        i = copy(zr[0:n, k, 1 + SEQ:].rearrange("p (b s) -> p b s", b=NB)[:, :, 1:], sample)
                    elif kind == "zg":
                        i = A(zg[:, k, :], b[:, 0:NT], ACT.Silu)
                    else:
                        i = A(rtz[:, k, :], b[:, 0:NT], ACT.Silu if k >= 4 else ACT.Copy)
                    i.then_inc(free, 1)
                    act.wait_ge(free, fills[(l, "z", m)][1] + 1)
                    settle()
                    nc.scalar.nop().then_inc(z_ok.sem, 1)
                    if m in (11, 14, 17):
                        g = (m - 11) // 3
                        wait(act, conv_ok, l, g)
                        own(A(conv[:, 3 * g:3 * g + 3, 0:SEQ], tmp3[:, :, 0:SEQ], ACT.Silu))
                        for x in range(3):
                            own(A(conv[:, 3 * g + x, SEQ:].rearrange("p (b s) -> p b s", b=NB),
                                  tmp3[:, x, PADC + SEQ:].rearrange("p (b s) -> p b s", b=NB)[:, :, 0:DS], ACT.Silu))
                        settle()
                        nc.scalar.nop().then_inc(qkv_ok.sem, 1)

            def lora(l):
                wait(act, ab_ok, l, 0)
                A(dn[:, 1, :, :], ab[:, :, H:], ACT.Sigmoid).then_inc(beta_ok.sem, 1)
                wait(act, zs_ok, l, 0)
                own(A(zs[0:64, 9, :], zs[0:64, 9, :], ACT.Tanh))
                own(A(zs[:, 10, :], zs[:, 10, :], ACT.Sigmoid))
                own(A(zs[0:32, 11, :], zs[0:32, 11, :], ACT.Sigmoid))
                settle()
                nc.scalar.nop().then_inc(lora_ok.sem, 1)
                for t, (t0, n) in enumerate(TILES):
                    b, free = take(act, l, "y", t)
                    A(sg[0:n, t, :], b[0:n, 0:384], ACT.Sigmoid).then_inc(free, 1)
                    act.wait_ge(free, fills[(l, "y", t)][1] + 1)
                    nc.scalar.nop().then_inc(sg_ok.sem, 1)
                for f in range(3):
                    b, free = take(act, l, "a", f)
                    A(aT[:, f, :], b[:, 0:NT], ACT.Sigmoid, bias=par(l, "a0", f)).then_inc(free, 1)
                    act.wait_ge(free, fills[(l, "a", f)][1] + 1)
                    nc.scalar.nop().then_inc(aT_ok.sem, 1)
                take(act, l, "g", 2)
                for f in range(3):
                    b, free = take(act, l, "g", f)
                    copy(zs[:, 9 + f, :], b[:, 0:NT]).then_inc(free, 1)
                    act.wait_ge(free, fills[(l, "g", f)][1] + 1)
                nc.scalar.nop().then_inc(gT_ok.sem, 1)

            def inverse_root(l, key, out, eps_k, done, factor=None):
                b, free = take(act, l, *key)
                A(out, b[:, 0:NT], ACT.Ln, bias=eps(eps_k)).then_inc(free, 1)
                act.wait_ge(free, fills[(l, *key)][1] + 1)
                A(out, out, ACT.Exp, scale=-0.5, bias=factor if factor is not None else 0.0).then_inc(done.sem, 1)

            def dn_prepare(l):
                A(dn[:, 11, 0, :], par(l, "a_log", 0, H), ACT.Exp).then_inc(negA_ok.sem, 1)
                wait(act, dtb_ok, l, 0)
                own(A(dn[:, 3, :, :], dn[:, 2, :, :], ACT.Abs))
                settle()
                own(A(dn[:, 3, :, :], dn[:, 3, :, :], ACT.Exp, scale=-1.0))
                settle()
                A(dn[:, 3, :, :], dn[:, 3, :, :], ACT.Ln, bias=1.0).then_inc(sp_ok.sem, 1)
                for i in range(6):
                    inverse_root(l, ("dnss", i), SQ[:, i, :], 1, rn_ok, eps(4) if i < 3 else None)
                wait(act, cum_ok, l, 0)
                A(dn[:, 7:9, :, :], dn[:, 5:7, :, :], ACT.Exp).then_inc(egn_ok.sem, 1)
                for p in range(3):
                    b, free = take(act, l, "bc_g", p)
                    A(eg[:, p, :], b[:, 0:NT], ACT.Exp).then_inc(free, 1)
                    act.wait_ge(free, fills[(l, "bc_g", p)][1] + 1)
                    nc.scalar.nop().then_inc(eg_ok.sem, 1)

            def dn_tile(l, t):
                n = TILES[t][1]
                for g in range(2):
                    b, free = take(act, l, "E", t, g)
                    for x in range(3):
                        h = 3 * g + x
                        i = A(DI[0:n, g, x, 0:n], b[0:n, x * n:(x + 1) * n], ACT.Exp, bias=dn[0:n, 10, t, h:h + 1])
                        if x < 2:
                            own(i)
                    i.then_inc(free, 1)
                    act.wait_ge(free, fills[(l, "E", t, g)][1] + 1)
                    settle()
                    nc.scalar.nop().then_inc(DI_ok.sem, 1)

            def rw_tile(l, t):
                n = TILES[t][1]
                if t:
                    wait(act, keys_ok, l, t - 1)
                for f in range(3):
                    b, free = take(act, l, "cumw", t, f)
                    own(A(E3[:, f, :, 0:n], b[:, 0:3 * n].rearrange("p (a b) -> p a b", a=3), ACT.Exp, scale=-RW_DECAY))
                    A(EI[:, f, 0:n], b[:, 0:n], ACT.Exp, scale=RW_DECAY).then_inc(free, 1)
                    act.wait_ge(free, fills[(l, "cumw", t, f)][1] + 1)
                settle()
                nc.scalar.nop().then_inc(E_ok.sem, 1)
                for k in range(4):
                    b, free = take(act, l, "rwnat", t, k)
                    copy(nat[0:n, k, :, :].rearrange("p a b -> p (a b)"), b[0:n, 0:384]).then_inc(free, 1)
                    act.wait_ge(free, fills[(l, "rwnat", t, k)][1] + 1)
                nc.scalar.nop().then_inc(natb_ok.sem, 1)

            def chunk_inputs(l, y, t):
                t0, n = TILES[t]
                b, free = take(act, l, y, "W", t)
                copy(Q[:, :, 3, t0:t0 + n], b[:, 0:3 * n].rearrange("p (a b) -> p a b", a=3)).then_inc(W_ok.sem, 1)
                wait(act, W_ok, l, y * 3 + t)
                nc.scalar.nop().then_inc(free, 1)
                b, free = take(act, l, y, "U0", t)
                A(U0[0:n, :, :].rearrange("p a b -> p (a b)"), b[0:n, 0:384], ACT.Copy, scale=-1.0 if y else 1.0)\
                    .then_inc(U0_ok.sem, 1)
                wait(act, U0_ok, l, y * 3 + t)
                nc.scalar.nop().then_inc(free, 1)

            def prompt_chunk(l, y, c):
                b, free = take(act, l, y, "O", c)
                copy(OT[:, 3 * y:3 * y + 3, CHUNK * c:CHUNK * (c + 1)], b[:, 0:3 * CHUNK].rearrange("p (a b) -> p a b", a=3))\
                    .then_inc(O_ok.sem, 1)
                wait(act, O_ok, l, y * 4 + c)
                nc.scalar.nop().then_inc(free, 1)

            def sample_chunks(l, y):
                b, free = take(act, l, y, "SU")
                copy(USO[:, :, :, :].rearrange("p a b c -> p (a b c)"), b[:, 0:192]).then_inc(USO_ok.sem, 1)
                wait(act, USO_ok, l, y)
                nc.scalar.nop().then_inc(free, 1)

            def rw_prepare(l):
                for f in range(3):
                    inverse_root(l, ("kss", f), SQ[:, f, :], 1, kk_rn)

            def retention(l):
                for t, (t0, n) in enumerate(TILES):
                    b, free = take(act, l, "rtn", t)
                    copy(sg[0:n, t, :], b[0:n, 0:384]).then_inc(free, 1)
                    act.wait_ge(free, fills[(l, "rtn", t)][1] + 1)
                    nc.scalar.nop().then_inc(rtk_ok.sem, 1)
                for p in range(2):
                    b, free = take(act, l, "rtc", p)
                    copy(USO[:, p, 0, :], b[:, 0:32]).then_inc(free, 1)
                    act.wait_ge(free, fills[(l, "rtc", p)][1] + 1)
                    nc.scalar.nop().then_inc(rtC_ok.sem, 1)
                b, free = take(act, l, "rts")
                copy(Sr[:, l, :], b[:, 0:HD]).then_inc(rtSp_ok.sem, 1)
                wait(act, rtSp_ok, l, 0)
                nc.scalar.nop().then_inc(free, 1)

            def out_norms(l):
                for p in range(8):
                    inverse_root(l, ("var", p), conv[:, p, :], 0 if p < 3 else 2 if p < 6 else 3, orn_ok)

            def routing(l):
                wait(act, diff_ok, 0, 0)
                A(stat[:, :, 8], stat[:, :, 7], ACT.Exp).then_inc(odds_ok.sem, 1)
                b, free = take(act, l, "combT")
                copy(combT[:, :], b[0:N_EXP, 0:NT]).then_inc(cT_ok.sem, 1)
                wait(act, cT_ok, 0, 0)
                nc.scalar.nop().then_inc(free, 1)
                for e in range(N_EXP):
                    b, free = take(act, l, "comb", e)
                    copy(comb[:, e, :], b[:, 0:NT]).then_inc(free, 1)
                    act.wait_ge(free, fills[(l, "comb", e)][1] + 1)
                nc.scalar.nop().then_inc(comb_ok.sem, 1)

            def feed_forward(l, blocks, base):
                n = UNROLL * FT
                whole, rest = divmod(blocks, UNROLL)

                def body(i, m):
                    for f in range(m * FT):
                        tile = base + i * n + f
                        act.wait_ge(h1_full, tile + 1)
                        if not isinstance(tile, int) or tile:
                            act.wait_ge(hid_ok, tile)
                        A(silu_h, banks[6][:, 0:NT], ACT.Silu).then_inc(silu_done, 1)
                body(0, UNROLL)
                with act.Fori(1, whole if rest else whole - 1) as i:
                    body(i, UNROLL)
                body(whole if rest else whole - 1, rest or UNROLL)

            act.wait_ge(inputs, 16 * N_IN)
            act.wait_ge(eps_ok, len(EPS))
            for l in range(DEPTH):
                rstd(l, 0)
                for k in range(2):
                    wait(act, seq_states, l, k)
                own(copy(seqs(zc[:, :, PADC + SEQ:])[:, :, :, 0:PADC], seqs(cvs[:, :, :])))
                wait(act, zeroed, l, 0)
                own(copy(zr[:, :, 1 + SEQ:].rearrange("p m (b s) -> p m b s", s=DS + 1)[:, :, :, 0], shs[:, :, :]))
                settle()
                nc.scalar.nop().then_inc(pads_ok.sem, 1)
                project(l)
                lora(l)
                dn_prepare(l)
                for y in range(2):
                    if y:
                        rw_prepare(l)
                    for t in range(3):
                        (rw_tile if y else dn_tile)(l, t)
                        chunk_inputs(l, y, t)
                        if t < 2:
                            prompt_chunk(l, y, 2 * t)
                            prompt_chunk(l, y, 2 * t + 1)
                        else:
                            sample_chunks(l, y)
                retention(l)
                out_norms(l)
                rstd(l, 1)
                if l:
                    routing(l)
                feed_forward(l, MOE_BLOCKS if l else FFN_BLOCKS, FFN_BLOCKS * FT if l else 0)
            rstd(None, 0)

        @block.sync
        def _(sp):
            for l in range(DEPTH):
                if l:
                    sp.wait_ge(hid_used, FFN_BLOCKS * FT)
                for i in range(MIX_LOADS):
                    s = i % 2
                    if i >= 2:
                        if i - 2 < len(WIN_LOADS):
                            wait(sp, z_ok, l, [m for m, z in enumerate(ZTILES) if z[2] < WIN_LOADS[i - 2][1]][-1])
                        else:
                            wait(sp, out_ok, l, i - 2 - len(WIN_LOADS))
                    if i < len(WIN_LOADS):
                        c0, c1 = WIN_LOADS[i]
                        dst = wslot[s][:, 0:KD * (c1 - c0)].rearrange("p (k c) -> p k c", k=KD)
                        src = w_in[l].rearrange("(k p) c -> p k c", p=P)[:, :, c0:c1]
                    else:
                        c0, c1 = WOUT_LOADS[i - len(WIN_LOADS)]
                        dst = wslot[s][:, 0:KD * (c1 - c0)].rearrange("p (k c) -> p k c", k=KD)
                        src = w_out[l].rearrange("(k p) c -> p k c", p=P)[:, :, c0:c1]
                    sp.dma_start(dst, src).then_inc(loaded[s].sem, 16)
                wait(sp, out_ok, l, len(WOUT_LOADS) - 1)
                blocks = MOE_BLOCKS if l else FFN_BLOCKS
                src = moe if l else ffn
                base = FFN_BLOCKS * FT if l else 0
                for s in range(SLOTS):
                    sp.dma_start(slot[s], src[s]).then_inc(block_loaded[s], 16)
                whole, rest = divmod(blocks, UNROLL)
                with sp.Fori(1, whole) as i:
                    for s in range(SLOTS):
                        sp.wait_ge(hid_used, base + FT * (SLOTS * (i - 1) + s + 1))
                        sp.dma_start(slot[s], src[bass.ds(i * SLOTS + s, 1)].rearrange("a p c -> p (a c)")).then_inc(block_loaded[s], 16)
                for s in range(rest):
                    sp.wait_ge(hid_used, base + FT * (SLOTS * (whole - 1) + s + 1))
                    sp.dma_start(slot[s], src[whole * SLOTS + s]).then_inc(block_loaded[s], 16)
            sp.wait_ge(hid_used, (FFN_BLOCKS + MOE_BLOCKS) * FT)
            sp.dma_start(lnf, ln_final).then_inc(lnf_in, 16)
            for t, (t0, n) in enumerate(TILES):
                wait(sp, final_ok, 0, t)
                sp.dma_start(y_out[t0:t0 + n, :], X[0:n, t, :]).then_inc(y_stored, 16)
            sp.wait_ge(y_stored, 48)

        @block.gpsimd
        def _(pool):
            pool.dma_start(C[:, :], consts).then_inc(inputs, 16)
            pool.dma_start(X[:, 0:2, :], x_in[0:SEQ, :].rearrange("(t p) d -> p t d", p=P)).then_inc(inputs, 16)
            pool.dma_start(X[0:32, 2, :], x_in[SEQ:NT, :]).then_inc(inputs, 16)
            pool.dma_start(PC[:, :, :], pcol.rearrange("l p c -> p l c")).then_inc(inputs, 16)
            pool.dma_start(rt_w[:, :, :], router.rearrange("(k p) e -> p k e", p=P)).then_inc(inputs, 16)
            for l in range(DEPTH):
                if l:
                    wait(pool, gT_ok, l - 1, 0)
                    wait(pool, SS_ok, l - 1, 1)
                pool.dma_start(cvs[:, :, :], conv_state[l]).then_inc(seq_states.sem, 16)
                pool.dma_start(shs[:, :, :], shift_state[l]).then_inc(seq_states.sem, 16)
                pool.dma_start(w2a2[:, :], rw_w2a2[l]).then_inc(lora_loaded.sem, 16)
                pool.dma_start(g2[:, :, :], rw_g2[l]).then_inc(lora_loaded.sem, 16)
                pool.dma_start(w0[:, :], rw_w0[l:l + 1, :]).then_inc(lora_loaded.sem, 16)
                if l:
                    wait(pool, rt_state_out, l - 1, 0)
                pool.dma_start(SSr[:, :, :], rt_state[l]).then_inc(rt_state_in.sem, 16)
                if l:
                    wait(pool, ss_out, l - 1, 1)
                pool.dma_start(SS[:, :, :, :], dn_state[l]).then_inc(ss_in.sem, 16)
                wait(pool, cvo_ok, l, 0)
                pool.dma_start(conv_out[l], cvo[:, 0, :, :]).then_inc(stored.sem, 16)
                wait(pool, sho_ok, l, 0)
                pool.dma_start(shift_out[l], sho[:, 0, :, :]).then_inc(stored.sem, 16)
                for y, (pp, ssx) in enumerate(((p_dn, s_dn), (p_rw, s_rw))):
                    wait(pool, S_ok, l, 4 * y + 3)
                    pool.dma_start(pp[l], S[:, y, :, :]).then_inc(stored.sem, 16)
                    wait(pool, SS_ok, l, y)
                    pool.dma_start(ssx[l], SS[:, :, :, :]).then_inc(ss_out.sem, 16)
                    if y == 0:
                        wait(pool, ss_out, l, 0)
                        pool.dma_start(SS[:, :, :, :], rw_state[l]).then_inc(ss_in.sem, 16)
                wait(pool, rtSp_ok, l, 0)
                pool.dma_start(p_rt[l], Sr[:, l, :]).then_inc(stored.sem, 16)
                wait(pool, rtS_ok, l, 0)
                pool.dma_start(s_rt[l], SSr[:, :, :]).then_inc(rt_state_out.sem, 16)
            wait(pool, stored, DEPTH - 1, 4)
            wait(pool, ss_out, DEPTH - 1, 1)
            wait(pool, rt_state_out, DEPTH - 1, 0)


def rows_to(a, rows=P):
    return np.swapaxes(a.reshape(a.shape[:-1] + (-1, rows)), -1, -2)


def kernel(**inp):
    import concourse.bacc as _bacc
    from concourse.bass_utils import run_bass_kernel_spmd as _run

    a = {k: np.asarray(v) for k, v in inp.items()}
    L = DEPTH
    f32 = np.float32

    def padded(x, n):
        out = np.zeros(x.shape[:-1] + (n,), x.dtype)
        out[..., :x.shape[-1]] = x
        return out

    cols = {
        "ln_mix": rows_to(a["ln_mix"]), "ln_ffn": rows_to(a["ln_ffn"]),
        "conv": np.ascontiguousarray(a["dn_conv"].reshape(L, CONV_W, 9, P).transpose(0, 3, 2, 1)).reshape(L, P, 36),
        "dn_norm": np.concatenate([a["dn_norm"]] * 2, 1)[:, :, None],
        "mu": rows_to(padded(a["rw_mu"], 12 * P)), "a0": rows_to(a["rw_a0"]), "kk": rows_to(a["rw_kk"]),
        "ka": rows_to(a["rw_ka"]), "rk": rows_to(a["rw_rk"].reshape(L, -1)), "ln_g": rows_to(a["rw_ln_g"]),
        "ln_b": rows_to(a["rw_ln_b"]), "rt_ln": rows_to(a["rt_ln"]),
        "a_log": np.repeat(a["dn_a_log"][:, None], P, 1), "dt": np.repeat(a["dn_dt_bias"][:, None], P, 1),
    }
    g2 = np.zeros((L, P, 2, 384), f32)
    g2[:, :, 0] = a["rw_g2"][:, :P]
    g2[:, :32, 1] = a["rw_g2"][:, P:]

    def blocks(w1, w3, w2):
        e, d, f = w1.shape
        up = lambda w: w.reshape(e, KD, P, f // FB, FB).transpose(0, 3, 2, 1, 4).reshape(e * f // FB, P, KD * FB)
        down = w2.reshape(e, f // FB, FT, P, D).transpose(0, 1, 3, 2, 4).reshape(e * f // FB, P, FT * D)
        return np.concatenate([up(w1), up(w3), down], 2)

    shift = padded(a["state_rw_shift"], 12 * P).reshape(L, NB, 12, P).transpose(0, 3, 2, 1)
    arrays = {
        "x_in": np.concatenate([a["x_prompt"].reshape(SEQ, D), a["x_sample"].reshape(NB * DS, D)]),
        "consts": constants(),
        "pcol": np.concatenate([cols[k] for k, _ in PCOLS], 2),
        "rw_w2a2": np.concatenate([a["rw_w2"], a["rw_a2"]], 1),
        "rw_g2": g2, "rw_w0": a["rw_w0"], "ln_final": np.repeat(a["ln_final"][None], P, 0),
        "router": a["moe_router"][0], "w_in": a["w_in"], "w_out": a["w_out"],
        "ffn": blocks(a["ffn_w1"], a["ffn_w3"], a["ffn_w2"]),
        "moe": blocks(a["moe_w1"][0], a["moe_w3"][0], a["moe_w2"][0]),
        "conv_state": a["state_dn_conv"].reshape(L, NB, PADC, 9, P).transpose(0, 4, 3, 1, 2).reshape(L, P, 9, 24),
        "shift_state": shift,
        "dn_state": a["state_dn"].reshape(L, NB, 3, P, HD).transpose(0, 3, 2, 1, 4),
        "rw_state": a["state_rw"].transpose(0, 1, 2, 4, 3).reshape(L, NB, 3, P, HD).transpose(0, 3, 2, 1, 4),
        "rt_state": a["state_rt"].reshape(L, NB, P, HD).transpose(0, 2, 1, 3),
    }
    outs = {"y_out": (NT, D), "conv_out": (L, P, 9, 27), "shift_out": (L, P, 12, 9), "p_dn": (L, P, 3, HD),
            "p_rw": (L, P, 3, HD), "p_rt": (L, P, HD), "s_dn": (L, P, 3, NB, HD), "s_rw": (L, P, 3, NB, HD),
            "s_rt": (L, P, NB, HD)}
    nc = _bacc.Bacc("TRN2", target_bir_lowering=False, num_devices=1)
    args, given = {}, {}
    for name, x in arrays.items():
        given[name + "_dram"] = np.ascontiguousarray(x)
        args[name] = nc.dram_tensor(name + "_dram", x.shape, F32, kind="ExternalInput").ap()
    for name, shape in outs.items():
        args[name] = nc.dram_tensor(name + "_dram", shape, F32, kind="ExternalOutput").ap()
    trunk(nc, **args)
    r = _run(nc, [given], core_ids=[0]).results[0]
    o = {name: r[name + "_dram"] for name in outs}
    conv = o["conv_out"].reshape(L, P, 9, 9, PADC).transpose(3, 0, 4, 2, 1).reshape(9, L, PADC, 9 * P)
    sh = o["shift_out"].transpose(3, 0, 2, 1).reshape(9, L, 12 * P)[:, :, :1440]
    heads = lambda x: x.transpose(0, 2, 1, 3).reshape(L, H, HD, HD)
    sheads = lambda x: x.transpose(0, 3, 2, 1, 4).reshape(L, NB, H, HD, HD)
    res = (o["y_out"][:SEQ].reshape(1, SEQ, D), o["y_out"][SEQ:].reshape(NB, DS, D),
           conv[0][:, None], heads(o["p_dn"])[:, None], sh[0][:, None],
           heads(o["p_rw"]).swapaxes(-1, -2)[:, None], o["p_rt"].reshape(L, 1, RT_H, RT_K, HD),
           conv[1:].transpose(1, 0, 2, 3), sheads(o["s_dn"]), sh[1:].transpose(1, 0, 2),
           sheads(o["s_rw"]).swapaxes(-1, -2), o["s_rt"].transpose(0, 2, 1, 3).reshape(L, NB, RT_H, RT_K, HD))
    return tuple(np.ascontiguousarray(x) for x in res)
```

```python
import math
from contextlib import ExitStack

import numpy as np

import concourse.bass as bass
from concourse import mybir

F32 = mybir.dt.float32
ALU = mybir.AluOpType
ACT = mybir.ActivationFunctionType
AX = mybir.AxisListType
MUL, ADD, SUB = ALU.mult, ALU.add, ALU.subtract

P = 128
D = 1024
KD = D // P
SEQ, NB, DS = 256, 8, 4
NT = SEQ + NB * DS
DEPTH = 2
TILES = [(0, 128), (128, 128), (256, 32)]
CHUNK = 64
H = 6
HD = 64
CONV_W = 4
DN_QKV = 9
P_IN = 3756
RT_H, RT_K = 4, 32
D_FF, N_EXP, D_EXP = 2816, 8, 3584
FB = P
FFN_BLOCKS = D_FF // FB
EXP_BLOCKS = D_EXP // FB
MOE_BLOCKS = N_EXP * EXP_BLOCKS
SLOT = 3 * KD * FB
SLOTS = 7
RING = 8 * SLOT
CAP = P
PADC = CONV_W - 1
ZC = PADC + SEQ + NB * (PADC + DS)
ZR = 1 + SEQ + NB * (1 + DS)
RW_DECAY = math.exp(-0.5)
NORM_EPS, RW_GN_EPS, RT_GN_EPS, L2_EPS = 1e-6, 64e-5, 1e-5, 1e-6
PAST_LEN = 2048
NEG = -1e30

DN0, RW0, RT0 = 0, 1548, 2988
ZTILES = [("conv", m, DN0 + P * m, P) for m in range(9)] + [("zg", m, 1152 + P * m, P) for m in range(3)]
ZTILES += [("rw", m, RW0 + P * m, P) for m in range(11)] + [("rw", 11, RW0 + 11 * P, 32)]
ZTILES += [("rt", m, RT0 + P * m, P) for m in range(6)]
WSLOT = KD * 384
WIN_LOADS = [(0, 384), (384, 768), (768, 1152), (1152, 1536), (1536, 1804), (1804, 2188), (2188, 2572), (2572, 2956),
             (2956, 3244), (3244, 3628), (3628, 3756)]
WOUT_LOADS = [(0, 384), (384, 768), (768, 1024)]
AB_LOAD = 4
MIX_LOADS = len(WIN_LOADS) + len(WOUT_LOADS)

PCOLS = [("ln_mix", 8), ("ln_ffn", 8), ("conv", 36), ("dn_norm", 1), ("mu", 12), ("a0", 3), ("kk", 3),
         ("ka", 3), ("rk", 3), ("ln_g", 3), ("ln_b", 3), ("rt_ln", 2), ("a_log", 6), ("dt", 6)]
CCOLS = [("ident", 128), ("tri", 384), ("tri_s", 96), ("neg", 128), ("neg_s", 32), ("level", 6 * 128),
         ("level0_t", 128), ("ones64", 128), ("mean64", 128), ("bmask", 8), ("rot", 128), ("cos", 2 * NT), ("qdec", 32), ("kdec", NT),
         ("g4", 1), ("rt_mask", 4 * SEQ), ("rt_mask_s", 128), ("rank", 8), ("ones", 128)]
ROUTE_N = 2 * P


def columns(cols):
    at, out = 0, {}
    for name, n in cols:
        out[name] = (at, n)
        at += n
    return out, at


PAT, PN = columns(PCOLS)
CAT, CN = columns(CCOLS)


def constants():
    c = np.zeros((P, CN), np.float64)

    def put(name, a, rows=P):
        at, n = CAT[name]
        c[:rows, at:at + n] = np.asarray(a).reshape(rows, n)

    i = np.arange(P)
    put("ident", np.eye(P))
    for name, size, n in (("tri", CHUNK, P), ("tri_s", DS, 32)):
        j, k = i[:n, None], i[None, :n]
        same = j // size == k // size
        put(name, np.concatenate([same & (j <= k), same & (j < k), same & (j > k)], 1), n)
        put("neg" + name[3:], np.where(same & (j <= k), 0.0, NEG), n)
    levels = []
    for s in (1, 2, 4, 8, 16, 32):
        a, b = i[:, None], i[None, :]
        levels.append(-1.0 * ((a // (2 * s) == b // (2 * s)) & (a % (2 * s) >= s) & (b % (2 * s) < s)))
    put("level", np.concatenate(levels, 1))
    put("level0_t", levels[0].T)
    blocks = (i[:, None] // HD == i[None, :] // HD) * 1.0
    put("ones64", blocks)
    put("mean64", blocks / HD)
    put("bmask", i[:32, None] // DS == np.arange(NB)[None], 32)
    rot = np.zeros((P, P))
    half = RT_K // 2
    for x in range(P):
        if x % RT_K < half:
            rot[x + half, x] = -1.0
        else:
            rot[x - half, x] = 1.0
    put("rot", rot)
    inv = (np.float32(10000.0) ** (-np.arange(half, dtype=np.float32) / np.float32(half))).astype(np.float32)
    pos = np.concatenate([np.arange(SEQ), np.tile(PAST_LEN + np.arange(DS), NB)]).astype(np.float32)
    ang = (pos[None, :] * inv[i % half][:, None]).astype(np.float32).astype(np.float64)
    put("cos", np.concatenate([np.cos(ang), np.sin(ang)], 1))
    lg = np.log1p(-np.exp2(-5.0 - np.arange(RT_H)))
    lgp = lg[i // RT_K][:, None]
    tok = np.tile(np.arange(DS), NB)[None]
    put("qdec", np.exp((tok + 1) * lgp))
    put("kdec", RT_K ** -0.5 * np.exp(np.concatenate([SEQ - 1 - np.arange(SEQ)[None] + 0 * lgp, DS - 1 - tok + 0 * lgp], 1) * lgp))
    put("g4", np.exp(DS * lgp))
    m = []
    for h in range(RT_H):
        d = np.arange(SEQ)[None] - i[:, None]
        m.append(RT_K ** -0.5 * np.where(d >= 0, np.exp(np.maximum(d, 0) * lg[h]), 0.0))
    put("rt_mask", np.concatenate(m, 1))
    j, k = i[:32, None], i[None, :32]
    put("rt_mask_s", RT_K ** -0.5 * np.concatenate([np.where((j // DS == k // DS) & (j <= k), np.exp(np.maximum(k - j, 0) * lg[h]), 0.0)
                                     for h in range(RT_H)], 1), 32)
    put("rank", np.tile(N_EXP - np.arange(N_EXP), (P, 1)))
    put("ones", np.ones((P, P)))
    return c.astype(np.float32)


def route_constants():
    return np.concatenate([np.tile(np.arange(P), (P, 1)), np.triu(np.ones((P, P)), 1)], 1).astype(np.float32)


def trunk(nc, x_in, consts, route_consts, pcol, rw_w2a2, rw_g2, rw_w0, ln_final, router, w_in, w_out, ffn, moe,
          conv_state, shift_state, dn_state, rw_state, rt_state,
          y_out, conv_out, shift_out, p_dn, p_rw, p_rt, s_dn, s_rw, s_rt):
    with ExitStack() as ctx:
        def sb(name, *free, rows=P):
            return ctx.enter_context(nc.sbuf_tensor(name, [rows, *free], F32))

        class Signal:

            def __init__(self, name, per, step=1):
                self.sem, self.per, self.step = ctx.enter_context(nc.semaphore(name)), per, step

            def at(self, layer, unit):
                assert 0 <= unit < self.per, (self.sem, unit)
                return self.step * (layer * self.per + unit + 1)

        def wait(eng, signal, layer, unit):
            eng.wait_ge(signal.sem, signal.at(layer, unit))

        ring = sb("ring", RING)
        wslot = [ring[:, s * WSLOT:(s + 1) * WSLOT] for s in range(2)]
        slot = [ring[:, s * SLOT:(s + 1) * SLOT] for s in range(SLOTS)]
        mix_at = [2 * WSLOT]

        def in_ring(*free, at=None):
            n = int(np.prod(free))
            a = mix_at[0] if at is None else at
            if at is None:
                mix_at[0] += n
            assert a + n <= RING, (a, n)
            names = "abcd"[:len(free)]
            if len(free) == 1:
                return ring[:, a:a + n]
            return ring[:, a:a + n].rearrange(f"p ({' '.join(names)}) -> p {' '.join(names)}", **dict(zip(names, free)))

        zc_at = mix_at[0]
        zc = in_ring(9, ZC)
        zr = in_ring(12, ZR)
        Q = in_ring(3, 4, NT, at=zc_at)
        UX = in_ring(4, NB, HD, at=zc_at + 12 * NT)
        assert 12 * NT + 4 * NB * HD <= 9 * ZC + 11 * ZR
        rtz = in_ring(6, NT)
        tmp3 = in_ring(3, ZC)
        R = in_ring(H, 4, P)
        nat = in_ring(4, H, HD)
        E3 = in_ring(3, 3, P)
        keys = in_ring(2, 3, P)

        X = sb("X", 3, D)
        hT = sb("hT", KD, NT)
        C = sb("C", CN)
        PC = sb("PC", DEPTH, PN)
        w2a2 = sb("w2a2", 384)
        g2 = sb("g2", 2, 384)
        w0 = sb("w0", 384, rows=1)
        rt_w = sb("rt_w", KD, N_EXP)
        conv = sb("conv", 9, NT)
        zg = sb("zg", 3, NT)
        zs = sb("zs", 12, NT)
        gate = sb("gate", 3, NT)
        aT = sb("aT", 3, NT)
        bonus = sb("bonus", 3, NT)
        TM = sb("TM", 2, 3, P)
        TT = sb("TT", 2, 3, P)
        XM = sb("XM", 2, 3, P)
        DI = XM
        EI = in_ring(3, P)
        ends = in_ring(2, 3, P)
        sg = in_ring(3, 384)
        U0 = sb("U0", H, HD)
        U = sb("U", H, HD)
        S = sb("S", 2, 3, HD)
        Sr = sb("Sr", DEPTH, HD)
        SS = sb("SS", 3, NB, HD)
        SSr = sb("SSr", NB, HD)
        USO = in_ring(3, 2, 32)
        early = U0[:, :, :].rearrange("p a b -> p (a b)")
        cvs = early[:, 0:216].rearrange("p (a b) -> p a b", a=9)
        shs = early[:, 216:312].rearrange("p (a b) -> p a b", a=12)
        cvo = sb("cvo", 1, 9, 27)
        sho = sb("sho", 1, 12, 9)
        ab = sb("ab", 3, 12)
        dn = sb("dn", 12, 3, H)
        gb8 = sb("gb8", 2, NT, rows=N_EXP)
        gb = gb8[0:H, :, :]
        decay = sb("decay", 3, 12)
        stat = sb("stat", 3, 12)
        EPS = [NORM_EPS, L2_EPS, RW_GN_EPS, RT_GN_EPS, -math.log(HD) / 2]
        eps_cols = sb("eps_cols", len(EPS))
        eps = lambda k: eps_cols[:, k:k + 1]
        small = sb("small", 6, 3, N_EXP)
        route = sb("route", 2, 3, N_EXP + 1)
        zeros = ctx.enter_context(nc.sbuf_tensor("zeros", [32, 512], mybir.dt.bfloat16))
        more = ctx.enter_context(nc.sbuf_tensor("more", [1, 1], mybir.dt.int32))
        hn = [conv[:, 0:4, :].rearrange("p a b -> p (a b)")[:, 0:D], conv[:, 4:8, :].rearrange("p a b -> p (a b)")[:, 0:D]]

        def hn_at(use, t):
            return hn_last if use and t == 2 else hn[t % 2]
        OT = hT
        SQ = R.rearrange("p a b c -> p (a b c)")[:, 0:6 * NT].rearrange("p (a b) -> p a b", b=NT)
        eg, KK = gate, gate
        hid = [zs[:, s, :] for s in range(SLOTS)]
        silu_h = zs[:, SLOTS, :]
        tail = SLOTS * SLOT
        lnf = ring[:, tail:tail + D]
        hn_last = ring[:, tail + D:tail + 2 * D]
        iota = ring[:, tail + 2 * D:tail + 2 * D + P]
        before = ring[:, tail + 2 * D + P:tail + 2 * D + 2 * P]
        spare = hT[:, :, :].rearrange("p a b -> p (a b)")
        hG = spare[:, 0:KD * CAP].rearrange("p (k s) -> p k s", k=KD)
        y_exp = spare[:, KD * CAP:KD * CAP + D]
        hot, hot_w, hot_t = TT[:, 0, :, :], TT[:, 1, :, :], TM[:, 0, :, :]
        pair_sel = bonus[0:H, :, :].rearrange("p a b -> p (a b)")[:, 0:H * HD]
        junk = zs[:, 0:4, :].rearrange("p a b -> p (a b)")[:, 0:D]
        rt_qd = EI[:, 0, 0:32]
        omka = stat[:, 0, 9:12]

        banks = [ctx.enter_context(nc.psum_tensor(f"bank{b}", [P, 512], F32)) for b in range(8)]

        def cst(name, a=0, n=None, rows=P):
            at, size = CAT[name]
            return C[0:rows, at + a:at + a + (size - a if n is None else n)]

        def par(layer, name, k=0, n=1):
            at = PAT[name][0] + k
            return PC[:, layer, at:at + n]

        def over(a, n, at=1):
            shape = list(a.shape)
            shape.insert(at, n)
            return a.unsqueeze(at).to_broadcast(shape)

        ident = cst("ident")
        tri = [cst("tri"), cst("tri"), cst("tri_s", rows=32)]
        neg = [cst("neg"), cst("neg"), cst("neg_s", rows=32)]
        LEVELS = [6, 6, 2]
        seqs = lambda a: a.rearrange("p m (b s) -> p m b s", b=NB)

        def sig(name, per, step=1):
            return Signal(name, per, step)

        loaded = [sig(f"wslot{s}_loaded", MIX_LOADS // 2, 16) for s in range(2)]
        out_ok = sig("out_columns_added", len(WOUT_LOADS))
        block_loaded = [ctx.enter_context(nc.semaphore(f"block_slot{s}_loaded")) for s in range(SLOTS)]
        bank_full = [ctx.enter_context(nc.semaphore(f"bank{b}_full")) for b in range(8)]
        bank_free = [ctx.enter_context(nc.semaphore(f"bank{b}_free")) for b in range(8)]
        inputs = ctx.enter_context(nc.semaphore("inputs_loaded"))
        stored = sig("outputs_stored", 5, 16)
        lora_loaded = sig("lora_loaded", 3, 16)
        seq_states = sig("conv_shift_states_loaded", 2, 16)
        rt_state_in = sig("rt_state_loaded", 1, 16)
        rt_state_out = sig("rt_state_stored", 1, 16)
        ss_in = sig("sample_state_loaded", 2, 16)
        ss_out = sig("sample_state_stored", 2, 16)
        dve_seq = ctx.enter_context(nc.semaphore("vector_steps"))
        act_seq = ctx.enter_context(nc.semaphore("scalar_steps"))
        ssq_ok = sig("squares_summed", 6)
        rstd_ok = sig("rstd_ready", 6)
        hn_ok = sig("normed", 6)
        hT_ok = sig("hT_ready", 12)
        ab_ok = sig("ab_ready", 1)
        zeroed = sig("pads_zeroed", 1)
        z_ok = sig("z_ready", 30)
        pads_ok = sig("pads_ready", 1)
        conv_ok = sig("conv_summed", 3)
        qkv_ok = sig("qkv_ready", 3)
        cvo_ok = sig("conv_tail_ready", 1)
        sho_ok = sig("shift_tail_ready", 1)
        zs_ok = sig("shifted", 1)
        lora_ok = sig("lora_inputs_ready", 1)
        sg_ok = sig("decay_sigmoid_ready", 3)
        aT_ok = sig("a_ready", 3)
        gT_ok = sig("g_ready", 1)
        beta_ok = sig("beta_ready", 1)
        negA_ok = sig("neg_A_ready", 1)
        dtb_ok = sig("dt_biased", 1)
        sp_ok = sig("softplus_log_ready", 1)
        g_ok = sig("g_log_decay_ready", 1)
        cum_ok = sig("cum_ready", 1)
        gb_ok = sig("g_beta_rows_ready", 1)
        egn_ok = sig("cum_exp_ready", 1)
        sq_ok = sig("qk_squares", 1)
        rn_ok = sig("qk_rnorm", 6)
        eg_ok = sig("eg_ready", 3)
        Q_ok = sig("queries_ready", 1)
        nat_ok = sig("naturals_ready", 3)
        natb_ok = sig("naturals_copied", 3)
        DI_ok = sig("pair_decays", 6)
        R_ok = sig("products_ready", 36)
        T_ok = sig("inverse_ready", 2 * 2 * (6 + 6 + 2))
        XM_ok = sig("masked_ready", 2 * 2 * (6 + 6 + 2))
        XV_ok = sig("av_ready", 3)
        U0_ok = sig("u0_ready", 6)
        W_ok = sig("w_ready", 6)
        U_ok = sig("u_ready", 10)
        O_ok = sig("o_ready", 8)
        Os_ok = sig("sample_o_ready", 2)
        S_ok = sig("state_ready", 8)
        USO_ok = sig("sample_state_read", 2)
        UX_ok = sig("spread_ready", 6)
        SS_ok = sig("sample_state_updated", 2)
        kk_sq = sig("kk_squares", 1)
        kk_rn = sig("kk_rnorm", 3)
        kk_ok = sig("kk_ready", 1)
        rk_ok = sig("rk_products", 1)
        E_ok = sig("rw_decays", 3)
        keys_ok = sig("rw_keys_ready", 3)
        rot_ok = sig("rotated", 1)
        rtk_ok = sig("rt_natural_ready", 3)
        rtR_ok = sig("rt_products", 8)
        rtO_ok = sig("rt_o_ready", 2)
        rtC_ok = sig("rt_cross_ready", 2)
        rtX_ok = sig("rt_spread_ready", 4)
        rtS_ok = sig("rt_state_updated", 1)
        rtSp_ok = sig("rt_prompt_state_ready", 1)
        dev_ok = sig("deviations_ready", 2)
        osq_ok = sig("o_squares_ready", 3)
        orn_ok = sig("o_rnorm_ready", 8)
        cat_ok = sig("mixed_ready", 1)
        X_ok = sig("x_mixed", 1)
        chosen_ok = sig("chosen_ready", 1)
        h1_full = ctx.enter_context(nc.semaphore("h1_full"))
        h3_full = ctx.enter_context(nc.semaphore("h3_full"))
        silu_done = ctx.enter_context(nc.semaphore("silu_done"))
        hid_ok = ctx.enter_context(nc.semaphore("hidden_ready"))
        hid_used = ctx.enter_context(nc.semaphore("hidden_used"))
        final_ok = sig("y_ready", 3)
        fss_ok = sig("last_squares_summed", 3)
        frs_ok = sig("last_rstd_ready", 3)
        diff_ok = sig("logit_difference", 1)
        odds_ok = sig("odds_ready", 1)
        def counter(name):
            return ctx.enter_context(nc.semaphore(name))

        route_in = counter("route_constants_loaded")
        pos_ok = counter("slots_assigned")
        more_ok = counter("overflow_flag_ready")
        lowered = counter("slots_lowered")
        hot_ok = counter("one_hots_built")
        gathered = counter("gathered_halves")
        hot_t_full = counter("one_hots_transposed")
        hot_t_ok = counter("one_hots_by_slot_ready")
        hG_ok = counter("expert_input_halves_ready")
        y_in = counter("expert_output_halves_ready")
        spread_full = counter("outputs_spread")
        x_added = counter("outputs_added")
        lnf_in = ctx.enter_context(nc.semaphore("last_norm_weights_loaded"))
        y_stored = ctx.enter_context(nc.semaphore("y_stored"))
        eps_ok = ctx.enter_context(nc.semaphore("eps_ready"))

        fills = {}

        def fill(pe, *key):
            b, turn = len(fills) % 8, len(fills) // 8
            assert key not in fills, key
            fills[key] = (b, turn)
            if turn:
                pe.wait_ge(bank_free[b], turn)
            return banks[b], bank_full[b]

        def take(eng, *key):
            b, turn = fills[key]
            eng.wait_ge(bank_full[b], turn + 1)
            return banks[b], bank_free[b]

        def mm(pe, out, lhsT, rhs, start=True, stop=True):
            return nc.tensor.matmul(out, lhsT, rhs, start=start, stop=stop, skip_group_check=True)

        def tr(pe, out, in_):
            n = in_.shape[0]
            return nc.tensor.transpose(out, in_, ident[0:n, 0:n])

        def half(h):
            return slice(64 * (h % 2), 64 * (h % 2) + 64), h // 2

        block = ctx.enter_context(nc.Block())
        N_IN = 5
        FFN_USES = [len(range(s, FFN_BLOCKS, SLOTS)) for s in range(SLOTS)]
        ROUND_TURNS = MOE_BLOCKS // SLOTS
        EXP_TURNS = EXP_BLOCKS // SLOTS
        SPREAD = [2, 3, 4, 5, 0, 1]

        def expert_rounds(eng, expert, start=lambda r: None):
            start(0)
            with eng.Fori(0, N_EXP) as e:
                expert(0, e)
            eng.wait_ge(more_ok, 1)
            overflow = eng.value_load(more[0:1, 0:1], min_val=0, max_val=1)
            with eng.If(overflow > 0):
                with eng.Fori(1, -(-NT // CAP)) as r:
                    start(r)
                    with eng.Fori(0, N_EXP) as e:
                        expert(r, e)

        @block.tensor
        def _(pe):
            def norm_transposes(l, use):
                for t, (t0, n) in enumerate(TILES):
                    u = use * 3 + t
                    wait(pe, hn_ok, l, u)
                    for part in range(2):
                        b, full = fill(pe, l, "hT", u, part)
                        for q in range(4):
                            k = part * 4 + q
                            i = tr(pe, b[:, q * P:q * P + n], hn_at(use, t)[0:n, k * P:(k + 1) * P])
                        i.then_inc(full, 1)

            def project(l):
                wait(pe, hT_ok, l, 5)
                tiles = list(enumerate(ZTILES))
                for i, (c0, c1) in enumerate(WIN_LOADS):
                    wait(pe, loaded[i % 2], l, i // 2)
                    w = wslot[i % 2][:, 0:KD * (c1 - c0)].rearrange("p (k c) -> p k c", k=KD)
                    last = None
                    if i == AB_LOAD:
                        b, full = fill(pe, l, "ab")
                        for t, (t0, n) in enumerate(TILES):
                            for k in range(KD):
                                last = mm(pe, b[0:n, t * 12:t * 12 + 12], hT[:, k, t0:t0 + n], w[:, k, 0:12],
                                          start=k == 0, stop=k == KD - 1)
                        last.then_inc(full, 1)
                    while tiles and tiles[0][1][2] < c1:
                        m, (_, _, c, n) = tiles.pop(0)
                        b, full = fill(pe, l, "z", m)
                        for k in range(KD):
                            last = mm(pe, b[0:n, 0:NT], w[:, k, c - c0:c - c0 + n], hT[:, k, :],
                                      start=k == 0, stop=k == KD - 1)
                        last.then_inc(full, 1)

            def lora(l):
                wait(pe, lora_loaded, l, 2)
                wait(pe, lora_ok, l, 0)
                for t, (t0, n) in enumerate(TILES):
                    b, full = fill(pe, l, "y", t)
                    mm(pe, b[0:n, 0:384], cst("ones", 0, n, rows=1), w0[:, :], stop=False)
                    mm(pe, b[0:n, 0:384], zs[0:64, 9, t0:t0 + n], w2a2[0:64, :], start=False).then_inc(full, 1)
                for f in range(3):
                    b, full = fill(pe, l, "a", f)
                    mm(pe, b[:, 0:NT], w2a2[64:128, f * P:(f + 1) * P], zs[64:128, 9, :]).then_inc(full, 1)
                for f in range(3):
                    b, full = fill(pe, l, "g", f)
                    mm(pe, b[:, 0:NT], g2[:, 0, f * P:(f + 1) * P], zs[:, 10, :], stop=False)
                    mm(pe, b[:, 0:NT], g2[0:32, 1, f * P:(f + 1) * P], zs[0:32, 11, :], start=False).then_inc(full, 1)

            def dn_prepare(l):
                wait(pe, sq_ok, l, 0)
                for i in range(6):
                    b, full = fill(pe, l, "dnss", i)
                    mm(pe, b[:, 0:NT], cst("ones64"), SQ[:, i, :]).then_inc(full, 1)
                wait(pe, g_ok, l, 0)
                wait(pe, beta_ok, l, 0)
                b, full = fill(pe, l, "cum")
                for t, (t0, n) in enumerate(TILES):
                    mm(pe, b[0:n, t * 12:t * 12 + 6], tri[t][:, 0:n], dn[0:n, 0, t, :])
                    i = mm(pe, b[0:n, t * 12 + 6:t * 12 + 12], tri[t][:, 2 * n:3 * n], dn[0:n, 0, t, :])
                i.then_inc(full, 1)
                b, full = fill(pe, l, "rows_g")
                for t, (t0, n) in enumerate(TILES):
                    i = mm(pe, b[0:H, t0:t0 + n], dn[0:n, 0, t, :], tri[t][:, 0:n])
                i.then_inc(full, 1)
                b, full = fill(pe, l, "rows_b")
                for t, (t0, n) in enumerate(TILES):
                    i = mm(pe, b[0:H, t0:t0 + n], dn[0:n, 1, t, :], ident[0:n, 0:n])
                i.then_inc(full, 1)
                wait(pe, gb_ok, l, 0)
                for p in range(3):
                    sel = pair_sel[:, p * P:(p + 1) * P]
                    b, full = fill(pe, l, "bc_g", p)
                    mm(pe, b[:, 0:NT], sel, gb[:, 0, :]).then_inc(full, 1)
                    b, full = fill(pe, l, "bc_b", p)
                    mm(pe, b[:, 0:NT], sel, gb[:, 1, :]).then_inc(full, 1)

            def dn_tile(l, t):
                t0, n = TILES[t]
                wait(pe, Q_ok, l, 0)
                for name, m in (("k", 3), ("v", 6)):
                    b, full = fill(pe, l, "dn" + name, t)
                    for p in range(3):
                        i = tr(pe, b[0:n, p * P:(p + 1) * P], conv[:, m + p, t0:t0 + n])
                    i.then_inc(full, 1)
                for g in range(2):
                    b, full = fill(pe, l, "E", t, g)
                    for x in range(3):
                        h = 3 * g + x
                        mm(pe, b[0:n, x * n:(x + 1) * n], ident[0:H, h:h + 1].to_broadcast([H, n]), gb[:, 0, t0:t0 + n], stop=False)
                        i = mm(pe, b[0:n, x * n:(x + 1) * n], ident[0:n, 0:n], neg[t][:, 0:n], start=False)
                    i.then_inc(full, 1)
                    for x in range(3):
                        s, p = half(3 * g + x)
                        b, full = fill(pe, l, 0, "products", t, 3 * g + x)
                        mm(pe, b[0:n, 0:2 * n].rearrange("p (a b) -> p a b", a=2), conv[s, 3 + p, t0:t0 + n],
                           Q[s, p, 0:2, t0:t0 + n]).then_inc(full, 1)

            def rw_prepare(l):
                wait(pe, kk_sq, l, 0)
                for f in range(3):
                    b, full = fill(pe, l, "kss", f)
                    mm(pe, b[:, 0:NT], cst("ones64"), SQ[:, f, :]).then_inc(full, 1)
                wait(pe, rk_ok, l, 0)
                for f in range(3):
                    b, full = fill(pe, l, "bonus", f)
                    mm(pe, b[:, 0:NT], cst("ones64"), SQ[:, 3 + f, :]).then_inc(full, 1)

            def rw_tile(l, t):
                t0, n = TILES[t]
                wait(pe, sg_ok, l, t)
                for f in range(3):
                    b, full = fill(pe, l, "cumw", t, f)
                    mm(pe, b[:, 0:3 * n], sg[0:n, t, f * P:(f + 1) * P], tri[t]).then_inc(full, 1)
                wait(pe, keys_ok, l, t)
                srcs = [Q[:, :, 1, t0:t0 + n], ends[:, 0, :, 0:n], zs[:, 6:9, t0:t0 + n], ends[:, 1, :, 0:n]]
                for k, src in enumerate(srcs):
                    b, full = fill(pe, l, "rwnat", t, k)
                    for p in range(3):
                        i = tr(pe, b[0:n, p * P:(p + 1) * P], src[:, p, :])
                    i.then_inc(full, 1)
                for h in range(H):
                    s, p = half(h)
                    b, full = fill(pe, l, 1, "products", t, h)
                    for k in range(2):
                        i = mm(pe, b[0:n, 2 * k * n:2 * (k + 1) * n].rearrange("p (a b) -> p a b", a=2),
                               keys[s, k, p, 0:n], Q[s, p, 0:2, t0:t0 + n])
                    i.then_inc(full, 1)

            def inverses(l, y, t):
                n = TILES[t][1]
                done = (y * 14 + sum(LEVELS[:t])) * 2
                for g in range(2):
                    wait(pe, R_ok, l, y * 18 + t * 6 + 3 * g + 2)
                    b, full = fill(pe, l, y, "L0", t, g)
                    for x in range(3):
                        i = tr(pe, b[0:n, x * n:(x + 1) * n], R[0:n, 3 * g + x, 1, 0:n])
                    i.then_inc(full, 1)
                for lev in range(1, LEVELS[t]):
                    for g in range(2):
                        wait(pe, T_ok, l, done + (lev - 1) * 2 + g)
                        b, full = fill(pe, l, y, "AT", t, lev, g)
                        for x in range(3):
                            i = mm(pe, b[0:n, x * n:(x + 1) * n], R[0:n, 3 * g + x, 1, 0:n], TM[0:n, g, x, 0:n])
                        i.then_inc(full, 1)
                    for g in range(2):
                        wait(pe, XM_ok, l, done + lev * 2 + g)
                        b, full = fill(pe, l, y, "TX", t, lev, g)
                        for x in range(3):
                            i = mm(pe, b[0:n, x * n:(x + 1) * n], TT[0:n, g, x, 0:n], XM[0:n, g, x, 0:n])
                        i.then_inc(full, 1)
                        b, full = fill(pe, l, y, "XT", t, lev, g)
                        for x in range(3):
                            i = mm(pe, b[0:n, x * n:(x + 1) * n], XM[0:n, g, x, 0:n], TT[0:n, g, x, 0:n])
                        i.then_inc(full, 1)
                for g in range(2):
                    wait(pe, T_ok, l, done + (LEVELS[t] - 1) * 2 + g)

            def chunk_inputs(l, y, t):
                n = TILES[t][1]
                wait(pe, natb_ok if y else nat_ok, l, t)
                if y:
                    b, full = fill(pe, l, "XV", t)
                    for h in range(H):
                        i = mm(pe, b[0:n, h * HD:(h + 1) * HD], R[0:n, h, 3, 0:n], nat[0:n, 2, h, :])
                    i.then_inc(full, 1)
                b, full = fill(pe, l, y, "W", t)
                for h in range(H):
                    s, p = half(h)
                    i = mm(pe, b[s, p * n:(p + 1) * n], nat[0:n, 0, h, :], TT[0:n, h // 3, h % 3, 0:n])
                i.then_inc(full, 1)
                if y:
                    wait(pe, XV_ok, l, t)
                v = U if y else nat[:, 2, :, :]
                b, full = fill(pe, l, y, "U0", t)
                for h in range(H):
                    i = mm(pe, b[0:n, h * HD:(h + 1) * HD], TT[0:n, h // 3, h % 3, 0:n], v[0:n, h, :])
                i.then_inc(full, 1)

            def prompt_chunk(l, y, c):
                t, cc = c // 2, c % 2
                rows = slice(64 * cc, 64 * cc + 64)
                cols = slice(CHUNK * c, CHUNK * (c + 1))
                st = S[:, y, :, :]
                if c:
                    wait(pe, W_ok, l, y * 3 + t)
                    wait(pe, S_ok, l, y * 4 + c - 1)
                    for odd in range(2):
                        b, full = fill(pe, l, y, "WS", c, odd)
                        for p in range(3):
                            s = slice(64 * odd, 64 * odd + 64)
                            i = mm(pe, b[rows, p * HD:(p + 1) * HD], Q[s, p, 3, cols], st[s, p, :])
                        i.then_inc(full, 1)
                wait(pe, U_ok, l, y * 5 + c)
                b, full = fill(pe, l, y, "O", c)
                for h in range(H):
                    s, p = half(h)
                    out = b[s, p * CHUNK:(p + 1) * CHUNK]
                    inner = slice(64 * cc, 64 * cc + 64)
                    if c:
                        mm(pe, out, st[s, p, :], Q[s, p, 0 if y else 2, cols], stop=False)
                    if y:
                        mm(pe, out, nat[:, 2, h, :], R[:, h, 2, inner], start=c == 0, stop=False)
                    i = mm(pe, out, U[:, h, :], R[:, h, 0, inner], start=c == 0 and not y)
                i.then_inc(full, 1)
                b, full = fill(pe, l, y, "S", c)
                for h in range(H):
                    s, p = half(h)
                    out = b[s, p * HD:(p + 1) * HD]
                    if y:
                        mm(pe, out, nat[rows, 3, h, :], nat[rows, 2, h, :], stop=False)
                    i = mm(pe, out, nat[rows, 1, h, :], U[rows, h, :], start=not y)
                i.then_inc(full, 1)

            def sample_chunks(l, y):
                wait(pe, W_ok, l, y * 3 + 2)
                wait(pe, ss_in, l, y)
                b, full = fill(pe, l, y, "SU")
                for h in range(H):
                    s, p = half(h)
                    for q in range(NB):
                        cols = slice(SEQ + DS * q, SEQ + DS * (q + 1))
                        both = Q[s, p, 0:4:3, cols] if y else Q[s, p, 2:4, cols]
                        out = b[s, p * 64:(p + 1) * 64].rearrange("p (a b) -> p a b", a=2)[:, :, DS * q:DS * (q + 1)]
                        i = mm(pe, out, SS[s, p, q, :], both)
                i.then_inc(full, 1)
                wait(pe, USO_ok, l, y)
                b, full = fill(pe, l, y, "SUT")
                for p in range(3):
                    i = tr(pe, b[0:32, p * P:(p + 1) * P], USO[:, p, 1, :])
                i.then_inc(full, 1)
                wait(pe, U_ok, l, y * 5 + 4)
                b, full = fill(pe, l, y, "O", 4)
                for h in range(H):
                    s, p = half(h)
                    out = b[s, p * 32:(p + 1) * 32]
                    if y:
                        mm(pe, out, nat[0:32, 2, h, :], R[0:32, h, 2, 0:32], stop=False)
                    i = mm(pe, out, U[0:32, h, :], R[0:32, h, 0, 0:32], start=not y)
                i.then_inc(full, 1)
                for p in range(3):
                    wait(pe, UX_ok, l, y * 3 + p)
                    b, full = fill(pe, l, y, "SS", p)
                    for q in range(2):
                        h = 2 * p + q
                        s = half(h)[0]
                        flat = lambda k: UX[0:32, k, :, :].rearrange("p a b -> p (a b)")
                        if y:
                            mm(pe, b[s, :], nat[0:32, 3, h, :], flat(2 + q), stop=False)
                        i = mm(pe, b[s, :], nat[0:32, 1, h, :], flat(q), start=not y)
                    i.then_inc(full, 1)

            def retention(l):
                wait(pe, z_ok, l, 29)
                for k in range(2):
                    b, full = fill(pe, l, "rot", k)
                    mm(pe, b[:, 0:NT], cst("rot"), rtz[:, k, :]).then_inc(full, 1)
                wait(pe, rot_ok, l, 0)
                for t, (t0, n) in enumerate(TILES):
                    b, full = fill(pe, l, "rtn", t)
                    for k, src in enumerate([aT[:, 2, t0:t0 + n], rtz[:, 2, t0:t0 + n], rtz[:, 3, t0:t0 + n]]):
                        i = tr(pe, b[0:n, k * P:(k + 1) * P], src)
                    i.then_inc(full, 1)
                q, k = aT[:, 0, :], aT[:, 1, :]
                for h in range(RT_H):
                    s = slice(32 * h, 32 * h + 32)
                    b, full = fill(pe, l, "rtp", h)
                    mm(pe, b[:, 0:SEQ], k[s, 0:P], q[s, 0:SEQ])
                    mm(pe, b[:, SEQ:SEQ + P], k[s, P:SEQ], q[s, P:SEQ]).then_inc(full, 1)
                for h in range(RT_H):
                    s = slice(32 * h, 32 * h + 32)
                    b, full = fill(pe, l, "rtp", 4 + h)
                    mm(pe, b[0:32, 0:32], k[s, SEQ:NT], q[s, SEQ:NT]).then_inc(full, 1)
                wait(pe, rtR_ok, l, 7)
                wait(pe, rtk_ok, l, 2)
                wait(pe, rt_state_in, l, 0)
                rp = R.rearrange("p a b c -> p (a b c)")
                rs = keys.rearrange("p a b c -> p (a b c)")
                nat_rt = lambda t: sg[:, t, :]
                V = lambda t, h: nat_rt(t)[:, P + h * HD:P + (h + 1) * HD]
                Kn = lambda t, h: nat_rt(t)[:, 32 * h:32 * h + 32]
                for p in range(2):
                    b, full = fill(pe, l, "rto", p)
                    for hh in range(2):
                        h, s = 2 * p + hh, slice(64 * hh, 64 * hh + 64)
                        m = rp[:, h * 384:(h + 1) * 384]
                        mm(pe, b[s, 0:P], V(0, h), m[:, 0:P])
                        mm(pe, b[s, P:SEQ], V(0, h), m[:, P:SEQ], stop=False)
                        mm(pe, b[s, P:SEQ], V(1, h), m[:, SEQ:SEQ + P], start=False)
                        i = mm(pe, b[s, SEQ:NT], V(2, h)[0:32, :], rs[0:32, 32 * h:32 * h + 32])
                    i.then_inc(full, 1)
                    b, full = fill(pe, l, "rtc", p)
                    for hh in range(2):
                        h, s = 2 * p + hh, slice(64 * hh, 64 * hh + 64)
                        k4 = slice(32 * h, 32 * h + 32)
                        for x in range(NB):
                            i = mm(pe, b[s, DS * x:DS * (x + 1)], SSr[k4, x, :], rt_qd[k4, DS * x:DS * (x + 1)])
                    i.then_inc(full, 1)
                b, full = fill(pe, l, "rts")
                for h in range(RT_H):
                    s = slice(32 * h, 32 * h + 32)
                    mm(pe, b[s, 0:HD], Kn(0, h), V(0, h), stop=False)
                    i = mm(pe, b[s, 0:HD], Kn(1, h), V(1, h), start=False)
                i.then_inc(full, 1)
                b, full = fill(pe, l, "rtss")
                for h in range(RT_H):
                    wait(pe, rtX_ok, l, h)
                    i = mm(pe, b[32 * h:32 * h + 32, :], Kn(2, h)[0:32, :], UX[0:32, h, :, :].rearrange("p a b -> p (a b)"))
                i.then_inc(full, 1)

            def out_norms(l):
                for y, (a, n) in enumerate(((3, 3), (6, 2))):
                    if y == 0:
                        wait(pe, O_ok, l, 7)
                        wait(pe, Os_ok, l, 1)
                    else:
                        wait(pe, rtO_ok, l, 1)
                    for p in range(a, a + n):
                        b, full = fill(pe, l, "mean", p)
                        mm(pe, b[:, 0:NT], cst("mean64"), OT[:, p, :]).then_inc(full, 1)
                for y, (a, n) in enumerate(((0, 3), (3, 3), (6, 2))):
                    wait(pe, osq_ok, l, y)
                    for p in range(a, a + n):
                        b, full = fill(pe, l, "var", p)
                        mm(pe, b[:, 0:NT], cst("mean64"), conv[:, p, :]).then_inc(full, 1)

            def out_projection(l):
                wait(pe, cat_ok, l, 0)
                for c, (c0, c1) in enumerate(WOUT_LOADS):
                    n_load = len(WIN_LOADS) + c
                    s = n_load % 2
                    wait(pe, loaded[s], l, n_load // 2)
                    w = wslot[s][:, 0:KD * (c1 - c0)].rearrange("p (k c) -> p k c", k=KD)
                    for t, (t0, n) in enumerate(TILES):
                        b, full = fill(pe, l, "out", t, c)
                        for k in range(KD):
                            i = mm(pe, b[0:n, 0:c1 - c0], OT[:, k, t0:t0 + n], w[:, k, :], start=k == 0, stop=k == KD - 1)
                        i.then_inc(full, 1)

            def routing(l):
                b, full = fill(pe, l, "logits")
                for t, (t0, n) in enumerate(TILES):
                    for k in range(KD):
                        i = mm(pe, b[0:n, t * N_EXP:(t + 1) * N_EXP], hT[:, k, t0:t0 + n], rt_w[:, k, :],
                               start=k == 0, stop=k == KD - 1)
                i.then_inc(full, 1)
                wait(pe, chosen_ok, 0, 0)
                pe.wait_ge(route_in, 16)
                b, full = fill(pe, l, "slots")
                for t, (t0, n) in enumerate(TILES):
                    for x in range(t):
                        mm(pe, b[0:n, t * N_EXP:(t + 1) * N_EXP], cst("ones", 0, n), small[:, 1, x, :], start=x == 0, stop=False)
                    mm(pe, b[0:n, t * N_EXP:(t + 1) * N_EXP], before[0:n, 0:n], small[0:n, 1, t, :], start=t == 0)
                for t, (t0, n) in enumerate(TILES):
                    i = mm(pe, b[:, 3 * N_EXP:4 * N_EXP], cst("ones", rows=n), small[0:n, 1, t, :], start=t == 0, stop=t == 2)
                i.then_inc(full, 1)

            def hidden(s, turn, tile, src, n):
                w13 = ring[:, s * SLOT:s * SLOT + 2 * KD * FB].rearrange("p (x k f) -> p x k f", x=2, k=KD)
                pe.wait_ge(block_loaded[s], 16 * (turn + 1))
                for x, (full, free) in enumerate(((h1_full, silu_done), (h3_full, hid_ok))):
                    if not (isinstance(tile, int) and tile == 0):
                        pe.wait_ge(free, tile)
                    for k in range(KD):
                        i = mm(pe, banks[6 + x][:, 0:n], w13[:, x, k, :], src[:, k, 0:n], start=k == 0, stop=k == KD - 1)
                    i.then_inc(full, 1)

            def down(s, tile, outs, start, stop):
                w2 = ring[:, s * SLOT + 2 * KD * FB:(s + 1) * SLOT]
                pe.wait_ge(hid_ok, tile + 1)
                for bank, (t0, n) in outs:
                    for c in range(2):
                        i = mm(pe, banks[bank + c][0:n, :], hid[s][:, t0:t0 + n], w2[:, c * 512:(c + 1) * 512], start=start, stop=stop)
                i.then_inc(hid_used, 1)

            def turn_of_ring(slots, turns, tile0, src, n, outs, first=False, last=False):
                for s in range(slots):
                    hidden(s, turns[s], tile0 + s, src, n)
                    if s:
                        down(s - 1, tile0 + s - 1, outs, first and s == 1, False)
                down(slots - 1, tile0 + slots - 1, outs, first and slots == 1, last)

            def dense(l):
                for b in range(8):
                    pe.wait_ge(bank_free[b], len([1 for v in fills.values() if v[0] == b]))
                turns, rest = divmod(FFN_BLOCKS, SLOTS)
                outs = [(2 * t, tile) for t, tile in enumerate(TILES)]
                turn_of_ring(SLOTS, [0] * SLOTS, 0, hT, NT, outs, first=True)
                with pe.Fori(1, turns) as i:
                    turn_of_ring(SLOTS, [i] * SLOTS, i * SLOTS, hT, NT, outs)
                turn_of_ring(rest, [turns] * rest, turns * SLOTS, hT, NT, outs, last=True)

            def expert(r, e):
                job = r * N_EXP + e
                pe.wait_ge(hot_ok, 6 * (r * (N_EXP + 1) + e + 1))
                pe.wait_ge(x_added, 6 * job + 1)
                for part in range(2):
                    for q in range(4):
                        k = 4 * part + q
                        for t, (t0, n) in enumerate(TILES):
                            i = mm(pe, banks[2 + part][:, q * CAP:(q + 1) * CAP], hn_at(1, t)[0:n, k * P:(k + 1) * P],
                                   hot[0:n, t, :], start=t == 0, stop=t == 2)
                    i.then_inc(gathered, 1)
                for t, (t0, n) in enumerate(TILES):
                    i = tr(pe, banks[4][:, t0:t0 + n], hot_w[0:n, t, :])
                i.then_inc(hot_t_full, 1)
                for c in range(2):
                    nc.tensor.matmul(banks[c][:, :], zeros[:, 0:P], zeros[:, :], start=True, stop=False, skip_group_check=True)
                with pe.Fori(0, EXP_TURNS) as i:
                    turn = job * EXP_TURNS + i
                    pe.wait_ge(hG_ok, 2 * (job + 1))
                    turn_of_ring(SLOTS, [FFN_USES[s] + turn for s in range(SLOTS)], FFN_BLOCKS + turn * SLOTS, hG, CAP,
                                 [(0, (0, CAP))])
                pe.wait_ge(hot_t_ok, job + 1)
                pe.wait_ge(y_in, 2 * (job + 1))
                for t, (t0, n) in enumerate(TILES):
                    for c in range(2):
                        mm(pe, banks[SPREAD[2 * t + c]][0:n, :], hot_at(t), y_exp[:, c * 512:(c + 1) * 512]).then_inc(spread_full, 1)

            def hot_at(t):
                t0, n = TILES[t]
                return TM[:, 0, :, :].rearrange("p a b -> p (a b)")[:, t0:t0 + n]

            pe.wait_ge(inputs, 16 * N_IN)
            for l in range(DEPTH):
                norm_transposes(l, 0)
                project(l)
                lora(l)
                dn_prepare(l)
                for y in range(2):
                    if y:
                        rw_prepare(l)
                    for t in range(3):
                        (rw_tile if y else dn_tile)(l, t)
                        inverses(l, y, t)
                        chunk_inputs(l, y, t)
                        if t < 2:
                            prompt_chunk(l, y, 2 * t)
                            prompt_chunk(l, y, 2 * t + 1)
                        else:
                            sample_chunks(l, y)
                retention(l)
                out_norms(l)
                out_projection(l)
                norm_transposes(l, 1)
                wait(pe, hT_ok, l, 11)
                if l == 0:
                    dense(l)
                else:
                    routing(l)
                    for b in range(8):
                        pe.wait_ge(bank_free[b], len([1 for v in fills.values() if v[0] == b]))
                    expert_rounds(pe, expert)

        @block.vector
        def _(dve):
            V = nc.vector
            steps = [0]

            def own(ins):
                steps[0] += 1
                ins.then_inc(dve_seq, 1)
                return steps[0]

            def settle():
                dve.wait_ge(dve_seq, steps[0])

            def tt(out, a, b, op):
                return V.tensor_tensor(out, a, b, op)

            def norm(l, use):
                for t, (t0, n) in enumerate(TILES):
                    own(V.tensor_tensor_reduce(junk[0:n], X[0:n, t, :], X[0:n, t, :], 1.0, 0.0, MUL, ADD,
                                               stat[0:n, t, 0:1]))
                    settle()
                    V.nop().then_inc(ssq_ok.sem, 1)
                for t, (t0, n) in enumerate(TILES):
                    wait(dve, rstd_ok, l, use * 3 + t)
                    V.tensor_scalar(hn_at(use, t)[0:n], X[0:n, t, :], stat[0:n, t, 2:3], None, MUL).then_inc(hn_ok.sem, 1)
                    if t:
                        transposed(l, use, t - 1)
                transposed(l, use, 2)

            def transposed(l, use, t):
                t0, n = TILES[t]
                for part in range(2):
                    b, free = take(dve, l, "hT", use * 3 + t, part)
                    w = par(l, "ln_ffn" if use else "ln_mix", 4 * part, 4)
                    tt(hT[:, 4 * part:4 * part + 4, t0:t0 + n], b[:, :].rearrange("p (a b) -> p a b", a=4)[:, :, 0:n],
                       over(w, n, 2), MUL).then_inc(free, 1)
                    V.engine_nop().then_inc(hT_ok.sem, 1)

            def convolve(l):
                n = ZC - PADC
                for g in range(3):
                    wait(dve, z_ok, l, 3 * g + 2)
                    if g:
                        wait(dve, qkv_ok, l, g - 1)
                    for j in range(CONV_W):
                        for m in range(3):
                            w = par(l, "conv", 4 * (3 * g + m) + j)
                            src = zc[:, 3 * g + m, j:j + n]
                            if j == 0:
                                own(V.tensor_scalar(tmp3[:, m, 0:n], src, w, None, MUL))
                            elif j < CONV_W - 1 or m < 2:
                                own(V.scalar_tensor_tensor(tmp3[:, m, 0:n], src, w, tmp3[:, m, 0:n], MUL, ADD))
                            else:
                                V.scalar_tensor_tensor(tmp3[:, m, 0:n], src, w, tmp3[:, m, 0:n], MUL, ADD)\
                                    .then_inc(conv_ok.sem, 1)
                        settle()
                if l:
                    wait(dve, stored, l - 1, 4)
                own(V.tensor_copy(cvo[:, 0, :, 0:PADC], zc[:, :, SEQ:SEQ + PADC]))
                settle()
                V.tensor_copy(seqs(cvo[:, 0, :, PADC:]), seqs(zc[:, :, SEQ + PADC:])[:, :, :, DS:]).then_inc(cvo_ok.sem, 1)

            def gates(l):
                b, free = take(dve, l, "ab")
                own(V.tensor_copy(ab[:, 0:2, :], b[:, 0:24].rearrange("p (a b) -> p a b", a=2)))
                V.tensor_copy(ab[0:32, 2, :], b[0:32, 24:36]).then_inc(free, 1)
                dve.wait_ge(free, fills[(l, "ab")][1] + 1)
                settle()
                V.engine_nop().then_inc(ab_ok.sem, 1)
                tt(dn[:, 2, :, :], ab[:, :, 0:H], over(par(l, "dt", 0, H), 3), ADD).then_inc(dtb_ok.sem, 1)

            def shift(l):
                wait(dve, z_ok, l, 23)
                wait(dve, qkv_ok, l, 2)
                for g in range(4):
                    ms = slice(3 * g, 3 * g + 3)
                    own(tt(tmp3[:, :, 0:ZR - 1], zr[:, ms, 0:ZR - 1], zr[:, ms, 1:ZR], SUB))
                    settle()
                    for m in range(3 * g, 3 * g + 3):
                        x = tmp3[:, m - 3 * g, :]
                        own(V.scalar_tensor_tensor(zs[:, m, 0:SEQ], x[:, 0:SEQ], par(l, "mu", m), zr[:, m, 1:SEQ + 1], MUL, ADD))
                        own(V.scalar_tensor_tensor(zs[:, m, SEQ:].rearrange("p (b s) -> p b s", b=NB),
                                                   five(x, SEQ + 1),
                                                   par(l, "mu", m), five(zr[:, m, :], SEQ + 2), MUL, ADD))
                    settle()
                own(V.tensor_copy(sho[:, 0, :, 0:1], zr[:, :, SEQ:SEQ + 1]))
                settle()
                V.tensor_copy(sho[:, 0, :, 1:], zr[:, :, SEQ + 1:].rearrange("p m (b s) -> p m b s", s=DS + 1)[:, :, :, DS])\
                    .then_inc(sho_ok.sem, 1)
                wait(dve, sho_ok, l, 0)
                V.engine_nop().then_inc(zs_ok.sem, 1)

            def five(a, start):
                base = start - (SEQ + 1)
                return a[:, SEQ + 1:SEQ + 1 + NB * (DS + 1)].rearrange("p (b s) -> p b s", b=NB)[:, :, base:base + DS]

            def dn_prepare(l):
                tt(SQ[:, :, :], conv[:, 0:6, :], conv[:, 0:6, :], MUL).then_inc(sq_ok.sem, 1)
                wait(dve, dtb_ok, l, 0)
                own(V.tensor_scalar(dn[:, 4, :, :], dn[:, 2, :, :], 0.0, None, ALU.max))
                wait(dve, sp_ok, l, 0)
                settle()
                own(tt(dn[:, 4, :, :], dn[:, 4, :, :], dn[:, 3, :, :], ADD))
                wait(dve, negA_ok, l, 0)
                settle()
                V.scalar_tensor_tensor(dn[:, 0, :, :], dn[:, 4, :, :], -1.0, over(dn[:, 11, 0, :], 3), MUL, MUL)\
                    .then_inc(g_ok.sem, 1)
                b, free = take(dve, l, "cum")
                wait(dve, beta_ok, l, 0)
                c = b[:, 0:36].rearrange("p (t k h) -> p k t h", t=3, k=2)
                own(V.tensor_copy(dn[:, 5:7, 0:2, :], c[:, :, 0:2, :]))
                own(V.tensor_copy(dn[0:32, 5:7, 2, :], c[0:32, :, 2, :]))
                settle()
                V.tensor_scalar(dn[:, 10, :, :], dn[:, 5, :, :], -1.0, None, MUL).then_inc(cum_ok.sem, 1)
                V.engine_nop().then_inc(free, 1)
                own(V.tensor_copy(pair_sel.rearrange("p (h d) -> p h d", h=H), over(ident[0:H, 0:H], HD, 2)))
                settle()
                for k, name in enumerate(("rows_g", "rows_b")):
                    b, free = take(dve, l, name)
                    V.tensor_copy(gb[:, k, :], b[0:H, 0:NT]).then_inc(free, 1)
                    dve.wait_ge(free, fills[(l, name)][1] + 1)
                V.engine_nop().then_inc(gb_ok.sem, 1)
                wait(dve, rn_ok, l, 5)
                own(tt(Q[:, :, 0, :], conv[:, 0:3, :], SQ[:, 0:3, :], MUL))
                own(tt(conv[:, 3:6, :], conv[:, 3:6, :], SQ[:, 3:6, :], MUL))
                settle()
                for p in range(3):
                    b, free = take(dve, l, "bc_b", p)
                    tt(Q[:, p, 1, :], conv[:, 3 + p, :], b[:, 0:NT], MUL).then_inc(free, 1)
                wait(dve, eg_ok, l, 2)
                own(tt(Q[:, :, 2, :], Q[:, :, 0, :], eg[:, :, :], MUL))
                wait(dve, egn_ok, l, 0)
                own(tt(dn[:, 9, :, :], dn[:, 7, :, :], dn[:, 1, :, :], MUL))
                settle()
                V.engine_nop().then_inc(Q_ok.sem, 1)

            def dn_tile(l, t):
                n = TILES[t][1]
                heads = lambda b: b[0:n, 0:384].rearrange("p (h d) -> p h d", h=H)
                sc = lambda k: over(dn[0:n, k, t, :], HD, 2)
                b, free = take(dve, l, "dnk", t)
                own(tt(nat[0:n, 0, :, :], heads(b), sc(9), MUL))
                tt(nat[0:n, 1, :, :], heads(b), sc(8), MUL).then_inc(free, 1)
                dve.wait_ge(free, fills[(l, "dnk", t)][1] + 1)
                b, free = take(dve, l, "dnv", t)
                tt(nat[0:n, 2, :, :], heads(b), sc(1), MUL).then_inc(free, 1)
                dve.wait_ge(free, fills[(l, "dnv", t)][1] + 1)
                settle()
                V.engine_nop().then_inc(nat_ok.sem, 1)
                for h in range(H):
                    wait(dve, DI_ok, l, t * 2 + h // 3)
                    b, free = take(dve, l, 0, "products", t, h)
                    tt(R[0:n, h, 0:2, 0:n], b[0:n, 0:2 * n].rearrange("p (a b) -> p a b", a=2),
                       over(DI[0:n, h // 3, h % 3, 0:n], 2), MUL).then_inc(R_ok.sem, 1)
                    wait(dve, R_ok, l, t * 6 + h)
                    V.engine_nop().then_inc(free, 1)

            def inverses(l, y, t):
                n = TILES[t][1]
                done = (y * 14 + sum(LEVELS[:t])) * 2
                m = lambda a: over(a[0:n, 0:n], 3)
                three = lambda b: b[0:n, 0:3 * n].rearrange("p (a b) -> p a b", a=3)
                for g in range(2):
                    b, free = take(dve, l, y, "L0", t, g)
                    own(tt(TT[0:n, g, :, 0:n], R[0:n, 3 * g:3 * g + 3, 1, 0:n], m(cst("level0_t")), MUL))
                    tt(XM[0:n, g, :, 0:n], three(b), m(cst("level", 0, P)), MUL).then_inc(XM_ok.sem, 1)
                    wait(dve, XM_ok, l, done + g)
                    V.engine_nop().then_inc(free, 1)
                    settle()
                    own(tt(TM[0:n, g, :, 0:n], XM[0:n, g, :, 0:n], m(ident), ADD))
                    settle()
                    tt(TT[0:n, g, :, 0:n], TT[0:n, g, :, 0:n], m(ident), ADD).then_inc(T_ok.sem, 1)
                for lev in range(1, LEVELS[t]):
                    for g in range(2):
                        b, free = take(dve, l, y, "AT", t, lev, g)
                        tt(XM[0:n, g, :, 0:n], three(b), m(cst("level", lev * P, P)), MUL).then_inc(XM_ok.sem, 1)
                        wait(dve, XM_ok, l, done + lev * 2 + g)
                        V.engine_nop().then_inc(free, 1)
                    for g in range(2):
                        b, free = take(dve, l, y, "TX", t, lev, g)
                        tt(TM[0:n, g, :, 0:n], TM[0:n, g, :, 0:n], three(b), ADD).then_inc(free, 1)
                        dve.wait_ge(free, fills[(l, y, "TX", t, lev, g)][1] + 1)
                        b, free = take(dve, l, y, "XT", t, lev, g)
                        tt(TT[0:n, g, :, 0:n], TT[0:n, g, :, 0:n], three(b), ADD).then_inc(T_ok.sem, 1)
                        wait(dve, T_ok, l, done + lev * 2 + g)
                        V.engine_nop().then_inc(free, 1)

            def state_decay(y, p, c):
                return decay[:, p, c:c + 1] if y else eg[:, p, CHUNK * (c + 1) - 1:CHUNK * (c + 1)]

            def prompt_chunk(l, y, c):
                t, cc = c // 2, c % 2
                rows = slice(64 * cc, 64 * cc + 64)
                st = S[:, y, :, :]
                wait(dve, U0_ok, l, y * 3 + t)
                if cc == 0:
                    i = V.tensor_copy(U[:, :, :], U0[:, :, :])
                    if c:
                        own(i)
                        settle()
                    else:
                        i.then_inc(U_ok.sem, 1)
                if c:
                    for odd in range(2):
                        b, free = take(dve, l, y, "WS", c, odd)
                        heads = slice(odd, H, 2)
                        tt(U[rows, heads, :], U0[rows, heads, :], b[rows, 0:192].rearrange("p (a b) -> p a b", a=3), SUB)\
                            .then_inc(free, 1)
                        dve.wait_ge(free, fills[(l, y, "WS", c, odd)][1] + 1)
                    V.engine_nop().then_inc(U_ok.sem, 1)
                b, free = take(dve, l, y, "S", c)
                for p in range(3):
                    new = b[:, p * HD:(p + 1) * HD]
                    if c == 0:
                        i = V.tensor_copy(st[:, p, :], new)
                    else:
                        i = V.scalar_tensor_tensor(st[:, p, :], st[:, p, :], state_decay(y, p, c), new, MUL, ADD)
                    if p < 2:
                        own(i)
                settle()
                i.then_inc(S_ok.sem, 1)
                wait(dve, S_ok, l, y * 4 + c)
                V.engine_nop().then_inc(free, 1)

            def spread(out, src):
                return tt(out, over(src, NB, 1), over(cst("bmask", rows=32), HD, 2), MUL)

            def sample_chunks(l, y):
                flat = lambda a: a[0:32, :, :].rearrange("p a b -> p (a b)")
                b, free = take(dve, l, y, "SUT")
                wait(dve, U0_ok, l, y * 3 + 2)
                tt(flat(U), flat(U0), b[0:32, 0:384], SUB).then_inc(U_ok.sem, 1)
                wait(dve, U_ok, l, y * 5 + 4)
                V.engine_nop().then_inc(free, 1)
                b, free = take(dve, l, y, "O", 4)
                tt(OT[:, 3 * y:3 * y + 3, SEQ:], b[:, 0:96].rearrange("p (a b) -> p a b", a=3), USO[:, :, 0, :], ADD)\
                    .then_inc(Os_ok.sem, 1)
                wait(dve, Os_ok, l, y)
                V.engine_nop().then_inc(free, 1)
                for p in range(3):
                    own(spread(UX[0:32, 0, :, :], U[0:32, 2 * p, :]))
                    if y:
                        own(spread(UX[0:32, 2, :, :], nat[0:32, 2, 2 * p, :]))
                        own(spread(UX[0:32, 3, :, :], nat[0:32, 2, 2 * p + 1, :]))
                    own(spread(UX[0:32, 1, :, :], U[0:32, 2 * p + 1, :]))
                    settle()
                    V.engine_nop().then_inc(UX_ok.sem, 1)
                    dec = decay[:, p, 4:12] if y else eg[:, p, SEQ + DS - 1::DS]
                    own(tt(SS[:, p, :, :], SS[:, p, :, :], over(dec, HD, 2), MUL))
                    b, free = take(dve, l, y, "SS", p)
                    settle()
                    tt(SS[:, p, :, :], SS[:, p, :, :], b[:, :].rearrange("p (a b) -> p a b", a=NB), ADD).then_inc(free, 1)
                    dve.wait_ge(free, fills[(l, y, "SS", p)][1] + 1)
                V.engine_nop().then_inc(SS_ok.sem, 1)

            def rw_prepare(l):
                own(V.tensor_scalar(omka, par(l, "ka", 0, 3), -1.0, 1.0, MUL, ADD))
                for f in range(3):
                    own(V.tensor_scalar(KK[:, f, :], zs[:, 3 + f, :], par(l, "kk", f), None, MUL))
                settle()
                tt(SQ[:, 0:3, :], KK[:, :, :], KK[:, :, :], MUL).then_inc(kk_sq.sem, 1)
                wait(dve, aT_ok, l, 2)
                for f in range(3):
                    own(V.tensor_scalar(bonus[:, f, :], aT[:, f, :], par(l, "ka", f), omka[:, f:f + 1], MUL, ADD))
                settle()
                own(tt(zs[:, 3:6, :], zs[:, 3:6, :], bonus[:, :, :], MUL))
                settle()
                for f in range(3):
                    own(V.scalar_tensor_tensor(SQ[:, 3 + f, :], zs[:, f, :], par(l, "rk", f), zs[:, 3 + f, :], MUL, MUL))
                settle()
                V.engine_nop().then_inc(rk_ok.sem, 1)
                wait(dve, kk_rn, l, 2)
                own(tt(KK[:, :, :], KK[:, :, :], SQ[:, 0:3, :], MUL))
                settle()
                own(tt(aT[:, :, :], aT[:, :, :], KK[:, :, :], MUL))
                for f in range(3):
                    b, free = take(dve, l, "bonus", f)
                    tt(bonus[:, f, :], b[:, 0:NT], zs[:, 6 + f, :], MUL).then_inc(free, 1)
                    dve.wait_ge(free, fills[(l, "bonus", f)][1] + 1)
                settle()

            def rw_tile(l, t):
                t0, n = TILES[t]
                tok = slice(t0, t0 + n)
                wait(dve, E_ok, l, t)
                own(tt(Q[:, :, 0, tok], zs[:, 0:3, tok], E3[:, :, 0, 0:n], MUL))
                own(tt(Q[:, :, 1, tok], KK[:, :, tok], E3[:, :, 1, 0:n], MUL))
                own(tt(keys[:, 0, :, 0:n], aT[:, :, tok], EI[:, :, 0:n], MUL))
                own(tt(keys[:, 1, :, 0:n], zs[:, 3:6, tok], EI[:, :, 0:n], MUL))
                own(tt(ends[:, 0, :, 0:n], aT[:, :, tok], E3[:, :, 2, 0:n], MUL))
                own(tt(ends[:, 1, :, 0:n], zs[:, 3:6, tok], E3[:, :, 2, 0:n], MUL))
                if t < 2:
                    own(V.tensor_copy(decay[:, :, 2 * t:2 * t + 2], E3[:, :, 0, CHUNK - 1::CHUNK]))
                else:
                    own(V.tensor_copy(decay[:, :, 4:12], E3[:, :, 0, DS - 1:32:DS]))
                settle()
                V.engine_nop().then_inc(keys_ok.sem, 1)
                for h in range(H):
                    b, free = take(dve, l, 1, "products", t, h)
                    four = lambda a: a.rearrange("p (k a) c -> p k a c", k=2)
                    tt(four(R[0:n, h, :, :])[:, :, :, 0:n], b[0:n, 0:4 * n].rearrange("p (k a c) -> p k a c", k=2, a=2),
                       over(tri[t][:, 0:2 * n].rearrange("p (a c) -> p a c", a=2), 2), MUL).then_inc(R_ok.sem, 1)
                    wait(dve, R_ok, l, 18 + t * 6 + h)
                    V.engine_nop().then_inc(free, 1)

            def copy_av(l, t):
                n = TILES[t][1]
                b, free = take(dve, l, "XV", t)
                V.tensor_copy(U[0:n, :, :].rearrange("p a b -> p (a b)"), b[0:n, 0:384]).then_inc(XV_ok.sem, 1)
                wait(dve, XV_ok, l, t)
                V.engine_nop().then_inc(free, 1)

            def retention(l):
                for k in range(2):
                    b, free = take(dve, l, "rot", k)
                    own(tt(aT[:, k, :], rtz[:, k, :], cst("cos", 0, NT), MUL))
                    tt(gate[:, k, :], b[:, 0:NT], cst("cos", NT, NT), MUL).then_inc(free, 1)
                    dve.wait_ge(free, fills[(l, "rot", k)][1] + 1)
                    settle()
                    own(tt(aT[:, k, :], aT[:, k, :], gate[:, k, :], ADD))
                settle()
                own(tt(aT[:, 2, :], aT[:, 1, :], cst("kdec"), MUL))
                own(tt(rt_qd, aT[:, 0, SEQ:], cst("qdec"), MUL))
                settle()
                V.engine_nop().then_inc(rot_ok.sem, 1)
                rp = R.rearrange("p a b c -> p (a b c)")
                for h in range(RT_H):
                    b, free = take(dve, l, "rtp", h)
                    own(tt(rp[:, h * 384:h * 384 + SEQ], b[:, 0:SEQ], cst("rt_mask", h * SEQ, SEQ), MUL))
                    tt(rp[:, h * 384 + SEQ:(h + 1) * 384], b[:, SEQ:384], cst("rt_mask", h * SEQ, P), MUL).then_inc(free, 1)
                    dve.wait_ge(free, fills[(l, "rtp", h)][1] + 1)
                    settle()
                    V.engine_nop().then_inc(rtR_ok.sem, 1)
                for h in range(RT_H):
                    b, free = take(dve, l, "rtp", 4 + h)
                    tt(keys.rearrange("p a b c -> p (a b c)")[0:32, 32 * h:32 * h + 32], b[0:32, 0:32],
                       cst("rt_mask_s", 32 * h, 32, rows=32), MUL).then_inc(free, 1)
                    dve.wait_ge(free, fills[(l, "rtp", 4 + h)][1] + 1)
                    V.engine_nop().then_inc(rtR_ok.sem, 1)
                wait(dve, rtk_ok, l, 2)
                for h in range(RT_H):
                    spread(UX[0:32, h, :, :], sg[0:32, 2, P + h * HD:P + (h + 1) * HD]).then_inc(rtX_ok.sem, 1)
                for p in range(2):
                    b, free = take(dve, l, "rto", p)
                    own(V.tensor_copy(OT[:, 6 + p, 0:SEQ], b[:, 0:SEQ]))
                    wait(dve, rtC_ok, l, p)
                    tt(OT[:, 6 + p, SEQ:], b[:, SEQ:NT], USO[:, p, 0, :], ADD).then_inc(free, 1)
                    dve.wait_ge(free, fills[(l, "rto", p)][1] + 1)
                    settle()
                    V.engine_nop().then_inc(rtO_ok.sem, 1)
                b, free = take(dve, l, "rtss")
                x = SSr[:, :, :].rearrange("p a b -> p (a b)")
                V.scalar_tensor_tensor(x, x, cst("g4"), b[:, :], MUL, ADD).then_inc(rtS_ok.sem, 1)
                wait(dve, rtS_ok, l, 0)
                V.engine_nop().then_inc(free, 1)

            def out_norms(l):
                wait(dve, O_ok, l, 7)
                wait(dve, rtO_ok, l, 1)
                tt(conv[:, 0:3, :], OT[:, 0:3, :], OT[:, 0:3, :], MUL).then_inc(osq_ok.sem, 1)
                for a, n in ((3, 3), (6, 2)):
                    for p in range(a, a + n):
                        b, free = take(dve, l, "mean", p)
                        tt(OT[:, p, :], OT[:, p, :], b[:, 0:NT], SUB).then_inc(free, 1)
                        dve.wait_ge(free, fills[(l, "mean", p)][1] + 1)
                    tt(conv[:, a:a + n, :], OT[:, a:a + n, :], OT[:, a:a + n, :], MUL).then_inc(osq_ok.sem, 1)
                weights = [par(l, "dn_norm")] * 3 + [par(l, "ln_g", f) for f in range(3)] + [par(l, "rt_ln", f) for f in range(2)]
                for p in range(8):
                    wait(dve, orn_ok, l, p)
                    own(V.scalar_tensor_tensor(OT[:, p, :], OT[:, p, :], weights[p], conv[:, p, :], MUL, MUL))
                settle()
                for f in range(3):
                    own(V.scalar_tensor_tensor(OT[:, 3 + f, :], OT[:, 3 + f, :], par(l, "ln_b", f), bonus[:, f, :], ADD, ADD))
                own(tt(OT[:, 0:3, :], OT[:, 0:3, :], zg[:, :, :], MUL))
                own(tt(OT[:, 6:8, :], OT[:, 6:8, :], rtz[:, 4:6, :], MUL))
                wait(dve, gT_ok, l, 0)
                settle()
                tt(OT[:, 3:6, :], OT[:, 3:6, :], zs[:, 9:12, :], MUL).then_inc(cat_ok.sem, 1)

            def residual(l):
                for c, (c0, c1) in enumerate(WOUT_LOADS):
                    for t, (t0, n) in enumerate(TILES):
                        b, free = take(dve, l, "out", t, c)
                        x = X[0:n, t, c0:c1]
                        tt(x, x, b[0:n, 0:c1 - c0], ADD).then_inc(free, 1)
                        dve.wait_ge(free, fills[(l, "out", t, c)][1] + 1)
                    V.engine_nop().then_inc(out_ok.sem, 1)

            def routing(l):
                b, free = take(dve, l, "logits")
                own(V.tensor_copy(small[:, 0, 0:2, :], b[:, 0:16].rearrange("p (a b) -> p a b", a=2)))
                V.tensor_copy(small[0:32, 0, 2, :], b[0:32, 16:24]).then_inc(free, 1)
                dve.wait_ge(free, fills[(l, "logits")][1] + 1)
                settle()
                rank = over(cst("rank"), 3)
                top = lambda k: over(stat[:, :, k], N_EXP, 2)

                def pick(src, scored, hot, k):
                    own(V.tensor_reduce(stat[:, :, k], small[:, src, :, :], AX.X, ALU.max))
                    settle()
                    own(tt(small[:, scored, :, :], small[:, src, :, :], top(k), ALU.is_equal))
                    settle()
                    own(tt(small[:, scored, :, :], small[:, scored, :, :], rank, MUL))
                    settle()
                    own(V.tensor_reduce(stat[:, :, k + 1], small[:, scored, :, :], AX.X, ALU.max))
                    settle()
                    own(tt(small[:, hot, :, :], small[:, scored, :, :], top(k + 1), ALU.is_equal))
                    settle()

                pick(0, 1, 2, 3)
                own(V.scalar_tensor_tensor(small[:, 3, :, :], small[:, 2, :, :], -3e38, small[:, 0, :, :], MUL, ADD))
                settle()
                pick(3, 4, 5, 5)
                tt(small[:, 1, :, :], small[:, 2, :, :], small[:, 5, :, :], ADD).then_inc(chosen_ok.sem, 1)
                own(tt(stat[:, :, 7], stat[:, :, 5], stat[:, :, 3], SUB))
                settle()
                V.engine_nop().then_inc(diff_ok.sem, 1)
                wait(dve, odds_ok, 0, 0)
                own(V.tensor_scalar(stat[:, :, 3], stat[:, :, 8], 1.0, None, ADD))
                settle()
                own(V.reciprocal(stat[:, :, 5], stat[:, :, 3]))
                settle()
                own(tt(stat[:, :, 6], stat[:, :, 5], stat[:, :, 8], MUL))
                own(tt(small[:, 2, :, :], small[:, 2, :, :], top(5), MUL))
                settle()
                own(tt(small[:, 5, :, :], small[:, 5, :, :], top(6), MUL))
                settle()
                own(tt(route[:, 1, :, 0:N_EXP], small[:, 2, :, :], small[:, 5, :, :], ADD))
                b, free = take(dve, l, "slots")
                own(V.tensor_copy(small[:, 0, 0:2, :], b[:, 0:2 * N_EXP].rearrange("p (a b) -> p a b", a=2)))
                own(V.tensor_copy(small[0:32, 0, 2, :], b[0:32, 2 * N_EXP:3 * N_EXP]))
                V.tensor_reduce(stat[:, 0, 3:4], b[:, 3 * N_EXP:4 * N_EXP], AX.X, ALU.max).then_inc(free, 1)
                dve.wait_ge(free, fills[(l, "slots")][1] + 1)
                settle()
                own(V.scalar_tensor_tensor(small[:, 3, :, :], small[:, 0, :, :], 1.0, small[:, 1, :, :], ADD, MUL))
                own(V.tensor_scalar(stat[0:1, 0, 4:5], stat[0:1, 0, 3:4], CAP + 0.5, None, ALU.is_gt))
                settle()
                own(V.tensor_scalar(route[:, 0, :, 0:N_EXP], small[:, 3, :, :], -1.0, None, ADD))
                V.tensor_copy(more[0:1, 0:1], stat[0:1, 0, 4:5]).then_inc(more_ok, 1)
                dve.wait_ge(more_ok, 1)
                settle()
                dve.wait_ge(route_in, 16)
                V.engine_nop().then_inc(x_added, 1)

            def hidden(s, tile, n):
                dve.wait_ge(silu_done, tile + 1)
                dve.wait_ge(h3_full, tile + 1)
                if not isinstance(tile, int) or tile >= SLOTS:
                    dve.wait_ge(hid_used, tile + 1 - SLOTS)
                tt(hid[s][:, 0:n], silu_h[:, 0:n], banks[7][:, 0:n], MUL).then_inc(hid_ok, 1)

            def dense(l):
                turns, rest = divmod(FFN_BLOCKS, SLOTS)
                for s in range(SLOTS):
                    hidden(s, s, NT)
                with dve.Fori(1, turns) as i:
                    for s in range(SLOTS):
                        hidden(s, i * SLOTS + s, NT)
                for s in range(rest):
                    hidden(s, turns * SLOTS + s, NT)
                dve.wait_ge(hid_used, FFN_BLOCKS)
                for t, (t0, m) in enumerate(TILES):
                    for c in range(2):
                        x = X[0:m, t, c * 512:(c + 1) * 512]
                        own(tt(x, x, banks[2 * t + c][0:m, :], ADD))
                settle()

            def build(r, e):
                for t, (t0, n) in enumerate(TILES):
                    pos, weight = (column(n, k, t, e) for k in range(2))
                    V.tensor_scalar(hot[0:n, t, :], iota[0:n, :], pos, None, ALU.is_equal).then_inc(hot_ok, 1)
                    V.tensor_scalar(hot_w[0:n, t, :], iota[0:n, :], pos, weight, ALU.is_equal, MUL).then_inc(hot_ok, 1)

            def column(n, k, t, e):
                if isinstance(e, int):
                    return route[0:n, k, t, e:e + 1]
                return route[0:n, k, t, bass.ds(e, 1)]

            def start_round(r):
                if not isinstance(r, int):
                    dve.wait_ge(hot_t_full, N_EXP * r)
                    V.tensor_scalar(route[:, 0, :, :], route[:, 0, :, :], -float(CAP), None, ADD).then_inc(lowered, 1)
                    dve.wait_ge(lowered, r)
                build(r, 0)

            def expert(r, e):
                job = r * N_EXP + e
                for part in range(2):
                    dve.wait_ge(gathered, 2 * job + part + 1)
                    w = par(1, "ln_ffn", 4 * part, 4)
                    tt(hG[:, 4 * part:4 * part + 4, :], banks[2 + part][:, :].rearrange("p (a b) -> p a b", a=4),
                       over(w, CAP, 2), MUL).then_inc(hG_ok, 1)
                with dve.Fori(0, EXP_TURNS) as i:
                    for s in range(SLOTS):
                        hidden(s, FFN_BLOCKS + (job * EXP_TURNS + i) * SLOTS + s, CAP)
                dve.wait_ge(hot_t_full, job + 1)
                build(r, e + 1)
                dve.wait_ge(hid_used, FFN_BLOCKS + EXP_BLOCKS * (job + 1))
                V.tensor_copy(y_exp[:, 512:], banks[1][:, :]).then_inc(y_in, 1)
                for t, (t0, n) in enumerate(TILES):
                    for c in range(2):
                        dve.wait_ge(spread_full, 6 * job + 2 * t + c + 1)
                        x = X[0:n, t, c * 512:(c + 1) * 512]
                        tt(x, x, banks[SPREAD[2 * t + c]][0:n, :], ADD).then_inc(x_added, 1)
                dve.wait_ge(x_added, 6 * (job + 1) + 1)

            for k, e in enumerate(EPS):
                V.memset(eps(k), e).then_inc(eps_ok, 1)
            own(V.memset(ab[:, :, :], 0.0))
            own(V.memset(dn[:, :, :, :], 0.0))
            own(V.memset(small[:, :, :, :], 0.0))
            own(V.memset(route[:, :, :, :], -1.0))
            own(V.memset(zeros[:, :], 0.0))
            own(V.memset(stat[:, :, :], 0.0))
            settle()
            dve.wait_ge(inputs, 16 * N_IN)
            for l in range(DEPTH):
                own(V.memset(zc[:, :, 0:PADC], 0.0))
                own(V.memset(zr[:, :, 0:1], 0.0))
                own(V.memset(zr[:, 11, 1:], 0.0))
                settle()
                V.engine_nop().then_inc(zeroed.sem, 1)
                norm(l, 0)
                wait(dve, pads_ok, l, 0)
                convolve(l)
                gates(l)
                shift(l)
                dn_prepare(l)
                for y in range(2):
                    if y:
                        rw_prepare(l)
                    for t in range(3):
                        (rw_tile if y else dn_tile)(l, t)
                        inverses(l, y, t)
                        if y:
                            copy_av(l, t)
                        if t < 2:
                            prompt_chunk(l, y, 2 * t)
                            prompt_chunk(l, y, 2 * t + 1)
                        else:
                            sample_chunks(l, y)
                retention(l)
                out_norms(l)
                residual(l)
                norm(l, 1)
                if l == 0:
                    dense(l)
                else:
                    routing(l)
                    expert_rounds(dve, expert, start_round)
            dve.wait_ge(lnf_in, 16)
            for t, (t0, n) in enumerate(TILES):
                own(V.tensor_tensor_reduce(junk[0:n], X[0:n, t, :], X[0:n, t, :], 1.0, 0.0, MUL, ADD, stat[0:n, t, 0:1]))
                settle()
                V.engine_nop().then_inc(fss_ok.sem, 1)
            for t, (t0, n) in enumerate(TILES):
                wait(dve, frs_ok, 0, t)
                V.scalar_tensor_tensor(X[0:n, t, :], X[0:n, t, :], stat[0:n, t, 2:3], lnf[0:n, :], MUL, MUL)\
                    .then_inc(final_ok.sem, 1)

        @block.scalar
        def _(act):
            A = nc.scalar.activation
            steps = [0]

            def own(ins):
                steps[0] += 1
                ins.then_inc(act_seq, 1)

            def settle():
                act.wait_ge(act_seq, steps[0])

            def copy(out, in_):
                return A(out, in_, ACT.Copy)

            def rstd(l, use):
                for t, (t0, n) in enumerate(TILES):
                    if l is None:
                        wait(act, fss_ok, 0, t)
                    else:
                        wait(act, ssq_ok, l, use * 3 + t)
                    own(A(stat[0:n, t, 1:2], stat[0:n, t, 0:1], ACT.Ln, bias=eps(0)[0:n], scale=1.0 / D))
                    settle()
                    A(stat[0:n, t, 2:3], stat[0:n, t, 1:2], ACT.Exp, scale=-0.5).then_inc((frs_ok if l is None else rstd_ok).sem, 1)

            def project(l):
                for m, (kind, k, _, n) in enumerate(ZTILES):
                    if m == 12:
                        wait(act, zeroed, l, 0)
                    b, free = take(act, l, "z", m)
                    sample = b[0:n, SEQ:NT].rearrange("p (b s) -> p b s", b=NB)
                    if kind == "conv":
                        own(copy(zc[:, k, PADC:PADC + SEQ], b[:, 0:SEQ]))
                        i = copy(zc[:, k, PADC + SEQ:].rearrange("p (b s) -> p b s", b=NB)[:, :, PADC:], sample)
                    elif kind == "rw":
                        own(copy(zr[0:n, k, 1:1 + SEQ], b[0:n, 0:SEQ]))
                        i = copy(zr[0:n, k, 1 + SEQ:].rearrange("p (b s) -> p b s", b=NB)[:, :, 1:], sample)
                    elif kind == "zg":
                        i = A(zg[:, k, :], b[:, 0:NT], ACT.Silu)
                    else:
                        i = A(rtz[:, k, :], b[:, 0:NT], ACT.Silu if k >= 4 else ACT.Copy)
                    i.then_inc(free, 1)
                    act.wait_ge(free, fills[(l, "z", m)][1] + 1)
                    settle()
                    nc.scalar.nop().then_inc(z_ok.sem, 1)
                    if m in (11, 14, 17):
                        g = (m - 11) // 3
                        wait(act, conv_ok, l, g)
                        own(A(conv[:, 3 * g:3 * g + 3, 0:SEQ], tmp3[:, :, 0:SEQ], ACT.Silu))
                        for x in range(3):
                            own(A(conv[:, 3 * g + x, SEQ:].rearrange("p (b s) -> p b s", b=NB),
                                  tmp3[:, x, PADC + SEQ:].rearrange("p (b s) -> p b s", b=NB)[:, :, 0:DS], ACT.Silu))
                        settle()
                        nc.scalar.nop().then_inc(qkv_ok.sem, 1)

            def lora(l):
                wait(act, ab_ok, l, 0)
                A(dn[:, 1, :, :], ab[:, :, H:], ACT.Sigmoid).then_inc(beta_ok.sem, 1)
                wait(act, zs_ok, l, 0)
                own(A(zs[0:64, 9, :], zs[0:64, 9, :], ACT.Tanh))
                own(A(zs[:, 10, :], zs[:, 10, :], ACT.Sigmoid))
                own(A(zs[0:32, 11, :], zs[0:32, 11, :], ACT.Sigmoid))
                settle()
                nc.scalar.nop().then_inc(lora_ok.sem, 1)
                for t, (t0, n) in enumerate(TILES):
                    b, free = take(act, l, "y", t)
                    A(sg[0:n, t, :], b[0:n, 0:384], ACT.Sigmoid).then_inc(free, 1)
                    act.wait_ge(free, fills[(l, "y", t)][1] + 1)
                    nc.scalar.nop().then_inc(sg_ok.sem, 1)
                for f in range(3):
                    b, free = take(act, l, "a", f)
                    A(aT[:, f, :], b[:, 0:NT], ACT.Sigmoid, bias=par(l, "a0", f)).then_inc(free, 1)
                    act.wait_ge(free, fills[(l, "a", f)][1] + 1)
                    nc.scalar.nop().then_inc(aT_ok.sem, 1)
                take(act, l, "g", 2)
                for f in range(3):
                    b, free = take(act, l, "g", f)
                    copy(zs[:, 9 + f, :], b[:, 0:NT]).then_inc(free, 1)
                    act.wait_ge(free, fills[(l, "g", f)][1] + 1)
                nc.scalar.nop().then_inc(gT_ok.sem, 1)

            def inverse_root(l, key, out, eps_k, done, factor=None):
                b, free = take(act, l, *key)
                A(out, b[:, 0:NT], ACT.Ln, bias=eps(eps_k)).then_inc(free, 1)
                act.wait_ge(free, fills[(l, *key)][1] + 1)
                A(out, out, ACT.Exp, scale=-0.5, bias=factor if factor is not None else 0.0).then_inc(done.sem, 1)

            def dn_prepare(l):
                A(dn[:, 11, 0, :], par(l, "a_log", 0, H), ACT.Exp).then_inc(negA_ok.sem, 1)
                wait(act, dtb_ok, l, 0)
                own(A(dn[:, 3, :, :], dn[:, 2, :, :], ACT.Abs))
                settle()
                own(A(dn[:, 3, :, :], dn[:, 3, :, :], ACT.Exp, scale=-1.0))
                settle()
                A(dn[:, 3, :, :], dn[:, 3, :, :], ACT.Ln, bias=1.0).then_inc(sp_ok.sem, 1)
                for i in range(6):
                    inverse_root(l, ("dnss", i), SQ[:, i, :], 1, rn_ok, eps(4) if i < 3 else None)
                wait(act, cum_ok, l, 0)
                A(dn[:, 7:9, :, :], dn[:, 5:7, :, :], ACT.Exp).then_inc(egn_ok.sem, 1)
                for p in range(3):
                    b, free = take(act, l, "bc_g", p)
                    A(eg[:, p, :], b[:, 0:NT], ACT.Exp).then_inc(free, 1)
                    act.wait_ge(free, fills[(l, "bc_g", p)][1] + 1)
                    nc.scalar.nop().then_inc(eg_ok.sem, 1)

            def dn_tile(l, t):
                n = TILES[t][1]
                for g in range(2):
                    b, free = take(act, l, "E", t, g)
                    for x in range(3):
                        h = 3 * g + x
                        i = A(DI[0:n, g, x, 0:n], b[0:n, x * n:(x + 1) * n], ACT.Exp, bias=dn[0:n, 10, t, h:h + 1])
                        if x < 2:
                            own(i)
                    i.then_inc(free, 1)
                    act.wait_ge(free, fills[(l, "E", t, g)][1] + 1)
                    settle()
                    nc.scalar.nop().then_inc(DI_ok.sem, 1)

            def rw_tile(l, t):
                n = TILES[t][1]
                if t:
                    wait(act, keys_ok, l, t - 1)
                for f in range(3):
                    b, free = take(act, l, "cumw", t, f)
                    own(A(E3[:, f, :, 0:n], b[:, 0:3 * n].rearrange("p (a b) -> p a b", a=3), ACT.Exp, scale=-RW_DECAY))
                    A(EI[:, f, 0:n], b[:, 0:n], ACT.Exp, scale=RW_DECAY).then_inc(free, 1)
                    act.wait_ge(free, fills[(l, "cumw", t, f)][1] + 1)
                settle()
                nc.scalar.nop().then_inc(E_ok.sem, 1)
                for k in range(4):
                    b, free = take(act, l, "rwnat", t, k)
                    copy(nat[0:n, k, :, :].rearrange("p a b -> p (a b)"), b[0:n, 0:384]).then_inc(free, 1)
                    act.wait_ge(free, fills[(l, "rwnat", t, k)][1] + 1)
                nc.scalar.nop().then_inc(natb_ok.sem, 1)

            def chunk_inputs(l, y, t):
                t0, n = TILES[t]
                b, free = take(act, l, y, "W", t)
                copy(Q[:, :, 3, t0:t0 + n], b[:, 0:3 * n].rearrange("p (a b) -> p a b", a=3)).then_inc(W_ok.sem, 1)
                wait(act, W_ok, l, y * 3 + t)
                nc.scalar.nop().then_inc(free, 1)
                b, free = take(act, l, y, "U0", t)
                A(U0[0:n, :, :].rearrange("p a b -> p (a b)"), b[0:n, 0:384], ACT.Copy, scale=-1.0 if y else 1.0)\
                    .then_inc(U0_ok.sem, 1)
                wait(act, U0_ok, l, y * 3 + t)
                nc.scalar.nop().then_inc(free, 1)

            def prompt_chunk(l, y, c):
                b, free = take(act, l, y, "O", c)
                copy(OT[:, 3 * y:3 * y + 3, CHUNK * c:CHUNK * (c + 1)], b[:, 0:3 * CHUNK].rearrange("p (a b) -> p a b", a=3))\
                    .then_inc(O_ok.sem, 1)
                wait(act, O_ok, l, y * 4 + c)
                nc.scalar.nop().then_inc(free, 1)

            def sample_chunks(l, y):
                b, free = take(act, l, y, "SU")
                copy(USO[:, :, :, :].rearrange("p a b c -> p (a b c)"), b[:, 0:192]).then_inc(USO_ok.sem, 1)
                wait(act, USO_ok, l, y)
                nc.scalar.nop().then_inc(free, 1)

            def rw_prepare(l):
                for f in range(3):
                    inverse_root(l, ("kss", f), SQ[:, f, :], 1, kk_rn)

            def retention(l):
                for t, (t0, n) in enumerate(TILES):
                    b, free = take(act, l, "rtn", t)
                    copy(sg[0:n, t, :], b[0:n, 0:384]).then_inc(free, 1)
                    act.wait_ge(free, fills[(l, "rtn", t)][1] + 1)
                    nc.scalar.nop().then_inc(rtk_ok.sem, 1)
                for p in range(2):
                    b, free = take(act, l, "rtc", p)
                    copy(USO[:, p, 0, :], b[:, 0:32]).then_inc(free, 1)
                    act.wait_ge(free, fills[(l, "rtc", p)][1] + 1)
                    nc.scalar.nop().then_inc(rtC_ok.sem, 1)
                b, free = take(act, l, "rts")
                copy(Sr[:, l, :], b[:, 0:HD]).then_inc(rtSp_ok.sem, 1)
                wait(act, rtSp_ok, l, 0)
                nc.scalar.nop().then_inc(free, 1)

            def out_norms(l):
                for p in range(8):
                    inverse_root(l, ("var", p), conv[:, p, :], 0 if p < 3 else 2 if p < 6 else 3, orn_ok)

            def routing(l):
                wait(act, diff_ok, 0, 0)
                A(stat[:, :, 8], stat[:, :, 7], ACT.Exp).then_inc(odds_ok.sem, 1)

            def silu(tile, n):
                act.wait_ge(h1_full, tile + 1)
                if not isinstance(tile, int) or tile:
                    act.wait_ge(hid_ok, tile)
                A(silu_h[:, 0:n], banks[6][:, 0:n], ACT.Silu).then_inc(silu_done, 1)

            def dense(l):
                turns, rest = divmod(FFN_BLOCKS, SLOTS)
                for s in range(SLOTS):
                    silu(s, NT)
                with act.Fori(1, turns) as i:
                    for s in range(SLOTS):
                        silu(i * SLOTS + s, NT)
                for s in range(rest):
                    silu(turns * SLOTS + s, NT)

            def expert(r, e):
                job = r * N_EXP + e
                act.wait_ge(hot_t_full, job + 1)
                copy(TM[:, 0, :, :].rearrange("p a b -> p (a b)")[:, 0:NT], banks[4][:, 0:NT]).then_inc(hot_t_ok, 1)
                with act.Fori(0, EXP_TURNS) as i:
                    for s in range(SLOTS):
                        silu(FFN_BLOCKS + (job * EXP_TURNS + i) * SLOTS + s, CAP)
                act.wait_ge(hid_used, FFN_BLOCKS + EXP_BLOCKS * (job + 1))
                copy(y_exp[:, 0:512], banks[0][:, :]).then_inc(y_in, 1)

            act.wait_ge(inputs, 16 * N_IN)
            act.wait_ge(eps_ok, len(EPS))
            for l in range(DEPTH):
                rstd(l, 0)
                for k in range(2):
                    wait(act, seq_states, l, k)
                own(copy(seqs(zc[:, :, PADC + SEQ:])[:, :, :, 0:PADC], seqs(cvs[:, :, :])))
                wait(act, zeroed, l, 0)
                own(copy(zr[:, :, 1 + SEQ:].rearrange("p m (b s) -> p m b s", s=DS + 1)[:, :, :, 0], shs[:, :, :]))
                settle()
                nc.scalar.nop().then_inc(pads_ok.sem, 1)
                project(l)
                lora(l)
                dn_prepare(l)
                for y in range(2):
                    if y:
                        rw_prepare(l)
                    for t in range(3):
                        (rw_tile if y else dn_tile)(l, t)
                        chunk_inputs(l, y, t)
                        if t < 2:
                            prompt_chunk(l, y, 2 * t)
                            prompt_chunk(l, y, 2 * t + 1)
                        else:
                            sample_chunks(l, y)
                retention(l)
                out_norms(l)
                rstd(l, 1)
                if l == 0:
                    dense(l)
                else:
                    routing(l)
                    expert_rounds(act, expert)
            rstd(None, 0)

        @block.sync
        def _(sp):
            def load(s, src, turn, used):
                sp.wait_ge(hid_used, used)
                sp.dma_start(slot[s], src[bass.ds(turn * SLOTS + s, 1)].rearrange("a p c -> p (a c)")).then_inc(block_loaded[s], 16)

            for l in range(DEPTH):
                if l:
                    sp.wait_ge(hid_used, FFN_BLOCKS)
                for i in range(MIX_LOADS):
                    s = i % 2
                    if i >= 2:
                        if i - 2 < len(WIN_LOADS):
                            wait(sp, z_ok, l, [m for m, z in enumerate(ZTILES) if z[2] < WIN_LOADS[i - 2][1]][-1])
                        else:
                            wait(sp, out_ok, l, i - 2 - len(WIN_LOADS))
                    if i < len(WIN_LOADS):
                        c0, c1 = WIN_LOADS[i]
                        dst = wslot[s][:, 0:KD * (c1 - c0)].rearrange("p (k c) -> p k c", k=KD)
                        src = w_in[l].rearrange("(k p) c -> p k c", p=P)[:, :, c0:c1]
                    else:
                        c0, c1 = WOUT_LOADS[i - len(WIN_LOADS)]
                        dst = wslot[s][:, 0:KD * (c1 - c0)].rearrange("p (k c) -> p k c", k=KD)
                        src = w_out[l].rearrange("(k p) c -> p k c", p=P)[:, :, c0:c1]
                    sp.dma_start(dst, src).then_inc(loaded[s].sem, 16)
                wait(sp, out_ok, l, len(WOUT_LOADS) - 1)
                src, done = (moe, FFN_BLOCKS) if l else (ffn, 0)
                turns, rest = (ROUND_TURNS, 0) if l else divmod(FFN_BLOCKS, SLOTS)
                if l:
                    sp.dma_start(ring[:, tail + 2 * D:tail + 2 * D + ROUTE_N], route_consts).then_inc(route_in, 16)
                for s in range(SLOTS):
                    sp.dma_start(slot[s], src[s]).then_inc(block_loaded[s], 16)
                with sp.Fori(1, turns) as i:
                    for s in range(SLOTS):
                        load(s, src, i, done + SLOTS * (i - 1) + s + 1)
                for s in range(rest):
                    sp.wait_ge(hid_used, done + SLOTS * (turns - 1) + s + 1)
                    sp.dma_start(slot[s], src[turns * SLOTS + s]).then_inc(block_loaded[s], 16)
            sp.dma_start(lnf, ln_final).then_inc(lnf_in, 16)
            sp.wait_ge(more_ok, 1)
            overflow = sp.value_load(more[0:1, 0:1], min_val=0, max_val=1)
            with sp.If(overflow > 0):
                with sp.Fori(1, -(-NT // CAP)) as r:
                    with sp.Fori(0, ROUND_TURNS) as i:
                        for s in range(SLOTS):
                            load(s, moe, i, FFN_BLOCKS + SLOTS * (r * ROUND_TURNS + i - 1) + s + 1)
            for t, (t0, n) in enumerate(TILES):
                wait(sp, final_ok, 0, t)
                sp.dma_start(y_out[t0:t0 + n, :], X[0:n, t, :]).then_inc(y_stored, 16)
            sp.wait_ge(y_stored, 48)

        @block.gpsimd
        def _(pool):
            pool.dma_start(C[:, :], consts).then_inc(inputs, 16)
            pool.dma_start(X[:, 0:2, :], x_in[0:SEQ, :].rearrange("(t p) d -> p t d", p=P)).then_inc(inputs, 16)
            pool.dma_start(X[0:32, 2, :], x_in[SEQ:NT, :]).then_inc(inputs, 16)
            pool.dma_start(PC[:, :, :], pcol.rearrange("l p c -> p l c")).then_inc(inputs, 16)
            pool.dma_start(rt_w[:, :, :], router.rearrange("(k p) e -> p k e", p=P)).then_inc(inputs, 16)
            for l in range(DEPTH):
                if l:
                    wait(pool, gT_ok, l - 1, 0)
                    wait(pool, SS_ok, l - 1, 1)
                pool.dma_start(cvs[:, :, :], conv_state[l]).then_inc(seq_states.sem, 16)
                pool.dma_start(shs[:, :, :], shift_state[l]).then_inc(seq_states.sem, 16)
                pool.dma_start(w2a2[:, :], rw_w2a2[l]).then_inc(lora_loaded.sem, 16)
                pool.dma_start(g2[:, :, :], rw_g2[l]).then_inc(lora_loaded.sem, 16)
                pool.dma_start(w0[:, :], rw_w0[l:l + 1, :]).then_inc(lora_loaded.sem, 16)
                if l:
                    wait(pool, rt_state_out, l - 1, 0)
                pool.dma_start(SSr[:, :, :], rt_state[l]).then_inc(rt_state_in.sem, 16)
                if l:
                    wait(pool, ss_out, l - 1, 1)
                pool.dma_start(SS[:, :, :, :], dn_state[l]).then_inc(ss_in.sem, 16)
                wait(pool, cvo_ok, l, 0)
                pool.dma_start(conv_out[l], cvo[:, 0, :, :]).then_inc(stored.sem, 16)
                wait(pool, sho_ok, l, 0)
                pool.dma_start(shift_out[l], sho[:, 0, :, :]).then_inc(stored.sem, 16)
                for y, (pp, ssx) in enumerate(((p_dn, s_dn), (p_rw, s_rw))):
                    wait(pool, S_ok, l, 4 * y + 3)
                    pool.dma_start(pp[l], S[:, y, :, :]).then_inc(stored.sem, 16)
                    wait(pool, SS_ok, l, y)
                    pool.dma_start(ssx[l], SS[:, :, :, :]).then_inc(ss_out.sem, 16)
                    if y == 0:
                        wait(pool, ss_out, l, 0)
                        pool.dma_start(SS[:, :, :, :], rw_state[l]).then_inc(ss_in.sem, 16)
                wait(pool, rtSp_ok, l, 0)
                pool.dma_start(p_rt[l], Sr[:, l, :]).then_inc(stored.sem, 16)
                wait(pool, rtS_ok, l, 0)
                pool.dma_start(s_rt[l], SSr[:, :, :]).then_inc(rt_state_out.sem, 16)
            wait(pool, stored, DEPTH - 1, 4)
            wait(pool, ss_out, DEPTH - 1, 1)
            wait(pool, rt_state_out, DEPTH - 1, 0)


def rows_to(a, rows=P):
    return np.swapaxes(a.reshape(a.shape[:-1] + (-1, rows)), -1, -2)


def kernel(**inp):
    import concourse.bacc as _bacc
    from concourse.bass_utils import run_bass_kernel_spmd as _run

    a = {k: np.asarray(v) for k, v in inp.items()}
    L = DEPTH
    f32 = np.float32

    def padded(x, n):
        out = np.zeros(x.shape[:-1] + (n,), x.dtype)
        out[..., :x.shape[-1]] = x
        return out

    cols = {
        "ln_mix": rows_to(a["ln_mix"]), "ln_ffn": rows_to(a["ln_ffn"]),
        "conv": np.ascontiguousarray(a["dn_conv"].reshape(L, CONV_W, 9, P).transpose(0, 3, 2, 1)).reshape(L, P, 36),
        "dn_norm": np.concatenate([a["dn_norm"]] * 2, 1)[:, :, None],
        "mu": rows_to(padded(a["rw_mu"], 12 * P)), "a0": rows_to(a["rw_a0"]), "kk": rows_to(a["rw_kk"]),
        "ka": rows_to(a["rw_ka"]), "rk": rows_to(a["rw_rk"].reshape(L, -1)), "ln_g": rows_to(a["rw_ln_g"]),
        "ln_b": rows_to(a["rw_ln_b"]), "rt_ln": rows_to(a["rt_ln"]),
        "a_log": np.repeat(a["dn_a_log"][:, None], P, 1), "dt": np.repeat(a["dn_dt_bias"][:, None], P, 1),
    }
    g2 = np.zeros((L, P, 2, 384), f32)
    g2[:, :, 0] = a["rw_g2"][:, :P]
    g2[:, :32, 1] = a["rw_g2"][:, P:]

    def blocks(w1, w3, w2):
        e, d, f = w1.shape
        up = lambda w: w.reshape(e, KD, P, f // FB, FB).transpose(0, 3, 2, 1, 4).reshape(e * f // FB, P, KD * FB)
        down = w2.reshape(e * f // FB, P, D)
        return np.concatenate([up(w1), up(w3), down], 2)

    shift = padded(a["state_rw_shift"], 12 * P).reshape(L, NB, 12, P).transpose(0, 3, 2, 1)
    arrays = {
        "x_in": np.concatenate([a["x_prompt"].reshape(SEQ, D), a["x_sample"].reshape(NB * DS, D)]),
        "consts": constants(),
        "route_consts": route_constants(),
        "pcol": np.concatenate([cols[k] for k, _ in PCOLS], 2),
        "rw_w2a2": np.concatenate([a["rw_w2"], a["rw_a2"]], 1),
        "rw_g2": g2, "rw_w0": a["rw_w0"], "ln_final": np.repeat(a["ln_final"][None], P, 0),
        "router": a["moe_router"][0], "w_in": a["w_in"], "w_out": a["w_out"],
        "ffn": blocks(a["ffn_w1"], a["ffn_w3"], a["ffn_w2"]),
        "moe": blocks(a["moe_w1"][0], a["moe_w3"][0], a["moe_w2"][0]),
        "conv_state": a["state_dn_conv"].reshape(L, NB, PADC, 9, P).transpose(0, 4, 3, 1, 2).reshape(L, P, 9, 24),
        "shift_state": shift,
        "dn_state": a["state_dn"].reshape(L, NB, 3, P, HD).transpose(0, 3, 2, 1, 4),
        "rw_state": a["state_rw"].transpose(0, 1, 2, 4, 3).reshape(L, NB, 3, P, HD).transpose(0, 3, 2, 1, 4),
        "rt_state": a["state_rt"].reshape(L, NB, P, HD).transpose(0, 2, 1, 3),
    }
    outs = {"y_out": (NT, D), "conv_out": (L, P, 9, 27), "shift_out": (L, P, 12, 9), "p_dn": (L, P, 3, HD),
            "p_rw": (L, P, 3, HD), "p_rt": (L, P, HD), "s_dn": (L, P, 3, NB, HD), "s_rw": (L, P, 3, NB, HD),
            "s_rt": (L, P, NB, HD)}
    nc = _bacc.Bacc("TRN2", target_bir_lowering=False, num_devices=1)
    args, given = {}, {}
    for name, x in arrays.items():
        given[name + "_dram"] = np.ascontiguousarray(x)
        args[name] = nc.dram_tensor(name + "_dram", x.shape, F32, kind="ExternalInput").ap()
    for name, shape in outs.items():
        args[name] = nc.dram_tensor(name + "_dram", shape, F32, kind="ExternalOutput").ap()
    trunk(nc, **args)
    r = _run(nc, [given], core_ids=[0]).results[0]
    o = {name: r[name + "_dram"] for name in outs}
    conv = o["conv_out"].reshape(L, P, 9, 9, PADC).transpose(3, 0, 4, 2, 1).reshape(9, L, PADC, 9 * P)
    sh = o["shift_out"].transpose(3, 0, 2, 1).reshape(9, L, 12 * P)[:, :, :1440]
    heads = lambda x: x.transpose(0, 2, 1, 3).reshape(L, H, HD, HD)
    sheads = lambda x: x.transpose(0, 3, 2, 1, 4).reshape(L, NB, H, HD, HD)
    res = (o["y_out"][:SEQ].reshape(1, SEQ, D), o["y_out"][SEQ:].reshape(NB, DS, D),
           conv[0][:, None], heads(o["p_dn"])[:, None], sh[0][:, None],
           heads(o["p_rw"]).swapaxes(-1, -2)[:, None], o["p_rt"].reshape(L, 1, RT_H, RT_K, HD),
           conv[1:].transpose(1, 0, 2, 3), sheads(o["s_dn"]), sh[1:].transpose(1, 0, 2),
           sheads(o["s_rw"]).swapaxes(-1, -2), o["s_rt"].transpose(0, 2, 1, 3).reshape(L, NB, RT_H, RT_K, HD))
    return tuple(np.ascontiguousarray(x) for x in res)
```

```python
import math
from contextlib import ExitStack

import numpy as np

import concourse.bass as bass
from concourse import mybir

F32 = mybir.dt.float32
ALU = mybir.AluOpType
ACT = mybir.ActivationFunctionType
AX = mybir.AxisListType
MUL, ADD, SUB = ALU.mult, ALU.add, ALU.subtract

P = 128
D = 1024
KD = D // P
SEQ, NB, DS = 256, 8, 4
NT = SEQ + NB * DS
DEPTH = 2
TILES = [(0, 128), (128, 128), (256, 32)]
CHUNK = 64
H = 6
HD = 64
CONV_W = 4
RT_H, RT_K = 4, 32
D_FF, N_EXP, D_EXP = 2816, 8, 3584
FB = P
FFN_BLOCKS = D_FF // FB
EXP_BLOCKS = D_EXP // FB
MOE_BLOCKS = N_EXP * EXP_BLOCKS
SLOT = 3 * KD * FB
SLOTS = 7
RING = 8 * SLOT
CAP = P
PADC = CONV_W - 1
ZC = PADC + SEQ + NB * (PADC + DS)
ZR = 1 + SEQ + NB * (1 + DS)
RW_DECAY = math.exp(-0.5)
NORM_EPS, RW_GN_EPS, RT_GN_EPS, L2_EPS = 1e-6, 64e-5, 1e-5, 1e-6
PAST_LEN = 2048
NEG = -1e30

DN0, RW0, RT0 = 0, 1548, 2988
ZTILES = [("conv", m, DN0 + P * m, P) for m in range(9)] + [("zg", m, 1152 + P * m, P) for m in range(3)]
ZTILES += [("rw", m, RW0 + P * m, P) for m in range(11)] + [("rw", 11, RW0 + 11 * P, 32)]
ZTILES += [("rt", m, RT0 + P * m, P) for m in range(6)]
WSLOT = KD * 384
WIN_LOADS = [(0, 384), (384, 768), (768, 1152), (1152, 1536), (1536, 1804), (1804, 2188), (2188, 2572), (2572, 2956),
             (2956, 3244), (3244, 3628), (3628, 3756)]
WOUT_LOADS = [(0, 384), (384, 768), (768, 1024)]
AB_LOAD = 4
MIX_LOADS = len(WIN_LOADS) + len(WOUT_LOADS)

PCOLS = [("ln_mix", 8), ("ln_ffn", 8), ("conv", 36), ("dn_norm", 1), ("mu", 12), ("a0", 3), ("kk", 3),
         ("ka", 3), ("rk", 3), ("ln_g", 3), ("ln_b", 3), ("rt_ln", 2), ("a_log", 6), ("dt", 6)]
CCOLS = [("ident", 128), ("tri", 384), ("tri_s", 96), ("neg", 128), ("neg_s", 32), ("level", 6 * 128),
         ("level0_t", 128), ("ones64", 128), ("mean64", 128), ("bmask", 8), ("rot", 128), ("cos", 2 * NT), ("qdec", 32), ("kdec", NT),
         ("g4", 1), ("rt_mask", 4 * SEQ), ("rt_mask_s", 128), ("rank", 8), ("ones", 128)]
ROUTE_N = 2 * P


def columns(cols):
    at, out = 0, {}
    for name, n in cols:
        out[name] = (at, n)
        at += n
    return out, at


PAT, PN = columns(PCOLS)
CAT, CN = columns(CCOLS)


def constants():
    c = np.zeros((P, CN), np.float64)

    def put(name, a, rows=P):
        at, n = CAT[name]
        c[:rows, at:at + n] = np.asarray(a).reshape(rows, n)

    i = np.arange(P)
    put("ident", np.eye(P))
    for name, size, n in (("tri", CHUNK, P), ("tri_s", DS, 32)):
        j, k = i[:n, None], i[None, :n]
        same = j // size == k // size
        put(name, np.concatenate([same & (j <= k), same & (j < k), same & (j > k)], 1), n)
        put("neg" + name[3:], np.where(same & (j <= k), 0.0, NEG), n)
    levels = []
    for s in (1, 2, 4, 8, 16, 32):
        a, b = i[:, None], i[None, :]
        levels.append(-1.0 * ((a // (2 * s) == b // (2 * s)) & (a % (2 * s) >= s) & (b % (2 * s) < s)))
    put("level", np.concatenate(levels, 1))
    put("level0_t", levels[0].T)
    blocks = (i[:, None] // HD == i[None, :] // HD) * 1.0
    put("ones64", blocks)
    put("mean64", blocks / HD)
    put("bmask", i[:32, None] // DS == np.arange(NB)[None], 32)
    rot = np.zeros((P, P))
    half = RT_K // 2
    for x in range(P):
        if x % RT_K < half:
            rot[x + half, x] = -1.0
        else:
            rot[x - half, x] = 1.0
    put("rot", rot)
    inv = (np.float32(10000.0) ** (-np.arange(half, dtype=np.float32) / np.float32(half))).astype(np.float32)
    pos = np.concatenate([np.arange(SEQ), np.tile(PAST_LEN + np.arange(DS), NB)]).astype(np.float32)
    ang = (pos[None, :] * inv[i % half][:, None]).astype(np.float32).astype(np.float64)
    put("cos", np.concatenate([np.cos(ang), np.sin(ang)], 1))
    lg = np.log1p(-np.exp2(-5.0 - np.arange(RT_H)))
    lgp = lg[i // RT_K][:, None]
    tok = np.tile(np.arange(DS), NB)[None]
    put("qdec", np.exp((tok + 1) * lgp))
    put("kdec", RT_K ** -0.5 * np.exp(np.concatenate([SEQ - 1 - np.arange(SEQ)[None] + 0 * lgp, DS - 1 - tok + 0 * lgp], 1) * lgp))
    put("g4", np.exp(DS * lgp))
    m = []
    for h in range(RT_H):
        d = np.arange(SEQ)[None] - i[:, None]
        m.append(RT_K ** -0.5 * np.where(d >= 0, np.exp(np.maximum(d, 0) * lg[h]), 0.0))
    put("rt_mask", np.concatenate(m, 1))
    j, k = i[:32, None], i[None, :32]
    put("rt_mask_s", RT_K ** -0.5 * np.concatenate([np.where((j // DS == k // DS) & (j <= k), np.exp(np.maximum(k - j, 0) * lg[h]), 0.0)
                                     for h in range(RT_H)], 1), 32)
    put("rank", np.tile(N_EXP - np.arange(N_EXP), (P, 1)))
    put("ones", np.ones((P, P)))
    return c.astype(np.float32)


def route_constants():
    return np.concatenate([np.tile(np.arange(P), (P, 1)), np.triu(np.ones((P, P)), 1)], 1).astype(np.float32)


def trunk(nc, x_in, consts, route_consts, pcol, rw_w2a2, rw_g2, rw_w0, ln_final, router, w_in, w_out, ffn, moe,
          conv_state, shift_state, dn_state, rw_state, rt_state,
          y_out, conv_out, shift_out, p_dn, p_rw, p_rt, s_dn, s_rw, s_rt):
    with ExitStack() as ctx:
        def sb(name, *free, rows=P):
            return ctx.enter_context(nc.sbuf_tensor(name, [rows, *free], F32))

        class Signal:

            def __init__(self, name, per, step=1):
                self.sem, self.per, self.step = ctx.enter_context(nc.semaphore(name)), per, step

            def at(self, layer, unit):
                assert 0 <= unit < self.per, (self.sem, unit)
                return self.step * (layer * self.per + unit + 1)

        def wait(eng, signal, layer, unit):
            eng.wait_ge(signal.sem, signal.at(layer, unit))

        ring = sb("ring", RING)
        wslot = [ring[:, s * WSLOT:(s + 1) * WSLOT] for s in range(2)]
        slot = [ring[:, s * SLOT:(s + 1) * SLOT] for s in range(SLOTS)]
        mix_at = [2 * WSLOT]

        def in_ring(*free, at=None):
            n = int(np.prod(free))
            a = mix_at[0] if at is None else at
            if at is None:
                mix_at[0] += n
            assert a + n <= RING, (a, n)
            names = "abcd"[:len(free)]
            if len(free) == 1:
                return ring[:, a:a + n]
            return ring[:, a:a + n].rearrange(f"p ({' '.join(names)}) -> p {' '.join(names)}", **dict(zip(names, free)))

        zc_at = mix_at[0]
        zc = in_ring(9, ZC)
        zr = in_ring(12, ZR)
        Q = in_ring(3, 4, NT, at=zc_at)
        UX = in_ring(4, NB, HD, at=zc_at + 12 * NT)
        assert 12 * NT + 4 * NB * HD <= 9 * ZC + 11 * ZR
        rtz = in_ring(6, NT)
        tmp3 = in_ring(3, ZC)
        R = in_ring(H, 4, P)
        nat = in_ring(4, H, HD)
        R_other = in_ring(H, 4, P, at=0)
        nat_other = in_ring(4, H, HD, at=WSLOT)
        E3 = in_ring(3, 3, P)
        keys = in_ring(2, 3, P)

        X = sb("X", 3, D)
        hT = sb("hT", KD, NT)
        C = sb("C", CN)
        PC = sb("PC", DEPTH, PN)
        w2a2 = sb("w2a2", 384)
        g2 = sb("g2", 2, 384)
        w0 = sb("w0", 384, rows=1)
        rt_w = sb("rt_w", KD, N_EXP)
        conv = sb("conv", 9, NT)
        zg = sb("zg", 3, NT)
        zs = sb("zs", 12, NT)
        gate = sb("gate", 3, NT)
        aT = sb("aT", 3, NT)
        bonus = sb("bonus", 3, NT)
        TM = sb("TM", 2, 3, P)
        TT = sb("TT", 2, 3, P)
        XM = sb("XM", 2, 3, P)
        DI = XM
        EI = in_ring(3, P)
        ends = in_ring(2, 3, P)
        sg = in_ring(3, 384)
        U0 = sb("U0", H, HD)
        U = sb("U", H, HD)
        S = sb("S", 2, 3, HD)
        Sr = sb("Sr", DEPTH, HD)
        SS = sb("SS", 3, NB, HD)
        SSr = sb("SSr", NB, HD)
        USO = in_ring(3, 2, 32)
        early = U0[:, :, :].rearrange("p a b -> p (a b)")
        cvs = early[:, 0:216].rearrange("p (a b) -> p a b", a=9)
        shs = early[:, 216:312].rearrange("p (a b) -> p a b", a=12)
        cvo = sb("cvo", 1, 9, 27)
        sho = sb("sho", 1, 12, 9)
        ab = sb("ab", 3, 12)
        dn = sb("dn", 12, 3, H)
        gb8 = sb("gb8", 2, NT, rows=N_EXP)
        gb = gb8[0:H, :, :]
        decay = sb("decay", 3, 12)
        stat = sb("stat", 3, 12)
        EPS = [NORM_EPS, L2_EPS, RW_GN_EPS, RT_GN_EPS, -math.log(HD) / 2]
        eps_cols = sb("eps_cols", len(EPS))
        eps = lambda k: eps_cols[:, k:k + 1]
        small = sb("small", 6, 3, N_EXP)
        route = sb("route", 2, 3, N_EXP + 1)
        zeros = ctx.enter_context(nc.sbuf_tensor("zeros", [32, 512], mybir.dt.bfloat16))
        more = ctx.enter_context(nc.sbuf_tensor("more", [1, 1], mybir.dt.int32))
        hn = [conv[:, 0:4, :].rearrange("p a b -> p (a b)")[:, 0:D], conv[:, 4:8, :].rearrange("p a b -> p (a b)")[:, 0:D]]

        def hn_at(use, t):
            return hn_last if use and t == 2 else hn[t % 2]

        OT = hT
        SQ = R.rearrange("p a b c -> p (a b c)")[:, 0:6 * NT].rearrange("p (a b) -> p a b", b=NT)
        eg, KK = gate, gate
        hid = [zs[:, s, :] for s in range(SLOTS)]
        silu_h = zs[:, SLOTS, :]
        tail = SLOTS * SLOT
        lnf = ring[:, tail:tail + D]
        hn_last = ring[:, tail + D:tail + 2 * D]
        iota = ring[:, tail + 2 * D:tail + 2 * D + P]
        before = ring[:, tail + 2 * D + P:tail + 2 * D + 2 * P]
        spare = hT[:, :, :].rearrange("p a b -> p (a b)")
        hG = spare[:, 0:KD * CAP].rearrange("p (k s) -> p k s", k=KD)
        y_exp = spare[:, KD * CAP:KD * CAP + D]
        hot, hot_w = TT[:, 0, :, :], TT[:, 1, :, :]
        hot_t = TM[:, 0, :, :].rearrange("p a b -> p (a b)")[:, 0:NT]
        pair_sel = bonus[0:H, :, :].rearrange("p a b -> p (a b)")[:, 0:H * HD]
        junk = zs[:, 8:12, :].rearrange("p a b -> p (a b)")[:, 0:D]
        short_y = gate[:, :, :].rearrange("p a b -> p (a b)")[:, 0:KD * TILES[2][1]]
        rt_qd = EI[:, 0, 0:32]
        omka = stat[:, 0, 9:12]

        banks = [ctx.enter_context(nc.psum_tensor(f"bank{b}", [P, 512], F32)) for b in range(8)]

        def cst(name, a=0, n=None, rows=P):
            at, size = CAT[name]
            return C[0:rows, at + a:at + a + (size - a if n is None else n)]

        def par(layer, name, k=0, n=1):
            at = PAT[name][0] + k
            return PC[:, layer, at:at + n]

        def over(a, n, at=1):
            shape = list(a.shape)
            shape.insert(at, n)
            return a.unsqueeze(at).to_broadcast(shape)

        ident = cst("ident")
        tri = [cst("tri"), cst("tri"), cst("tri_s", rows=32)]
        neg = [cst("neg"), cst("neg"), cst("neg_s", rows=32)]
        LEVELS = [6, 6, 2]
        seqs = lambda a: a.rearrange("p m (b s) -> p m b s", b=NB)

        def sig(name, per, step=1):
            return Signal(name, per, step)

        loaded = [sig(f"wslot{s}_loaded", MIX_LOADS // 2, 16) for s in range(2)]
        out_ok = sig("out_columns_added", len(WOUT_LOADS))
        block_loaded = [ctx.enter_context(nc.semaphore(f"block_slot{s}_loaded")) for s in range(SLOTS)]
        bank_full = [ctx.enter_context(nc.semaphore(f"bank{b}_full")) for b in range(8)]
        bank_free = [ctx.enter_context(nc.semaphore(f"bank{b}_free")) for b in range(8)]
        x_loaded = ctx.enter_context(nc.semaphore("x_loaded"))
        first_inputs = ctx.enter_context(nc.semaphore("identity_and_parameters_loaded"))
        inputs = ctx.enter_context(nc.semaphore("inputs_loaded"))
        stored = sig("outputs_stored", 5, 16)
        lora_loaded = sig("lora_loaded", 3, 16)
        seq_states = sig("conv_shift_states_loaded", 2, 16)
        rt_state_in = sig("rt_state_loaded", 1, 16)
        rt_state_out = sig("rt_state_stored", 1, 16)
        ss_in = sig("sample_state_loaded", 2, 16)
        ss_out = sig("sample_state_stored", 2, 16)
        dve_seq = ctx.enter_context(nc.semaphore("vector_steps"))
        act_seq = ctx.enter_context(nc.semaphore("scalar_steps"))
        ssq_ok = sig("squares_summed", 6)
        root_ok = sig("root_ready", 6)
        rstd_ok = sig("rstd_ready", 6)
        hn_ok = sig("normed", 6)
        hT_ok = sig("hT_ready", 12)
        ab_ok = sig("ab_ready", 1)
        zeroed = sig("pads_zeroed", 1)
        z_ok = sig("z_ready", 30)
        pads_ok = sig("pads_ready", 1)
        conv_ok = sig("conv_summed", 3)
        qkv_ok = sig("qkv_ready", 3)
        cvo_ok = sig("conv_tail_ready", 1)
        sho_ok = sig("shift_tail_ready", 1)
        zs_ok = sig("shifted", 1)
        lora_ok = sig("lora_inputs_ready", 1)
        sg_ok = sig("decay_sigmoid_ready", 3)
        aT_ok = sig("a_ready", 3)
        gT_ok = sig("g_ready", 1)
        beta_ok = sig("beta_ready", 1)
        negA_ok = sig("neg_A_ready", 1)
        dtb_ok = sig("dt_biased", 1)
        sp_ok = sig("softplus_log_ready", 1)
        g_ok = sig("g_log_decay_ready", 1)
        cum_ok = sig("cum_ready", 1)
        gb_ok = sig("g_beta_rows_ready", 1)
        egn_ok = sig("cum_exp_ready", 1)
        sq_ok = sig("qk_squares", 1)
        rn_ok = sig("qk_rnorm", 6)
        eg_ok = sig("eg_ready", 3)
        Q_ok = sig("queries_ready", 1)
        nat_ok = sig("naturals_ready", 3)
        natb_ok = sig("naturals_copied", 3)
        DI_ok = sig("pair_decays", 6)
        R_ok = sig("products_ready", 36)
        T_ok = sig("inverse_ready", 2 * 2 * (6 + 6 + 2))
        XM_ok = sig("masked_ready", 2 * 2 * (6 + 6 + 2))
        XV_ok = sig("av_ready", 3)
        U0_ok = sig("u0_ready", 6)
        W_ok = sig("w_ready", 6)
        U_ok = sig("u_ready", 10)
        O_ok = sig("o_ready", 8)
        Os_ok = sig("sample_o_ready", 2)
        S_ok = sig("state_ready", 8)
        USO_ok = sig("sample_state_read", 2)
        spread_seq = ctx.enter_context(nc.semaphore("spread_steps"))
        UX_ok = sig("spread_ready", 6)
        SS_ok = sig("sample_state_updated", 2)
        kk_sq = sig("kk_squares", 1)
        kk_rn = sig("kk_rnorm", 3)
        rk_ok = sig("rk_products", 1)
        E_ok = sig("rw_decays", 3)
        keys_ok = sig("rw_keys_ready", 3)
        rot_ok = sig("rotated", 1)
        rtk_ok = sig("rt_natural_ready", 3)
        rtR_ok = sig("rt_products", 8)
        rtO_ok = sig("rt_o_ready", 2)
        rtC_ok = sig("rt_cross_ready", 2)
        rtX_ok = sig("rt_spread_ready", 4)
        rtS_ok = sig("rt_state_updated", 1)
        rtSp_ok = sig("rt_prompt_state_ready", 1)
        osq_ok = sig("o_squares_ready", 3)
        orn_ok = sig("o_rnorm_ready", 8)
        rec_ok = sig("recurrent_outputs_ready", 1)
        cat_ok = sig("mixed_ready", 1)
        chosen_ok = sig("chosen_ready", 1)
        h1_full = ctx.enter_context(nc.semaphore("h1_full"))
        h3_full = ctx.enter_context(nc.semaphore("h3_full"))
        silu_done = ctx.enter_context(nc.semaphore("silu_done"))
        hid_ok = ctx.enter_context(nc.semaphore("hidden_ready"))
        hid_used = ctx.enter_context(nc.semaphore("hidden_used"))
        final_ok = sig("y_ready", 3)
        fss_ok = sig("last_squares_summed", 3)
        frs_ok = sig("last_rstd_ready", 3)
        diff_ok = sig("logit_difference", 1)
        odds_ok = sig("odds_ready", 1)
        def counter(name):
            return ctx.enter_context(nc.semaphore(name))

        short_out = counter("short_tile_output_copied")
        short_back = counter("short_tile_columns_transposed")
        dense_out = counter("dense_outputs_of_tile_ready")
        route_in = counter("route_constants_loaded")
        more_ok = counter("overflow_flag_ready")
        lowered = counter("slots_lowered")
        hot_ok = counter("one_hots_built")
        gathered = counter("gathered_halves")
        hot_t_full = counter("one_hots_transposed")
        hot_t_ok = counter("one_hots_by_slot_ready")
        hG_ok = counter("expert_input_halves_ready")
        y_in = counter("expert_output_halves_ready")
        spread_full = counter("outputs_spread")
        x_added = counter("outputs_added")
        lnf_in = ctx.enter_context(nc.semaphore("last_norm_weights_loaded"))
        y_stored = ctx.enter_context(nc.semaphore("y_stored"))
        eps_ok = ctx.enter_context(nc.semaphore("eps_ready"))

        fills = {}

        def fill(pe, *key):
            b, turn = len(fills) % 8, len(fills) // 8
            assert key not in fills, key
            fills[key] = (b, turn)
            if turn:
                pe.wait_ge(bank_free[b], turn)
            return banks[b], bank_full[b]

        def take(eng, *key):
            b, turn = fills[key]
            eng.wait_ge(bank_full[b], turn + 1)
            return banks[b], bank_free[b]

        def mm(pe, out, lhsT, rhs, start=True, stop=True):
            return nc.tensor.matmul(out, lhsT, rhs, start=start, stop=stop, skip_group_check=True)

        def tr(pe, out, in_):
            n = in_.shape[0]
            return nc.tensor.transpose(out, in_, ident[0:n, 0:n])

        def spread(eng, out, src):
            return eng.tensor_tensor(out, over(src, NB, 1), over(cst("bmask", rows=32), HD, 2), MUL)

        def chunk_stages(l, y, t, reads, outputs):
            if t < 0:
                return {"first": []}
            stages = [lambda f=f, c=c: f(l, y, c) for c in (2 * t, 2 * t + 1) for f in (reads, outputs)]
            if t == 0:
                return {"first": [], **{lev + 1: [f] for lev, f in enumerate(stages)}}
            return {"first": stages[:3], 1: stages[3:]}

        def tile_memory(t):
            return (R_other, nat_other) if t == 1 else (R, nat)

        def spread_at(y, p, k):
            if p % 2 == 0:
                return UX[0:32, k, :, :]
            if y == 0:
                return UX[0:32, 2 + k, :, :]
            return conv.rearrange("p a b -> p (a b)")[0:32, k * 512:(k + 1) * 512].rearrange("p (a b) -> p a b", a=NB)

        def half(h):
            return slice(64 * (h % 2), 64 * (h % 2) + 64), h // 2

        block = ctx.enter_context(nc.Block())
        FFN_USES = [len(range(s, FFN_BLOCKS, SLOTS)) for s in range(SLOTS)]
        ROUND_TURNS = MOE_BLOCKS // SLOTS
        EXP_TURNS = EXP_BLOCKS // SLOTS
        SPREAD = [4, 5, 0, 1, 2, 3]

        def expert_rounds(eng, expert, start=lambda r: None):
            start(0)
            with eng.Fori(0, N_EXP) as e:
                expert(0, e)
            eng.wait_ge(more_ok, 1)
            overflow = eng.value_load(more[0:1, 0:1], min_val=0, max_val=1)
            with eng.If(overflow > 0):
                with eng.Fori(1, -(-NT // CAP)) as r:
                    start(r)
                    with eng.Fori(0, N_EXP) as e:
                        expert(r, e)

        @block.tensor
        def _(pe):
            def norm_transposes(l, use):
                for t, (t0, n) in enumerate(TILES):
                    u = use * 3 + t
                    wait(pe, hn_ok, l, u)
                    for part in range(2):
                        b, full = fill(pe, l, "hT", u, part)
                        for q in range(4):
                            k = part * 4 + q
                            i = tr(pe, b[:, q * P:q * P + n], hn_at(use, t)[0:n, k * P:(k + 1) * P])
                        i.then_inc(full, 1)

            def project(l):
                wait(pe, hT_ok, l, 5)
                tiles = list(enumerate(ZTILES))
                for i, (c0, c1) in enumerate(WIN_LOADS):
                    wait(pe, loaded[i % 2], l, i // 2)
                    w = wslot[i % 2][:, 0:KD * (c1 - c0)].rearrange("p (k c) -> p k c", k=KD)
                    last = None
                    if i == AB_LOAD:
                        b, full = fill(pe, l, "ab")
                        for t, (t0, n) in enumerate(TILES):
                            for k in range(KD):
                                last = mm(pe, b[0:n, t * 12:t * 12 + 12], hT[:, k, t0:t0 + n], w[:, k, 0:12],
                                          start=k == 0, stop=k == KD - 1)
                        last.then_inc(full, 1)
                    while tiles and tiles[0][1][2] < c1:
                        m, (_, _, c, n) = tiles.pop(0)
                        b, full = fill(pe, l, "z", m)
                        for k in range(KD):
                            last = mm(pe, b[0:n, 0:NT], w[:, k, c - c0:c - c0 + n], hT[:, k, :],
                                      start=k == 0, stop=k == KD - 1)
                        last.then_inc(full, 1)

            def lora(l):
                wait(pe, lora_loaded, l, 2)
                wait(pe, lora_ok, l, 0)
                for t, (t0, n) in enumerate(TILES):
                    b, full = fill(pe, l, "y", t)
                    mm(pe, b[0:n, 0:384], cst("ones", 0, n, rows=1), w0[:, :], stop=False)
                    mm(pe, b[0:n, 0:384], zs[0:64, 9, t0:t0 + n], w2a2[0:64, :], start=False).then_inc(full, 1)
                for f in range(3):
                    b, full = fill(pe, l, "a", f)
                    mm(pe, b[:, 0:NT], w2a2[64:128, f * P:(f + 1) * P], zs[64:128, 9, :]).then_inc(full, 1)

            def dn_sums(l):
                wait(pe, sq_ok, l, 0)
                for i in range(6):
                    b, full = fill(pe, l, "dnss", i)
                    mm(pe, b[:, 0:NT], cst("ones64"), SQ[:, i, :]).then_inc(full, 1)
                wait(pe, g_ok, l, 0)
                wait(pe, beta_ok, l, 0)
                b, full = fill(pe, l, "cum")
                for t, (t0, n) in enumerate(TILES):
                    mm(pe, b[0:n, t * 12:t * 12 + 6], tri[t][:, 0:n], dn[0:n, 0, t, :])
                    i = mm(pe, b[0:n, t * 12 + 6:t * 12 + 12], tri[t][:, 2 * n:3 * n], dn[0:n, 0, t, :])
                i.then_inc(full, 1)
                b, full = fill(pe, l, "rows_g")
                for t, (t0, n) in enumerate(TILES):
                    i = mm(pe, b[0:H, t0:t0 + n], dn[0:n, 0, t, :], tri[t][:, 0:n])
                i.then_inc(full, 1)
                b, full = fill(pe, l, "rows_b")
                for t, (t0, n) in enumerate(TILES):
                    i = mm(pe, b[0:H, t0:t0 + n], dn[0:n, 1, t, :], ident[0:n, 0:n])
                i.then_inc(full, 1)

            def dn_prepare(l):
                wait(pe, gb_ok, l, 0)
                for p in range(3):
                    sel = pair_sel[:, p * P:(p + 1) * P]
                    b, full = fill(pe, l, "bc_g", p)
                    mm(pe, b[:, 0:NT], sel, gb[:, 0, :]).then_inc(full, 1)
                    b, full = fill(pe, l, "bc_b", p)
                    mm(pe, b[:, 0:NT], sel, gb[:, 1, :]).then_inc(full, 1)

            def dn_tile(l, t):
                t0, n = TILES[t]
                wait(pe, Q_ok, l, 0)
                for name, m in (("k", 3), ("v", 6)):
                    b, full = fill(pe, l, "dn" + name, t)
                    for p in range(3):
                        i = tr(pe, b[0:n, p * P:(p + 1) * P], conv[:, m + p, t0:t0 + n])
                    i.then_inc(full, 1)
                for g in range(2):
                    b, full = fill(pe, l, "E", t, g)
                    for x in range(3):
                        h = 3 * g + x
                        mm(pe, b[0:n, x * n:(x + 1) * n], ident[0:H, h:h + 1].to_broadcast([H, n]), gb[:, 0, t0:t0 + n], stop=False)
                        i = mm(pe, b[0:n, x * n:(x + 1) * n], ident[0:n, 0:n], neg[t][:, 0:n], start=False)
                    i.then_inc(full, 1)
                    for x in range(3):
                        s, p = half(3 * g + x)
                        b, full = fill(pe, l, 0, "products", t, 3 * g + x)
                        mm(pe, b[0:n, 0:2 * n].rearrange("p (a b) -> p a b", a=2), conv[s, 3 + p, t0:t0 + n],
                           Q[s, p, 0:2, t0:t0 + n]).then_inc(full, 1)

            def rw_prepare(l):
                wait(pe, kk_sq, l, 0)
                for f in range(3):
                    b, full = fill(pe, l, "kss", f)
                    mm(pe, b[:, 0:NT], cst("ones64"), SQ[:, f, :]).then_inc(full, 1)
                for f in range(3):
                    b, full = fill(pe, l, "g", f)
                    mm(pe, b[:, 0:NT], g2[:, 0, f * P:(f + 1) * P], zs[:, 10, :], stop=False)
                    mm(pe, b[:, 0:NT], g2[0:32, 1, f * P:(f + 1) * P], zs[0:32, 11, :], start=False).then_inc(full, 1)
                wait(pe, rk_ok, l, 0)
                for f in range(3):
                    b, full = fill(pe, l, "bonus", f)
                    mm(pe, b[:, 0:NT], cst("ones64"), SQ[:, 3 + f, :]).then_inc(full, 1)
                sample_states(l, 0)

            def rw_decays(l, t):
                n = TILES[t][1]
                wait(pe, sg_ok, l, t)
                for f in range(3):
                    b, full = fill(pe, l, "cumw", t, f)
                    mm(pe, b[:, 0:3 * n], sg[0:n, t, f * P:(f + 1) * P], tri[t]).then_inc(full, 1)

            def rw_tile(l, t):
                t0, n = TILES[t]
                wait(pe, keys_ok, l, t)
                srcs = [Q[:, :, 1, t0:t0 + n], ends[:, 0, :, 0:n], zs[:, 6:9, t0:t0 + n], ends[:, 1, :, 0:n]]
                for k, src in enumerate(srcs):
                    b, full = fill(pe, l, "rwnat", t, k)
                    for p in range(3):
                        i = tr(pe, b[0:n, p * P:(p + 1) * P], src[:, p, :])
                    i.then_inc(full, 1)
                for h in range(H):
                    s, p = half(h)
                    b, full = fill(pe, l, 1, "products", t, h)
                    for k in range(2):
                        i = mm(pe, b[0:n, 2 * k * n:2 * (k + 1) * n].rearrange("p (a b) -> p a b", a=2),
                               keys[s, k, p, 0:n], Q[s, p, 0:2, t0:t0 + n])
                    i.then_inc(full, 1)

            def inverses(l, y, t, fillers):
                for f in fillers["first"]:
                    f()
                n = TILES[t][1]
                R, nat = tile_memory(t)
                done = (y * 14 + sum(LEVELS[:t])) * 2
                for g in range(2):
                    wait(pe, R_ok, l, y * 18 + t * 6 + 3 * g + 2)
                    b, full = fill(pe, l, y, "L0", t, g)
                    for x in range(3):
                        i = tr(pe, b[0:n, x * n:(x + 1) * n], R[0:n, 3 * g + x, 1, 0:n])
                    i.then_inc(full, 1)
                for lev in range(1, LEVELS[t]):
                    for g in range(2):
                        wait(pe, T_ok, l, done + (lev - 1) * 2 + g)
                        b, full = fill(pe, l, y, "AT", t, lev, g)
                        for x in range(3):
                            i = mm(pe, b[0:n, x * n:(x + 1) * n], R[0:n, 3 * g + x, 1, 0:n], TM[0:n, g, x, 0:n])
                        i.then_inc(full, 1)
                    for f in fillers.get(lev, []):
                        f()
                    for g in range(2):
                        wait(pe, XM_ok, l, done + lev * 2 + g)
                        if lev < LEVELS[t] - 1:
                            b, full = fill(pe, l, y, "TX", t, lev, g)
                            for x in range(3):
                                i = mm(pe, b[0:n, x * n:(x + 1) * n], TT[0:n, g, x, 0:n], XM[0:n, g, x, 0:n])
                            i.then_inc(full, 1)
                        b, full = fill(pe, l, y, "XT", t, lev, g)
                        for x in range(3):
                            i = mm(pe, b[0:n, x * n:(x + 1) * n], XM[0:n, g, x, 0:n], TT[0:n, g, x, 0:n])
                        i.then_inc(full, 1)
                for g in range(2):
                    wait(pe, T_ok, l, done + (LEVELS[t] - 1) * 2 + g)

            def chunk_inputs(l, y, t):
                n = TILES[t][1]
                R, nat = tile_memory(t)
                wait(pe, natb_ok if y else nat_ok, l, t)
                if y:
                    b, full = fill(pe, l, "XV", t)
                    for h in range(H):
                        i = mm(pe, b[0:n, h * HD:(h + 1) * HD], R[0:n, h, 3, 0:n], nat[0:n, 2, h, :])
                    i.then_inc(full, 1)
                b, full = fill(pe, l, y, "W", t)
                for h in range(H):
                    s, p = half(h)
                    i = mm(pe, b[s, p * n:(p + 1) * n], nat[0:n, 0, h, :], TT[0:n, h // 3, h % 3, 0:n])
                i.then_inc(full, 1)
                if y:
                    wait(pe, XV_ok, l, t)
                v = U if y else nat[:, 2, :, :]
                b, full = fill(pe, l, y, "U0", t)
                for h in range(H):
                    i = mm(pe, b[0:n, h * HD:(h + 1) * HD], TT[0:n, h // 3, h % 3, 0:n], v[0:n, h, :])
                i.then_inc(full, 1)

            def chunk_reads(l, y, c):
                t, cc = c // 2, c % 2
                rows = slice(64 * cc, 64 * cc + 64)
                cols = slice(CHUNK * c, CHUNK * (c + 1))
                st = S[:, y, :, :]
                if c:
                    wait(pe, W_ok, l, y * 3 + t)
                    wait(pe, S_ok, l, y * 4 + c - 1)
                    for odd in range(2):
                        b, full = fill(pe, l, y, "WS", c, odd)
                        for p in range(3):
                            s = slice(64 * odd, 64 * odd + 64)
                            i = mm(pe, b[rows, p * HD:(p + 1) * HD], Q[s, p, 3, cols], st[s, p, :])
                        i.then_inc(full, 1)

            def chunk_outputs(l, y, c):
                t, cc = c // 2, c % 2
                R, nat = tile_memory(t)
                rows = slice(64 * cc, 64 * cc + 64)
                cols = slice(CHUNK * c, CHUNK * (c + 1))
                st = S[:, y, :, :]
                wait(pe, U_ok, l, y * 5 + c)
                b, full = fill(pe, l, y, "O", c)
                for h in range(H):
                    s, p = half(h)
                    out = b[s, p * CHUNK:(p + 1) * CHUNK]
                    inner = slice(64 * cc, 64 * cc + 64)
                    if c:
                        mm(pe, out, st[s, p, :], Q[s, p, 0 if y else 2, cols], stop=False)
                    if y:
                        mm(pe, out, nat[:, 2, h, :], R[:, h, 2, inner], start=c == 0, stop=False)
                    i = mm(pe, out, U[:, h, :], R[:, h, 0, inner], start=c == 0 and not y)
                i.then_inc(full, 1)
                b, full = fill(pe, l, y, "S", c)
                for h in range(H):
                    s, p = half(h)
                    out = b[s, p * HD:(p + 1) * HD]
                    if y:
                        mm(pe, out, nat[rows, 3, h, :], nat[rows, 2, h, :], stop=False)
                    i = mm(pe, out, nat[rows, 1, h, :], U[rows, h, :], start=not y)
                i.then_inc(full, 1)

            def sample_chunks(l, y):
                wait(pe, W_ok, l, y * 3 + 2)
                wait(pe, ss_in, l, y)
                b, full = fill(pe, l, y, "SU")
                for h in range(H):
                    s, p = half(h)
                    for q in range(NB):
                        cols = slice(SEQ + DS * q, SEQ + DS * (q + 1))
                        both = Q[s, p, 0:4:3, cols] if y else Q[s, p, 2:4, cols]
                        out = b[s, p * 64:(p + 1) * 64].rearrange("p (a b) -> p a b", a=2)[:, :, DS * q:DS * (q + 1)]
                        i = mm(pe, out, SS[s, p, q, :], both)
                i.then_inc(full, 1)
                wait(pe, USO_ok, l, y)
                b, full = fill(pe, l, y, "SUT")
                for p in range(3):
                    i = tr(pe, b[0:32, p * P:(p + 1) * P], USO[:, p, 1, :])
                i.then_inc(full, 1)
                wait(pe, U_ok, l, y * 5 + 4)
                b, full = fill(pe, l, y, "O", 4)
                for h in range(H):
                    s, p = half(h)
                    out = b[s, p * 32:(p + 1) * 32]
                    if y:
                        mm(pe, out, nat[0:32, 2, h, :], R[0:32, h, 2, 0:32], stop=False)
                    i = mm(pe, out, U[0:32, h, :], R[0:32, h, 0, 0:32], start=not y)
                i.then_inc(full, 1)

            def sample_states(l, y):
                for p in range(3):
                    wait(pe, UX_ok, l, y * 3 + p)
                    b, full = fill(pe, l, y, "SS", p)
                    for q in range(2):
                        h = 2 * p + q
                        s = half(h)[0]
                        flat = lambda k: spread_at(y, p, k).rearrange("p a b -> p (a b)")
                        if y:
                            mm(pe, b[s, :], nat[0:32, 3, h, :], flat(2 + q), stop=False)
                        i = mm(pe, b[s, :], nat[0:32, 1, h, :], flat(q), start=not y)
                    i.then_inc(full, 1)

            def retention(l):
                wait(pe, z_ok, l, 29)
                for k in range(2):
                    b, full = fill(pe, l, "rot", k)
                    mm(pe, b[:, 0:NT], cst("rot"), rtz[:, k, :]).then_inc(full, 1)
                wait(pe, rot_ok, l, 0)
                for t, (t0, n) in enumerate(TILES):
                    b, full = fill(pe, l, "rtn", t)
                    for k, src in enumerate([aT[:, 2, t0:t0 + n], rtz[:, 2, t0:t0 + n], rtz[:, 3, t0:t0 + n]]):
                        i = tr(pe, b[0:n, k * P:(k + 1) * P], src)
                    i.then_inc(full, 1)
                q, k = aT[:, 0, :], aT[:, 1, :]
                for h in range(RT_H):
                    s = slice(32 * h, 32 * h + 32)
                    b, full = fill(pe, l, "rtp", h)
                    mm(pe, b[:, 0:SEQ], k[s, 0:P], q[s, 0:SEQ])
                    mm(pe, b[:, SEQ:SEQ + P], k[s, P:SEQ], q[s, P:SEQ]).then_inc(full, 1)
                for h in range(RT_H):
                    s = slice(32 * h, 32 * h + 32)
                    b, full = fill(pe, l, "rtp", 4 + h)
                    mm(pe, b[0:32, 0:32], k[s, SEQ:NT], q[s, SEQ:NT]).then_inc(full, 1)
                sample_states(l, 1)
                wait(pe, O_ok, l, 7)
                wait(pe, Os_ok, l, 1)
                means(l, range(3, 6))
                variances(l, 0, range(3))
                variances(l, 1, range(3, 6))
                wait(pe, rtR_ok, l, 7)
                wait(pe, rtk_ok, l, 2)
                wait(pe, rt_state_in, l, 0)
                rp = R.rearrange("p a b c -> p (a b c)")
                rs = keys.rearrange("p a b c -> p (a b c)")
                nat_rt = lambda t: sg[:, t, :]
                V = lambda t, h: nat_rt(t)[:, P + h * HD:P + (h + 1) * HD]
                Kn = lambda t, h: nat_rt(t)[:, 32 * h:32 * h + 32]
                for p in range(2):
                    b, full = fill(pe, l, "rto", p)
                    for hh in range(2):
                        h, s = 2 * p + hh, slice(64 * hh, 64 * hh + 64)
                        m = rp[:, h * 384:(h + 1) * 384]
                        mm(pe, b[s, 0:P], V(0, h), m[:, 0:P])
                        mm(pe, b[s, P:SEQ], V(0, h), m[:, P:SEQ], stop=False)
                        mm(pe, b[s, P:SEQ], V(1, h), m[:, SEQ:SEQ + P], start=False)
                        i = mm(pe, b[s, SEQ:NT], V(2, h)[0:32, :], rs[0:32, 32 * h:32 * h + 32])
                    i.then_inc(full, 1)
                    b, full = fill(pe, l, "rtc", p)
                    for hh in range(2):
                        h, s = 2 * p + hh, slice(64 * hh, 64 * hh + 64)
                        k4 = slice(32 * h, 32 * h + 32)
                        for x in range(NB):
                            i = mm(pe, b[s, DS * x:DS * (x + 1)], SSr[k4, x, :], rt_qd[k4, DS * x:DS * (x + 1)])
                    i.then_inc(full, 1)
                b, full = fill(pe, l, "rts")
                for h in range(RT_H):
                    s = slice(32 * h, 32 * h + 32)
                    mm(pe, b[s, 0:HD], Kn(0, h), V(0, h), stop=False)
                    i = mm(pe, b[s, 0:HD], Kn(1, h), V(1, h), start=False)
                i.then_inc(full, 1)
                b, full = fill(pe, l, "rtss")
                for h in range(RT_H):
                    wait(pe, rtX_ok, l, h)
                    i = mm(pe, b[32 * h:32 * h + 32, :], Kn(2, h)[0:32, :], UX[0:32, h, :, :].rearrange("p a b -> p (a b)"))
                i.then_inc(full, 1)

            def means(l, pairs):
                for p in pairs:
                    b, full = fill(pe, l, "mean", p)
                    mm(pe, b[:, 0:NT], cst("mean64"), OT[:, p, :]).then_inc(full, 1)

            def variances(l, group, pairs):
                wait(pe, osq_ok, l, group)
                for p in pairs:
                    b, full = fill(pe, l, "var", p)
                    mm(pe, b[:, 0:NT], cst("mean64"), conv[:, p, :]).then_inc(full, 1)

            def out_products(l, t, c, bank, ks):
                (c0, c1), (t0, n) = WOUT_LOADS[c], TILES[t]
                n_load = len(WIN_LOADS) + c
                s = n_load % 2
                wait(pe, loaded[s], l, n_load // 2)
                w = wslot[s][:, 0:KD * (c1 - c0)].rearrange("p (k c) -> p k c", k=KD)
                for k in ks:
                    i = mm(pe, bank[0:n, 0:c1 - c0], OT[:, k, t0:t0 + n], w[:, k, :], start=k == 0, stop=k == KD - 1)
                return i

            def out_projection(l):
                ahead = []

                def go_ahead(t):
                    wait(pe, rec_ok, l, 0)
                    ahead.append(fill(pe, l, "out", t, 0))
                    out_products(l, t, 0, ahead[t][0], range(6))

                go_ahead(0)
                wait(pe, rtO_ok, l, 1)
                means(l, range(6, 8))
                go_ahead(1)
                variances(l, 2, range(6, 8))
                go_ahead(2)
                wait(pe, cat_ok, l, 0)
                for t in range(3):
                    out_products(l, t, 0, ahead[t][0], range(6, KD)).then_inc(ahead[t][1], 1)
                for c in range(1, len(WOUT_LOADS)):
                    for t in range(3):
                        bank, full = fill(pe, l, "out", t, c)
                        out_products(l, t, c, bank, range(KD)).then_inc(full, 1)

            def routing(l):
                b, full = fill(pe, l, "logits")
                for t, (t0, n) in enumerate(TILES):
                    for k in range(KD):
                        i = mm(pe, b[0:n, t * N_EXP:(t + 1) * N_EXP], hT[:, k, t0:t0 + n], rt_w[:, k, :],
                               start=k == 0, stop=k == KD - 1)
                i.then_inc(full, 1)
                wait(pe, chosen_ok, 0, 0)
                pe.wait_ge(route_in, 16)
                b, full = fill(pe, l, "slots")
                for t, (t0, n) in enumerate(TILES):
                    for x in range(t):
                        mm(pe, b[0:n, t * N_EXP:(t + 1) * N_EXP], cst("ones", 0, n), small[:, 1, x, :], start=x == 0, stop=False)
                    mm(pe, b[0:n, t * N_EXP:(t + 1) * N_EXP], before[0:n, 0:n], small[0:n, 1, t, :], start=t == 0)
                for t, (t0, n) in enumerate(TILES):
                    i = mm(pe, b[:, 3 * N_EXP:4 * N_EXP], cst("ones", rows=n), small[0:n, 1, t, :], start=t == 0, stop=t == 2)
                i.then_inc(full, 1)

            def hidden(s, turn, tile, src, n):
                w13 = ring[:, s * SLOT:s * SLOT + 2 * KD * FB].rearrange("p (x k f) -> p x k f", x=2, k=KD)
                pe.wait_ge(block_loaded[s], 16 * (turn + 1))
                for x, (full, free) in enumerate(((h1_full, silu_done), (h3_full, hid_ok))):
                    if not (isinstance(tile, int) and tile == 0):
                        pe.wait_ge(free, tile)
                    for k in range(KD):
                        i = mm(pe, banks[6 + x][:, 0:n], w13[:, x, k, :], src[:, k, 0:n], start=k == 0, stop=k == KD - 1)
                    i.then_inc(full, 1)

            def down(s, tile, outs, start, stop):
                w2 = ring[:, s * SLOT + 2 * KD * FB:(s + 1) * SLOT]
                pe.wait_ge(hid_ok, tile + 1)
                for bank, (t0, n) in outs:
                    if n < P:
                        for k in range(KD):
                            i = mm(pe, banks[bank][:, k * n:(k + 1) * n], w2[:, k * P:(k + 1) * P], hid[s][:, t0:t0 + n],
                                   start=False, stop=stop)
                        continue
                    for c in range(2):
                        i = mm(pe, banks[bank + c][0:n, :], hid[s][:, t0:t0 + n], w2[:, c * 512:(c + 1) * 512], start=start, stop=stop)
                    if stop:
                        i.then_inc(dense_out, 1)
                i.then_inc(hid_used, 1)

            def turn_of_ring(slots, turns, tile0, src, n, outs, first=False, last=False):
                for s in range(slots):
                    hidden(s, turns[s], tile0 + s, src, n)
                    if s:
                        down(s - 1, tile0 + s - 1, outs, first and s == 1, False)
                down(slots - 1, tile0 + slots - 1, outs, first and slots == 1, last)

            def start_at_zero(bank):
                nc.tensor.matmul(banks[bank][:, :], zeros[:, 0:P], zeros[:, :], start=True, stop=False, skip_group_check=True)

            def dense(l):
                for b in range(8):
                    pe.wait_ge(bank_free[b], len([1 for v in fills.values() if v[0] == b]))
                turns, rest = divmod(FFN_BLOCKS, SLOTS)
                outs = [(2 * t, tile) for t, tile in enumerate(TILES)]
                start_at_zero(4)
                turn_of_ring(SLOTS, [0] * SLOTS, 0, hT, NT, outs, first=True)
                with pe.Fori(1, turns) as i:
                    turn_of_ring(SLOTS, [i] * SLOTS, i * SLOTS, hT, NT, outs)
                turn_of_ring(rest, [turns] * rest, turns * SLOTS, hT, NT, outs, last=True)
                pe.wait_ge(short_out, 1)
                n = TILES[2][1]
                for k in range(KD):
                    tr(pe, banks[4 + k // 4][0:n, k % 4 * P:(k % 4 + 1) * P], short_y[:, k * n:(k + 1) * n]).then_inc(short_back, 1)

            def gather(r, e, job):
                pe.wait_ge(hot_ok, 6 * (r * (N_EXP + 1) + e + 1))
                pe.wait_ge(x_added, 6 * job + 1)
                for part in range(2):
                    for q in range(4):
                        k = 4 * part + q
                        for t, (t0, n) in enumerate(TILES):
                            i = mm(pe, banks[2 + part][:, q * CAP:(q + 1) * CAP], hn_at(1, t)[0:n, k * P:(k + 1) * P],
                                   hot[0:n, t, :], start=t == 0, stop=t == 2)
                    i.then_inc(gathered, 1)

            def expert(r, e):
                job, taken = r * N_EXP + e, r * (N_EXP + 1) + e
                pe.wait_ge(x_added, 6 * job + 1)
                for t, (t0, n) in enumerate(TILES):
                    i = tr(pe, banks[4][:, t0:t0 + n], hot_w[0:n, t, :])
                i.then_inc(hot_t_full, 1)
                for c in range(2):
                    start_at_zero(c)
                with pe.Fori(0, EXP_TURNS) as i:
                    turn = job * EXP_TURNS + i
                    pe.wait_ge(hG_ok, 2 * (taken + 1))
                    turn_of_ring(SLOTS, [FFN_USES[s] + turn for s in range(SLOTS)], FFN_BLOCKS + turn * SLOTS, hG, CAP,
                                 [(0, (0, CAP))])
                gather(r, e + 1, job)
                pe.wait_ge(hot_t_ok, job + 1)
                pe.wait_ge(y_in, 2 * (job + 1))
                for t, (t0, n) in enumerate(TILES):
                    if t == 2:
                        pe.wait_ge(hG_ok, 2 * (taken + 2))
                    for c in range(2):
                        mm(pe, banks[SPREAD[2 * t + c]][0:n, :], hot_t[:, t0:t0 + n], y_exp[:, c * 512:(c + 1) * 512]).then_inc(spread_full, 1)

            pe.wait_ge(first_inputs, 32)
            for l in range(DEPTH):
                norm_transposes(l, 0)
                project(l)
                if l == 0:
                    pe.wait_ge(inputs, 32)
                dn_sums(l)
                lora(l)
                dn_prepare(l)
                for y in range(2):
                    if y:
                        rw_decays(l, 0)
                        rw_prepare(l)
                    for t in range(3):
                        (rw_tile if y else dn_tile)(l, t)
                        if y and t < 2:
                            rw_decays(l, t + 1)
                        inverses(l, y, t, chunk_stages(l, y, t - 1, chunk_reads, chunk_outputs))
                        chunk_inputs(l, y, t)
                    sample_chunks(l, y)
                retention(l)
                out_projection(l)
                norm_transposes(l, 1)
                wait(pe, hT_ok, l, 11)
                if l == 0:
                    dense(l)
                else:
                    routing(l)
                    for b in range(8):
                        pe.wait_ge(bank_free[b], len([1 for v in fills.values() if v[0] == b]))
                    expert_rounds(pe, expert, lambda r: gather(r, 0, r * N_EXP))

        @block.vector
        def _(dve):
            V = nc.vector
            steps = [0]

            def own(ins):
                steps[0] += 1
                ins.then_inc(dve_seq, 1)
                return steps[0]

            def settle():
                dve.wait_ge(dve_seq, steps[0])

            def tt(out, a, b, op):
                return V.tensor_tensor(out, a, b, op)

            def square_sum(t, n, done):
                own(V.tensor_tensor_reduce(junk[0:n], X[0:n, t, :], X[0:n, t, :], 1.0, 0.0, MUL, ADD, stat[0:n, t, 0:1]))
                settle()
                V.nop().then_inc(done.sem, 1)

            def norm(l, use, add=lambda t: None):
                for t in range(4):
                    if t < 3:
                        add(t)
                        square_sum(t, TILES[t][1], ssq_ok)
                    if t:
                        n = TILES[t - 1][1]
                        wait(dve, root_ok, l, use * 3 + t - 1)
                        V.reciprocal(stat[0:n, t - 1, 2:3], stat[0:n, t - 1, 1:2]).then_inc(rstd_ok.sem, 1)
                if not use:
                    own(V.memset(zc[:, :, 0:PADC], 0.0))
                    own(V.memset(zr[:, :, 0:1], 0.0))
                    own(V.memset(zr[:, 11, 1:], 0.0))
                    settle()
                    V.engine_nop().then_inc(zeroed.sem, 1)
                dve.wait_ge(first_inputs, 32)
                for t in range(3):
                    transposed(l, use, t)
                dve.wait_ge(inputs, 32)

            def transposed(l, use, t):
                t0, n = TILES[t]
                for part in range(2):
                    b, free = take(dve, l, "hT", use * 3 + t, part)
                    w = par(l, "ln_ffn" if use else "ln_mix", 4 * part, 4)
                    tt(hT[:, 4 * part:4 * part + 4, t0:t0 + n], b[:, :].rearrange("p (a b) -> p a b", a=4)[:, :, 0:n],
                       over(w, n, 2), MUL).then_inc(free, 1)
                    V.engine_nop().then_inc(hT_ok.sem, 1)

            def convolve(l):
                n = ZC - PADC
                for g in range(3):
                    wait(dve, z_ok, l, 3 * g + 2)
                    if g:
                        wait(dve, qkv_ok, l, g - 1)
                    for j in range(CONV_W):
                        for m in range(3):
                            w = par(l, "conv", 4 * (3 * g + m) + j)
                            src = zc[:, 3 * g + m, j:j + n]
                            if j == 0:
                                own(V.tensor_scalar(tmp3[:, m, 0:n], src, w, None, MUL))
                            elif j < CONV_W - 1 or m < 2:
                                own(V.scalar_tensor_tensor(tmp3[:, m, 0:n], src, w, tmp3[:, m, 0:n], MUL, ADD))
                            else:
                                V.scalar_tensor_tensor(tmp3[:, m, 0:n], src, w, tmp3[:, m, 0:n], MUL, ADD)\
                                    .then_inc(conv_ok.sem, 1)
                        settle()
                if l:
                    wait(dve, stored, l - 1, 4)
                own(V.tensor_copy(cvo[:, 0, :, 0:PADC], zc[:, :, SEQ:SEQ + PADC]))
                settle()
                V.tensor_copy(seqs(cvo[:, 0, :, PADC:]), seqs(zc[:, :, SEQ + PADC:])[:, :, :, DS:]).then_inc(cvo_ok.sem, 1)

            def gates(l):
                b, free = take(dve, l, "ab")
                own(V.tensor_copy(ab[:, 0:2, :], b[:, 0:24].rearrange("p (a b) -> p a b", a=2)))
                V.tensor_copy(ab[0:32, 2, :], b[0:32, 24:36]).then_inc(free, 1)
                dve.wait_ge(free, fills[(l, "ab")][1] + 1)
                settle()
                V.engine_nop().then_inc(ab_ok.sem, 1)
                tt(dn[:, 2, :, :], ab[:, :, 0:H], over(par(l, "dt", 0, H), 3), ADD).then_inc(dtb_ok.sem, 1)

            def shift(l):
                wait(dve, z_ok, l, 23)
                wait(dve, qkv_ok, l, 2)
                for g in range(4):
                    ms = slice(3 * g, 3 * g + 3)
                    own(tt(tmp3[:, :, 0:ZR - 1], zr[:, ms, 0:ZR - 1], zr[:, ms, 1:ZR], SUB))
                    settle()
                    for m in range(3 * g, 3 * g + 3):
                        x = tmp3[:, m - 3 * g, :]
                        own(V.scalar_tensor_tensor(zs[:, m, 0:SEQ], x[:, 0:SEQ], par(l, "mu", m), zr[:, m, 1:SEQ + 1], MUL, ADD))
                        own(V.scalar_tensor_tensor(zs[:, m, SEQ:].rearrange("p (b s) -> p b s", b=NB),
                                                   five(x, SEQ + 1),
                                                   par(l, "mu", m), five(zr[:, m, :], SEQ + 2), MUL, ADD))
                    settle()
                own(V.tensor_copy(sho[:, 0, :, 0:1], zr[:, :, SEQ:SEQ + 1]))
                settle()
                V.tensor_copy(sho[:, 0, :, 1:], zr[:, :, SEQ + 1:].rearrange("p m (b s) -> p m b s", s=DS + 1)[:, :, :, DS])\
                    .then_inc(sho_ok.sem, 1)
                wait(dve, sho_ok, l, 0)
                V.engine_nop().then_inc(zs_ok.sem, 1)

            def five(a, start):
                base = start - (SEQ + 1)
                return a[:, SEQ + 1:SEQ + 1 + NB * (DS + 1)].rearrange("p (b s) -> p b s", b=NB)[:, :, base:base + DS]

            def dn_prepare(l):
                tt(SQ[:, :, :], conv[:, 0:6, :], conv[:, 0:6, :], MUL).then_inc(sq_ok.sem, 1)
                wait(dve, dtb_ok, l, 0)
                own(V.tensor_scalar(dn[:, 4, :, :], dn[:, 2, :, :], 0.0, None, ALU.max))
                wait(dve, sp_ok, l, 0)
                settle()
                own(tt(dn[:, 4, :, :], dn[:, 4, :, :], dn[:, 3, :, :], ADD))
                wait(dve, negA_ok, l, 0)
                settle()
                V.scalar_tensor_tensor(dn[:, 0, :, :], dn[:, 4, :, :], -1.0, over(dn[:, 11, 0, :], 3), MUL, MUL)\
                    .then_inc(g_ok.sem, 1)
                b, free = take(dve, l, "cum")
                wait(dve, beta_ok, l, 0)
                c = b[:, 0:36].rearrange("p (t k h) -> p k t h", t=3, k=2)
                own(V.tensor_copy(dn[:, 5:7, 0:2, :], c[:, :, 0:2, :]))
                own(V.tensor_copy(dn[0:32, 5:7, 2, :], c[0:32, :, 2, :]))
                settle()
                V.tensor_scalar(dn[:, 10, :, :], dn[:, 5, :, :], -1.0, None, MUL).then_inc(cum_ok.sem, 1)
                V.engine_nop().then_inc(free, 1)
                own(V.tensor_copy(pair_sel.rearrange("p (h d) -> p h d", h=H), over(ident[0:H, 0:H], HD, 2)))
                settle()
                for k, name in enumerate(("rows_g", "rows_b")):
                    b, free = take(dve, l, name)
                    V.tensor_copy(gb[:, k, :], b[0:H, 0:NT]).then_inc(free, 1)
                    dve.wait_ge(free, fills[(l, name)][1] + 1)
                V.engine_nop().then_inc(gb_ok.sem, 1)
                wait(dve, rn_ok, l, 5)
                own(tt(Q[:, :, 0, :], conv[:, 0:3, :], SQ[:, 0:3, :], MUL))
                own(tt(conv[:, 3:6, :], conv[:, 3:6, :], SQ[:, 3:6, :], MUL))
                settle()
                for p in range(3):
                    b, free = take(dve, l, "bc_b", p)
                    tt(Q[:, p, 1, :], conv[:, 3 + p, :], b[:, 0:NT], MUL).then_inc(free, 1)
                wait(dve, eg_ok, l, 2)
                own(tt(Q[:, :, 2, :], Q[:, :, 0, :], eg[:, :, :], MUL))
                wait(dve, egn_ok, l, 0)
                own(tt(dn[:, 9, :, :], dn[:, 7, :, :], dn[:, 1, :, :], MUL))
                settle()
                V.engine_nop().then_inc(Q_ok.sem, 1)

            def dn_tile(l, t):
                n = TILES[t][1]
                R, nat = tile_memory(t)
                heads = lambda b: b[0:n, 0:384].rearrange("p (h d) -> p h d", h=H)
                sc = lambda k: over(dn[0:n, k, t, :], HD, 2)
                b, free = take(dve, l, "dnk", t)
                own(tt(nat[0:n, 0, :, :], heads(b), sc(9), MUL))
                tt(nat[0:n, 1, :, :], heads(b), sc(8), MUL).then_inc(free, 1)
                dve.wait_ge(free, fills[(l, "dnk", t)][1] + 1)
                b, free = take(dve, l, "dnv", t)
                tt(nat[0:n, 2, :, :], heads(b), sc(1), MUL).then_inc(free, 1)
                dve.wait_ge(free, fills[(l, "dnv", t)][1] + 1)
                settle()
                V.engine_nop().then_inc(nat_ok.sem, 1)
                for h in range(H):
                    wait(dve, DI_ok, l, t * 2 + h // 3)
                    b, free = take(dve, l, 0, "products", t, h)
                    tt(R[0:n, h, 0:2, 0:n], b[0:n, 0:2 * n].rearrange("p (a b) -> p a b", a=2),
                       over(DI[0:n, h // 3, h % 3, 0:n], 2), MUL).then_inc(R_ok.sem, 1)
                    wait(dve, R_ok, l, t * 6 + h)
                    V.engine_nop().then_inc(free, 1)

            def inverses(l, y, t, fillers):
                n = TILES[t][1]
                R, nat = tile_memory(t)
                for f in fillers["first"]:
                    f()
                done = (y * 14 + sum(LEVELS[:t])) * 2
                m = lambda a: over(a[0:n, 0:n], 3)
                three = lambda b: b[0:n, 0:3 * n].rearrange("p (a b) -> p a b", a=3)
                for g in range(2):
                    b, free = take(dve, l, y, "L0", t, g)
                    own(tt(TT[0:n, g, :, 0:n], R[0:n, 3 * g:3 * g + 3, 1, 0:n], m(cst("level0_t")), MUL))
                    tt(XM[0:n, g, :, 0:n], three(b), m(cst("level", 0, P)), MUL).then_inc(XM_ok.sem, 1)
                    wait(dve, XM_ok, l, done + g)
                    V.engine_nop().then_inc(free, 1)
                    settle()
                    own(tt(TM[0:n, g, :, 0:n], XM[0:n, g, :, 0:n], m(ident), ADD))
                    settle()
                    tt(TT[0:n, g, :, 0:n], TT[0:n, g, :, 0:n], m(ident), ADD).then_inc(T_ok.sem, 1)
                for lev in range(1, LEVELS[t]):
                    for g in range(2):
                        b, free = take(dve, l, y, "AT", t, lev, g)
                        tt(XM[0:n, g, :, 0:n], three(b), m(cst("level", lev * P, P)), MUL).then_inc(XM_ok.sem, 1)
                        wait(dve, XM_ok, l, done + lev * 2 + g)
                        V.engine_nop().then_inc(free, 1)
                    for f in fillers.get(lev, []):
                        f()
                    for g in range(2):
                        if lev < LEVELS[t] - 1:
                            b, free = take(dve, l, y, "TX", t, lev, g)
                            tt(TM[0:n, g, :, 0:n], TM[0:n, g, :, 0:n], three(b), ADD).then_inc(free, 1)
                            dve.wait_ge(free, fills[(l, y, "TX", t, lev, g)][1] + 1)
                        b, free = take(dve, l, y, "XT", t, lev, g)
                        tt(TT[0:n, g, :, 0:n], TT[0:n, g, :, 0:n], three(b), ADD).then_inc(T_ok.sem, 1)
                        wait(dve, T_ok, l, done + lev * 2 + g)
                        V.engine_nop().then_inc(free, 1)

            def state_decay(y, p, c):
                return decay[:, p, c:c + 1] if y else eg[:, p, CHUNK * (c + 1) - 1:CHUNK * (c + 1)]

            def chunk_reads(l, y, c):
                t, cc = c // 2, c % 2
                rows = slice(64 * cc, 64 * cc + 64)
                wait(dve, U0_ok, l, y * 3 + t)
                if cc == 0:
                    i = V.tensor_copy(U[:, :, :], U0[:, :, :])
                    if c:
                        own(i)
                        settle()
                    else:
                        i.then_inc(U_ok.sem, 1)
                if c:
                    for odd in range(2):
                        b, free = take(dve, l, y, "WS", c, odd)
                        heads = slice(odd, H, 2)
                        tt(U[rows, heads, :], U0[rows, heads, :], b[rows, 0:192].rearrange("p (a b) -> p a b", a=3), SUB)\
                            .then_inc(free, 1)
                        dve.wait_ge(free, fills[(l, y, "WS", c, odd)][1] + 1)
                    V.engine_nop().then_inc(U_ok.sem, 1)

            def chunk_outputs(l, y, c):
                st = S[:, y, :, :]
                b, free = take(dve, l, y, "S", c)
                for p in range(3):
                    new = b[:, p * HD:(p + 1) * HD]
                    if c == 0:
                        i = V.tensor_copy(st[:, p, :], new)
                    else:
                        i = V.scalar_tensor_tensor(st[:, p, :], st[:, p, :], state_decay(y, p, c), new, MUL, ADD)
                    if p < 2:
                        own(i)
                settle()
                i.then_inc(S_ok.sem, 1)
                wait(dve, S_ok, l, y * 4 + c)
                V.engine_nop().then_inc(free, 1)

            def sample_chunks(l, y):
                flat = lambda a: a[0:32, :, :].rearrange("p a b -> p (a b)")
                b, free = take(dve, l, y, "SUT")
                wait(dve, U0_ok, l, y * 3 + 2)
                tt(flat(U), flat(U0), b[0:32, 0:384], SUB).then_inc(U_ok.sem, 1)
                wait(dve, U_ok, l, y * 5 + 4)
                V.engine_nop().then_inc(free, 1)
                b, free = take(dve, l, y, "O", 4)
                tt(OT[:, 3 * y:3 * y + 3, SEQ:], b[:, 0:96].rearrange("p (a b) -> p a b", a=3), USO[:, :, 0, :], ADD)\
                    .then_inc(Os_ok.sem, 1)
                wait(dve, Os_ok, l, y)
                V.engine_nop().then_inc(free, 1)
                if y == 0:
                    own(V.tensor_copy(decay[:, :, 4:12], eg[:, :, SEQ + DS - 1::DS]))
                    settle()

            def sample_states(l, y):
                for p in range(3):
                    own(tt(SS[:, p, :, :], SS[:, p, :, :], over(decay[:, p, 4:12], HD, 2), MUL))
                settle()
                for p in range(3):
                    b, free = take(dve, l, y, "SS", p)
                    tt(SS[:, p, :, :], SS[:, p, :, :], b[:, :].rearrange("p (a b) -> p a b", a=NB), ADD).then_inc(free, 1)
                    dve.wait_ge(free, fills[(l, y, "SS", p)][1] + 1)
                V.engine_nop().then_inc(SS_ok.sem, 1)

            def rw_prepare(l):
                own(V.tensor_scalar(omka, par(l, "ka", 0, 3), -1.0, 1.0, MUL, ADD))
                for f in range(3):
                    own(V.tensor_scalar(KK[:, f, :], zs[:, 3 + f, :], par(l, "kk", f), None, MUL))
                settle()
                tt(SQ[:, 0:3, :], KK[:, :, :], KK[:, :, :], MUL).then_inc(kk_sq.sem, 1)
                wait(dve, aT_ok, l, 2)
                for f in range(3):
                    own(V.tensor_scalar(bonus[:, f, :], aT[:, f, :], par(l, "ka", f), omka[:, f:f + 1], MUL, ADD))
                settle()
                own(tt(zs[:, 3:6, :], zs[:, 3:6, :], bonus[:, :, :], MUL))
                settle()
                for f in range(3):
                    own(V.scalar_tensor_tensor(SQ[:, 3 + f, :], zs[:, f, :], par(l, "rk", f), zs[:, 3 + f, :], MUL, MUL))
                settle()
                V.engine_nop().then_inc(rk_ok.sem, 1)
                wait(dve, kk_rn, l, 2)
                own(tt(KK[:, :, :], KK[:, :, :], SQ[:, 0:3, :], MUL))
                settle()
                own(tt(aT[:, :, :], aT[:, :, :], KK[:, :, :], MUL))
                settle()

            def rw_bonus(l):
                for f in range(3):
                    b, free = take(dve, l, "bonus", f)
                    tt(bonus[:, f, :], b[:, 0:NT], zs[:, 6 + f, :], MUL).then_inc(free, 1)
                    dve.wait_ge(free, fills[(l, "bonus", f)][1] + 1)
                settle()
                sample_states(l, 0)

            def rw_keys(l, t):
                t0, n = TILES[t]
                tok = slice(t0, t0 + n)
                wait(dve, E_ok, l, t)
                own(tt(Q[:, :, 0, tok], zs[:, 0:3, tok], E3[:, :, 0, 0:n], MUL))
                own(tt(Q[:, :, 1, tok], KK[:, :, tok], E3[:, :, 1, 0:n], MUL))
                own(tt(keys[:, 0, :, 0:n], aT[:, :, tok], EI[:, :, 0:n], MUL))
                own(tt(keys[:, 1, :, 0:n], zs[:, 3:6, tok], EI[:, :, 0:n], MUL))
                own(tt(ends[:, 0, :, 0:n], aT[:, :, tok], E3[:, :, 2, 0:n], MUL))
                own(tt(ends[:, 1, :, 0:n], zs[:, 3:6, tok], E3[:, :, 2, 0:n], MUL))
                if t < 2:
                    own(V.tensor_copy(decay[:, :, 2 * t:2 * t + 2], E3[:, :, 0, CHUNK - 1::CHUNK]))
                else:
                    own(V.tensor_copy(decay[:, :, 4:12], E3[:, :, 0, DS - 1:32:DS]))
                settle()
                V.engine_nop().then_inc(keys_ok.sem, 1)

            def rw_tile(l, t):
                n = TILES[t][1]
                R, nat = tile_memory(t)
                for h in range(H):
                    b, free = take(dve, l, 1, "products", t, h)
                    four = lambda a: a.rearrange("p (k a) c -> p k a c", k=2)
                    tt(four(R[0:n, h, :, :])[:, :, :, 0:n], b[0:n, 0:4 * n].rearrange("p (k a c) -> p k a c", k=2, a=2),
                       over(tri[t][:, 0:2 * n].rearrange("p (a c) -> p a c", a=2), 2), MUL).then_inc(R_ok.sem, 1)
                    wait(dve, R_ok, l, 18 + t * 6 + h)
                    V.engine_nop().then_inc(free, 1)

            def copy_av(l, t):
                n = TILES[t][1]
                b, free = take(dve, l, "XV", t)
                V.tensor_copy(U[0:n, :, :].rearrange("p a b -> p (a b)"), b[0:n, 0:384]).then_inc(XV_ok.sem, 1)
                wait(dve, XV_ok, l, t)
                V.engine_nop().then_inc(free, 1)

            def retention(l):
                for k in range(2):
                    b, free = take(dve, l, "rot", k)
                    own(tt(aT[:, k, :], rtz[:, k, :], cst("cos", 0, NT), MUL))
                    tt(gate[:, k, :], b[:, 0:NT], cst("cos", NT, NT), MUL).then_inc(free, 1)
                    dve.wait_ge(free, fills[(l, "rot", k)][1] + 1)
                    settle()
                    own(tt(aT[:, k, :], aT[:, k, :], gate[:, k, :], ADD))
                settle()
                own(tt(aT[:, 2, :], aT[:, 1, :], cst("kdec"), MUL))
                own(tt(rt_qd, aT[:, 0, SEQ:], cst("qdec"), MUL))
                settle()
                V.engine_nop().then_inc(rot_ok.sem, 1)
                rp = R.rearrange("p a b c -> p (a b c)")
                for h in range(RT_H):
                    b, free = take(dve, l, "rtp", h)
                    own(tt(rp[:, h * 384:h * 384 + SEQ], b[:, 0:SEQ], cst("rt_mask", h * SEQ, SEQ), MUL))
                    tt(rp[:, h * 384 + SEQ:(h + 1) * 384], b[:, SEQ:384], cst("rt_mask", h * SEQ, P), MUL).then_inc(free, 1)
                    dve.wait_ge(free, fills[(l, "rtp", h)][1] + 1)
                    settle()
                    V.engine_nop().then_inc(rtR_ok.sem, 1)
                for h in range(RT_H):
                    b, free = take(dve, l, "rtp", 4 + h)
                    tt(keys.rearrange("p a b c -> p (a b c)")[0:32, 32 * h:32 * h + 32], b[0:32, 0:32],
                       cst("rt_mask_s", 32 * h, 32, rows=32), MUL).then_inc(free, 1)
                    dve.wait_ge(free, fills[(l, "rtp", 4 + h)][1] + 1)
                    V.engine_nop().then_inc(rtR_ok.sem, 1)
                sample_states(l, 1)
                wait(dve, rtk_ok, l, 2)
                wait(dve, Os_ok, l, 1)
                recurrent_norms(l)
                for p in range(2):
                    b, free = take(dve, l, "rto", p)
                    own(V.tensor_copy(OT[:, 6 + p, 0:SEQ], b[:, 0:SEQ]))
                    wait(dve, rtC_ok, l, p)
                    tt(OT[:, 6 + p, SEQ:], b[:, SEQ:NT], USO[:, p, 0, :], ADD).then_inc(free, 1)
                    dve.wait_ge(free, fills[(l, "rto", p)][1] + 1)
                    settle()
                    V.engine_nop().then_inc(rtO_ok.sem, 1)
                b, free = take(dve, l, "rtss")
                x = SSr[:, :, :].rearrange("p a b -> p (a b)")
                V.scalar_tensor_tensor(x, x, cst("g4"), b[:, :], MUL, ADD).then_inc(rtS_ok.sem, 1)
                wait(dve, rtS_ok, l, 0)
                V.engine_nop().then_inc(free, 1)

            def deviations(l, pairs):
                for p in pairs:
                    b, free = take(dve, l, "mean", p)
                    tt(OT[:, p, :], OT[:, p, :], b[:, 0:NT], SUB).then_inc(free, 1)
                    dve.wait_ge(free, fills[(l, "mean", p)][1] + 1)
                squares(pairs)

            def squares(pairs):
                ps = slice(pairs[0], pairs[-1] + 1)
                tt(conv[:, ps, :], OT[:, ps, :], OT[:, ps, :], MUL).then_inc(osq_ok.sem, 1)

            def scaled(l, pairs, weights):
                for p, w in zip(pairs, weights):
                    wait(dve, orn_ok, l, p)
                    own(V.scalar_tensor_tensor(OT[:, p, :], OT[:, p, :], w, conv[:, p, :], MUL, MUL))
                settle()

            def recurrent_norms(l):
                wait(dve, O_ok, l, 7)
                squares(range(3))
                deviations(l, range(3, 6))
                scaled(l, range(6), [par(l, "dn_norm")] * 3 + [par(l, "ln_g", f) for f in range(3)])
                own(tt(OT[:, 0:3, :], OT[:, 0:3, :], zg[:, :, :], MUL))
                for f in range(3):
                    own(V.scalar_tensor_tensor(OT[:, 3 + f, :], OT[:, 3 + f, :], par(l, "ln_b", f), bonus[:, f, :], ADD, ADD))
                wait(dve, gT_ok, l, 0)
                settle()
                tt(OT[:, 3:6, :], OT[:, 3:6, :], zs[:, 9:12, :], MUL).then_inc(rec_ok.sem, 1)

            def retention_norms(l):
                deviations(l, range(6, 8))
                scaled(l, range(6, 8), [par(l, "rt_ln", f) for f in range(2)])
                tt(OT[:, 6:8, :], OT[:, 6:8, :], rtz[:, 4:6, :], MUL).then_inc(cat_ok.sem, 1)

            def residual(l):
                for c in range(len(WOUT_LOADS) - 1):
                    for t in range(3):
                        add_columns(l, t, c)
                    V.engine_nop().then_inc(out_ok.sem, 1)

            def add_columns(l, t, c):
                c0, c1 = WOUT_LOADS[c]
                n = TILES[t][1]
                b, free = take(dve, l, "out", t, c)
                x = X[0:n, t, c0:c1]
                tt(x, x, b[0:n, 0:c1 - c0], ADD).then_inc(free, 1)
                dve.wait_ge(free, fills[(l, "out", t, c)][1] + 1)

            def add_last_columns(l, t):
                add_columns(l, t, len(WOUT_LOADS) - 1)
                if t == 2:
                    V.engine_nop().then_inc(out_ok.sem, 1)

            def routing(l):
                b, free = take(dve, l, "logits")
                own(V.tensor_copy(small[:, 0, 0:2, :], b[:, 0:16].rearrange("p (a b) -> p a b", a=2)))
                V.tensor_copy(small[0:32, 0, 2, :], b[0:32, 16:24]).then_inc(free, 1)
                dve.wait_ge(free, fills[(l, "logits")][1] + 1)
                settle()
                rank = over(cst("rank"), 3)
                top = lambda k: over(stat[:, :, k], N_EXP, 2)

                def pick(src, scored, hot, k):
                    own(V.tensor_reduce(stat[:, :, k], small[:, src, :, :], AX.X, ALU.max))
                    settle()
                    own(tt(small[:, scored, :, :], small[:, src, :, :], top(k), ALU.is_equal))
                    settle()
                    own(tt(small[:, scored, :, :], small[:, scored, :, :], rank, MUL))
                    settle()
                    own(V.tensor_reduce(stat[:, :, k + 1], small[:, scored, :, :], AX.X, ALU.max))
                    settle()
                    own(tt(small[:, hot, :, :], small[:, scored, :, :], top(k + 1), ALU.is_equal))
                    settle()

                pick(0, 1, 2, 3)
                own(V.scalar_tensor_tensor(small[:, 3, :, :], small[:, 2, :, :], -3e38, small[:, 0, :, :], MUL, ADD))
                settle()
                pick(3, 4, 5, 5)
                tt(small[:, 1, :, :], small[:, 2, :, :], small[:, 5, :, :], ADD).then_inc(chosen_ok.sem, 1)
                own(tt(stat[:, :, 7], stat[:, :, 5], stat[:, :, 3], SUB))
                settle()
                V.engine_nop().then_inc(diff_ok.sem, 1)
                wait(dve, odds_ok, 0, 0)
                own(V.tensor_scalar(stat[:, :, 3], stat[:, :, 8], 1.0, None, ADD))
                settle()
                own(V.reciprocal(stat[:, :, 5], stat[:, :, 3]))
                settle()
                own(tt(stat[:, :, 6], stat[:, :, 5], stat[:, :, 8], MUL))
                own(tt(small[:, 2, :, :], small[:, 2, :, :], top(5), MUL))
                settle()
                own(tt(small[:, 5, :, :], small[:, 5, :, :], top(6), MUL))
                settle()
                own(tt(route[:, 1, :, 0:N_EXP], small[:, 2, :, :], small[:, 5, :, :], ADD))
                b, free = take(dve, l, "slots")
                own(V.tensor_copy(small[:, 0, 0:2, :], b[:, 0:2 * N_EXP].rearrange("p (a b) -> p a b", a=2)))
                own(V.tensor_copy(small[0:32, 0, 2, :], b[0:32, 2 * N_EXP:3 * N_EXP]))
                V.tensor_reduce(stat[:, 0, 3:4], b[:, 3 * N_EXP:4 * N_EXP], AX.X, ALU.max).then_inc(free, 1)
                dve.wait_ge(free, fills[(l, "slots")][1] + 1)
                settle()
                own(V.scalar_tensor_tensor(small[:, 3, :, :], small[:, 0, :, :], 1.0, small[:, 1, :, :], ADD, MUL))
                own(V.tensor_scalar(stat[0:1, 0, 4:5], stat[0:1, 0, 3:4], CAP + 0.5, None, ALU.is_gt))
                settle()
                own(V.tensor_scalar(route[:, 0, :, 0:N_EXP], small[:, 3, :, :], -1.0, None, ADD))
                V.tensor_copy(more[0:1, 0:1], stat[0:1, 0, 4:5]).then_inc(more_ok, 1)
                dve.wait_ge(more_ok, 1)
                settle()
                dve.wait_ge(route_in, 16)
                V.engine_nop().then_inc(x_added, 1)

            def hidden(s, tile, n):
                dve.wait_ge(silu_done, tile + 1)
                dve.wait_ge(h3_full, tile + 1)
                if not isinstance(tile, int) or tile >= SLOTS:
                    dve.wait_ge(hid_used, tile + 1 - SLOTS)
                tt(hid[s][:, 0:n], silu_h[:, 0:n], banks[7][:, 0:n], MUL).then_inc(hid_ok, 1)

            def dense(l):
                turns, rest = divmod(FFN_BLOCKS, SLOTS)
                for s in range(SLOTS):
                    hidden(s, s, NT)
                with dve.Fori(1, turns) as i:
                    for s in range(SLOTS):
                        hidden(s, i * SLOTS + s, NT)
                for s in range(rest):
                    hidden(s, turns * SLOTS + s, NT)

            def add_dense(t):
                m = TILES[t][1]
                if t < 2:
                    dve.wait_ge(dense_out, t + 1)
                else:
                    dve.wait_ge(hid_used, FFN_BLOCKS)
                    V.tensor_copy(short_y, banks[4][:, 0:KD * m]).then_inc(short_out, 1)
                for c in range(2):
                    if t == 2:
                        dve.wait_ge(short_back, 4 * (c + 1))
                    x = X[0:m, t, c * 512:(c + 1) * 512]
                    own(tt(x, x, banks[2 * t + c][0:m, :], ADD))
                settle()

            def build(r, e):
                for t, (t0, n) in enumerate(TILES):
                    pos, weight = (column(n, k, t, e) for k in range(2))
                    V.tensor_scalar(hot[0:n, t, :], iota[0:n, :], pos, None, ALU.is_equal).then_inc(hot_ok, 1)
                    V.tensor_scalar(hot_w[0:n, t, :], iota[0:n, :], pos, weight, ALU.is_equal, MUL).then_inc(hot_ok, 1)

            def column(n, k, t, e):
                if isinstance(e, int):
                    return route[0:n, k, t, e:e + 1]
                return route[0:n, k, t, bass.ds(e, 1)]

            def start_round(r):
                if not isinstance(r, int):
                    dve.wait_ge(gathered, 2 * (N_EXP + 1) * r)
                    V.tensor_scalar(route[:, 0, :, :], route[:, 0, :, :], -float(CAP), None, ADD).then_inc(lowered, 1)
                    dve.wait_ge(lowered, r)
                build(r, 0)
                take_gathered(r, 0)

            def take_gathered(r, e):
                for part in range(2):
                    dve.wait_ge(gathered, 2 * (r * (N_EXP + 1) + e) + part + 1)
                    w = par(1, "ln_ffn", 4 * part, 4)
                    tt(hG[:, 4 * part:4 * part + 4, :], banks[2 + part][:, :].rearrange("p (a b) -> p a b", a=4),
                       over(w, CAP, 2), MUL).then_inc(hG_ok, 1)

            def expert(r, e):
                job = r * N_EXP + e
                with dve.Fori(0, EXP_TURNS) as i:
                    for s in range(SLOTS):
                        hidden(s, FFN_BLOCKS + (job * EXP_TURNS + i) * SLOTS + s, CAP)
                dve.wait_ge(hot_t_full, job + 1)
                build(r, e + 1)
                dve.wait_ge(hid_used, FFN_BLOCKS + EXP_BLOCKS * (job + 1))
                V.tensor_copy(y_exp[:, 512:], banks[1][:, :]).then_inc(y_in, 1)
                take_gathered(r, e + 1)
                for t, (t0, n) in enumerate(TILES):
                    for c in range(2):
                        dve.wait_ge(spread_full, 6 * job + 2 * t + c + 1)
                        x = X[0:n, t, c * 512:(c + 1) * 512]
                        tt(x, x, banks[SPREAD[2 * t + c]][0:n, :], ADD).then_inc(x_added, 1)
                dve.wait_ge(x_added, 6 * (job + 1) + 1)

            for k, e in enumerate(EPS):
                V.memset(eps(k), e).then_inc(eps_ok, 1)
            own(V.memset(ab[:, :, :], 0.0))
            own(V.memset(dn[:, :, :, :], 0.0))
            own(V.memset(small[:, :, :, :], 0.0))
            own(V.memset(route[:, :, :, :], -1.0))
            own(V.memset(zeros[:, :], 0.0))
            own(V.memset(stat[:, :, :], 0.0))
            settle()
            dve.wait_ge(x_loaded, 48)
            for l in range(DEPTH):
                norm(l, 0, add_dense if l else lambda t: None)
                wait(dve, pads_ok, l, 0)
                convolve(l)
                gates(l)
                shift(l)
                dn_prepare(l)
                for y in range(2):
                    if y:
                        rw_prepare(l)
                        rw_keys(l, 0)
                        rw_bonus(l)
                    for t in range(3):
                        (rw_tile if y else dn_tile)(l, t)
                        fillers = chunk_stages(l, y, t - 1, chunk_reads, chunk_outputs)
                        if y and t < 2:
                            fillers[1] = [lambda: rw_keys(l, t + 1)] + fillers.get(1, [])
                        inverses(l, y, t, fillers)
                        if y:
                            copy_av(l, t)
                    sample_chunks(l, y)
                retention(l)
                retention_norms(l)
                residual(l)
                norm(l, 1, lambda t: add_last_columns(l, t))
                if l == 0:
                    dense(l)
                else:
                    routing(l)
                    expert_rounds(dve, expert, start_round)
            dve.wait_ge(lnf_in, 16)
            for t in range(4):
                if t < 3:
                    square_sum(t, TILES[t][1], fss_ok)
                if t:
                    n = TILES[t - 1][1]
                    wait(dve, frs_ok, 0, t - 1)
                    own(V.reciprocal(stat[0:n, t - 1, 2:3], stat[0:n, t - 1, 1:2]))
                    settle()
                    V.scalar_tensor_tensor(X[0:n, t - 1, :], X[0:n, t - 1, :], stat[0:n, t - 1, 2:3], lnf[0:n, :], MUL, MUL)\
                        .then_inc(final_ok.sem, 1)

        @block.scalar
        def _(act):
            A = nc.scalar.activation
            steps = [0]

            def own(ins):
                steps[0] += 1
                ins.then_inc(act_seq, 1)

            def settle():
                act.wait_ge(act_seq, steps[0])

            def copy(out, in_):
                return A(out, in_, ACT.Copy)

            def root(t, summed, done):
                n = TILES[t][1]
                wait(act, *summed)
                A(stat[0:n, t, 1:2], stat[0:n, t, 0:1], ACT.Sqrt, bias=eps(0)[0:n], scale=1.0 / D).then_inc(done.sem, 1)

            def norm(l, use):
                for t in range(4):
                    if t < 3:
                        root(t, (ssq_ok, l, use * 3 + t), root_ok)
                    if t:
                        n = TILES[t - 1][1]
                        wait(act, rstd_ok, l, use * 3 + t - 1)
                        if t == 3 and not use:
                            wait(act, hT_ok, l, 1)
                        A(hn_at(use, t - 1)[0:n], X[0:n, t - 1, :], ACT.Copy, scale=stat[0:n, t - 1, 2:3]).then_inc(hn_ok.sem, 1)

            LORA_AT = 27

            def project(l):
                for m, (kind, k, _, n) in enumerate(ZTILES):
                    if m == 12:
                        wait(act, zeroed, l, 0)
                    b, free = take(act, l, "z", m)
                    sample = b[0:n, SEQ:NT].rearrange("p (b s) -> p b s", b=NB)
                    if kind == "conv":
                        own(copy(zc[:, k, PADC:PADC + SEQ], b[:, 0:SEQ]))
                        i = copy(zc[:, k, PADC + SEQ:].rearrange("p (b s) -> p b s", b=NB)[:, :, PADC:], sample)
                    elif kind == "rw":
                        own(copy(zr[0:n, k, 1:1 + SEQ], b[0:n, 0:SEQ]))
                        i = copy(zr[0:n, k, 1 + SEQ:].rearrange("p (b s) -> p b s", b=NB)[:, :, 1:], sample)
                    elif kind == "zg":
                        i = A(zg[:, k, :], b[:, 0:NT], ACT.Silu)
                    else:
                        i = A(rtz[:, k, :], b[:, 0:NT], ACT.Silu if k >= 4 else ACT.Copy)
                    i.then_inc(free, 1)
                    act.wait_ge(free, fills[(l, "z", m)][1] + 1)
                    settle()
                    nc.scalar.nop().then_inc(z_ok.sem, 1)
                    if m == LORA_AT:
                        softplus(l)
                        lora_inputs(l)
                    if m in (11, 14, 17):
                        g = (m - 11) // 3
                        wait(act, conv_ok, l, g)
                        own(A(conv[:, 3 * g:3 * g + 3, 0:SEQ], tmp3[:, :, 0:SEQ], ACT.Silu))
                        for x in range(3):
                            own(A(conv[:, 3 * g + x, SEQ:].rearrange("p (b s) -> p b s", b=NB),
                                  tmp3[:, x, PADC + SEQ:].rearrange("p (b s) -> p b s", b=NB)[:, :, 0:DS], ACT.Silu))
                        settle()
                        nc.scalar.nop().then_inc(qkv_ok.sem, 1)

            def lora_inputs(l):
                wait(act, ab_ok, l, 0)
                A(dn[:, 1, :, :], ab[:, :, H:], ACT.Sigmoid).then_inc(beta_ok.sem, 1)
                wait(act, zs_ok, l, 0)
                own(A(zs[0:64, 9, :], zs[0:64, 9, :], ACT.Tanh))
                own(A(zs[:, 10, :], zs[:, 10, :], ACT.Sigmoid))
                own(A(zs[0:32, 11, :], zs[0:32, 11, :], ACT.Sigmoid))
                settle()
                nc.scalar.nop().then_inc(lora_ok.sem, 1)

            def lora(l):
                for t, (t0, n) in enumerate(TILES):
                    b, free = take(act, l, "y", t)
                    A(sg[0:n, t, :], b[0:n, 0:384], ACT.Sigmoid).then_inc(free, 1)
                    act.wait_ge(free, fills[(l, "y", t)][1] + 1)
                    nc.scalar.nop().then_inc(sg_ok.sem, 1)
                for f in range(3):
                    b, free = take(act, l, "a", f)
                    A(aT[:, f, :], b[:, 0:NT], ACT.Sigmoid, bias=par(l, "a0", f)).then_inc(free, 1)
                    act.wait_ge(free, fills[(l, "a", f)][1] + 1)
                    nc.scalar.nop().then_inc(aT_ok.sem, 1)

            GROUP_EPS = [0, 0, 0, 2, 2, 2, 3, 3]

            def inverse_roots(l, roots, done):
                for key, out, eps_k, _ in roots:
                    b, free = take(act, l, *key)
                    A(out, b[:, 0:NT], ACT.Ln, bias=eps(eps_k)).then_inc(free, 1)
                for key, out, _, factor in roots:
                    act.wait_ge(bank_free[fills[(l, *key)][0]], fills[(l, *key)][1] + 1)
                    A(out, out, ACT.Exp, scale=-0.5, bias=factor if factor is not None else 0.0).then_inc(done.sem, 1)

            def softplus(l):
                A(dn[:, 11, 0, :], par(l, "a_log", 0, H), ACT.Exp).then_inc(negA_ok.sem, 1)
                wait(act, dtb_ok, l, 0)
                own(A(dn[:, 3, :, :], dn[:, 2, :, :], ACT.Abs))
                settle()
                own(A(dn[:, 3, :, :], dn[:, 3, :, :], ACT.Exp, scale=-1.0))
                settle()
                A(dn[:, 3, :, :], dn[:, 3, :, :], ACT.Ln, bias=1.0).then_inc(sp_ok.sem, 1)

            def dn_prepare(l):
                for p in range(3):
                    b, free = take(act, l, "bc_g", p)
                    A(eg[:, p, :], b[:, 0:NT], ACT.Exp).then_inc(free, 1)
                    act.wait_ge(free, fills[(l, "bc_g", p)][1] + 1)
                    nc.scalar.nop().then_inc(eg_ok.sem, 1)

            def dn_tile(l, t):
                n = TILES[t][1]
                for g in range(2):
                    b, free = take(act, l, "E", t, g)
                    for x in range(3):
                        h = 3 * g + x
                        i = A(DI[0:n, g, x, 0:n], b[0:n, x * n:(x + 1) * n], ACT.Exp, bias=dn[0:n, 10, t, h:h + 1])
                        if x < 2:
                            own(i)
                    i.then_inc(free, 1)
                    act.wait_ge(free, fills[(l, "E", t, g)][1] + 1)
                    settle()
                    nc.scalar.nop().then_inc(DI_ok.sem, 1)

            def rw_decays(l, t):
                n = TILES[t][1]
                if t:
                    wait(act, keys_ok, l, t - 1)
                for f in range(3):
                    b, free = take(act, l, "cumw", t, f)
                    own(A(E3[:, f, :, 0:n], b[:, 0:3 * n].rearrange("p (a b) -> p a b", a=3), ACT.Exp, scale=-RW_DECAY))
                    A(EI[:, f, 0:n], b[:, 0:n], ACT.Exp, scale=RW_DECAY).then_inc(free, 1)
                    act.wait_ge(free, fills[(l, "cumw", t, f)][1] + 1)
                settle()
                nc.scalar.nop().then_inc(E_ok.sem, 1)

            def rw_tile(l, t):
                n = TILES[t][1]
                R, nat = tile_memory(t)
                for k in range(4):
                    b, free = take(act, l, "rwnat", t, k)
                    copy(nat[0:n, k, :, :].rearrange("p a b -> p (a b)"), b[0:n, 0:384]).then_inc(free, 1)
                    act.wait_ge(free, fills[(l, "rwnat", t, k)][1] + 1)
                nc.scalar.nop().then_inc(natb_ok.sem, 1)

            def chunk_inputs(l, y, t):
                t0, n = TILES[t]
                b, free = take(act, l, y, "W", t)
                copy(Q[:, :, 3, t0:t0 + n], b[:, 0:3 * n].rearrange("p (a b) -> p a b", a=3)).then_inc(W_ok.sem, 1)
                wait(act, W_ok, l, y * 3 + t)
                nc.scalar.nop().then_inc(free, 1)
                b, free = take(act, l, y, "U0", t)
                A(U0[0:n, :, :].rearrange("p a b -> p (a b)"), b[0:n, 0:384], ACT.Copy, scale=-1.0 if y else 1.0)\
                    .then_inc(U0_ok.sem, 1)
                wait(act, U0_ok, l, y * 3 + t)
                nc.scalar.nop().then_inc(free, 1)

            def prompt_chunk(l, y, c):
                b, free = take(act, l, y, "O", c)
                copy(OT[:, 3 * y:3 * y + 3, CHUNK * c:CHUNK * (c + 1)], b[:, 0:3 * CHUNK].rearrange("p (a b) -> p a b", a=3))\
                    .then_inc(O_ok.sem, 1)
                wait(act, O_ok, l, y * 4 + c)
                nc.scalar.nop().then_inc(free, 1)

            def sample_chunks(l, y):
                b, free = take(act, l, y, "SU")
                copy(USO[:, :, :, :].rearrange("p a b c -> p (a b c)"), b[:, 0:192]).then_inc(USO_ok.sem, 1)
                wait(act, USO_ok, l, y)
                nc.scalar.nop().then_inc(free, 1)

            def rw_prepare(l):
                inverse_roots(l, [(("kss", f), SQ[:, f, :], 1, None) for f in range(3)], kk_rn)
                take(act, l, "g", 2)
                for f in range(3):
                    b, free = take(act, l, "g", f)
                    copy(zs[:, 9 + f, :], b[:, 0:NT]).then_inc(free, 1)
                    act.wait_ge(free, fills[(l, "g", f)][1] + 1)
                nc.scalar.nop().then_inc(gT_ok.sem, 1)

            def retention(l):
                for t, (t0, n) in enumerate(TILES):
                    b, free = take(act, l, "rtn", t)
                    copy(sg[0:n, t, :], b[0:n, 0:384]).then_inc(free, 1)
                    act.wait_ge(free, fills[(l, "rtn", t)][1] + 1)
                    nc.scalar.nop().then_inc(rtk_ok.sem, 1)
                head_roots(l, range(6), GROUP_EPS)
                for p in range(2):
                    b, free = take(act, l, "rtc", p)
                    copy(USO[:, p, 0, :], b[:, 0:32]).then_inc(free, 1)
                    act.wait_ge(free, fills[(l, "rtc", p)][1] + 1)
                    nc.scalar.nop().then_inc(rtC_ok.sem, 1)
                b, free = take(act, l, "rts")
                copy(Sr[:, l, :], b[:, 0:HD]).then_inc(rtSp_ok.sem, 1)
                wait(act, rtSp_ok, l, 0)
                nc.scalar.nop().then_inc(free, 1)

            def head_roots(l, pairs, eps_k):
                inverse_roots(l, [(("var", p), conv[:, p, :], eps_k[p], None) for p in pairs], orn_ok)

            def routing(l):
                wait(act, diff_ok, 0, 0)
                A(stat[:, :, 8], stat[:, :, 7], ACT.Exp).then_inc(odds_ok.sem, 1)

            def silu(tile, n):
                act.wait_ge(h1_full, tile + 1)
                if not isinstance(tile, int) or tile:
                    act.wait_ge(hid_ok, tile)
                A(silu_h[:, 0:n], banks[6][:, 0:n], ACT.Silu).then_inc(silu_done, 1)

            def dense(l):
                turns, rest = divmod(FFN_BLOCKS, SLOTS)
                for s in range(SLOTS):
                    silu(s, NT)
                with act.Fori(1, turns) as i:
                    for s in range(SLOTS):
                        silu(i * SLOTS + s, NT)
                for s in range(rest):
                    silu(turns * SLOTS + s, NT)

            def expert(r, e):
                job = r * N_EXP + e
                act.wait_ge(hot_t_full, job + 1)
                copy(hot_t, banks[4][:, 0:NT]).then_inc(hot_t_ok, 1)
                with act.Fori(0, EXP_TURNS) as i:
                    for s in range(SLOTS):
                        silu(FFN_BLOCKS + (job * EXP_TURNS + i) * SLOTS + s, CAP)
                act.wait_ge(hid_used, FFN_BLOCKS + EXP_BLOCKS * (job + 1))
                copy(y_exp[:, 0:512], banks[0][:, :]).then_inc(y_in, 1)

            act.dma_start(C[:, 0:P], consts[:, 0:P]).then_inc(first_inputs, 16)
            act.dma_start(PC[:, :, :], pcol.rearrange("l p c -> p l c")).then_inc(first_inputs, 16)
            act.wait_ge(x_loaded, 48)
            act.wait_ge(eps_ok, len(EPS))
            for l in range(DEPTH):
                norm(l, 0)
                if l == 0:
                    act.wait_ge(inputs, 32)
                for k in range(2):
                    wait(act, seq_states, l, k)
                own(copy(seqs(zc[:, :, PADC + SEQ:])[:, :, :, 0:PADC], seqs(cvs[:, :, :])))
                wait(act, zeroed, l, 0)
                own(copy(zr[:, :, 1 + SEQ:].rearrange("p m (b s) -> p m b s", s=DS + 1)[:, :, :, 0], shs[:, :, :]))
                settle()
                nc.scalar.nop().then_inc(pads_ok.sem, 1)
                project(l)
                inverse_roots(l, [(("dnss", i), SQ[:, i, :], 1, eps(4) if i < 3 else None) for i in range(6)], rn_ok)
                wait(act, cum_ok, l, 0)
                A(dn[:, 7:9, :, :], dn[:, 5:7, :, :], ACT.Exp).then_inc(egn_ok.sem, 1)
                lora(l)
                dn_prepare(l)
                for y in range(2):
                    if y:
                        rw_decays(l, 0)
                        rw_prepare(l)
                    for t in range(3):
                        (rw_tile if y else dn_tile)(l, t)
                        if y and t < 2:
                            rw_decays(l, t + 1)
                        if t:
                            prompt_chunk(l, y, 2 * t - 2)
                            prompt_chunk(l, y, 2 * t - 1)
                        chunk_inputs(l, y, t)
                    sample_chunks(l, y)
                retention(l)
                head_roots(l, range(6, 8), GROUP_EPS)
                norm(l, 1)
                if l == 0:
                    dense(l)
                else:
                    routing(l)
                    expert_rounds(act, expert)
            for t in range(3):
                root(t, (fss_ok, 0, t), frs_ok)

        @block.sync
        def _(sp):
            def load(s, src, turn, used):
                sp.wait_ge(hid_used, used)
                sp.dma_start(slot[s], src[bass.ds(turn * SLOTS + s, 1)].rearrange("a p c -> p (a c)")).then_inc(block_loaded[s], 16)

            for t, (t0, n) in enumerate(TILES):
                sp.dma_start(X[0:n, t, :], x_in[t0:t0 + n, :]).then_inc(x_loaded, 16)
            sp.wait_ge(x_loaded, 48)
            for l in range(DEPTH):
                if l:
                    sp.wait_ge(hid_used, FFN_BLOCKS)
                for i in range(MIX_LOADS):
                    s = i % 2
                    if i >= 2:
                        if len(WIN_LOADS) <= i < len(WIN_LOADS) + 2:
                            wait(sp, S_ok, l, 7)
                        elif i - 2 < len(WIN_LOADS):
                            wait(sp, z_ok, l, [m for m, z in enumerate(ZTILES) if z[2] < WIN_LOADS[i - 2][1]][-1])
                        else:
                            wait(sp, out_ok, l, i - 2 - len(WIN_LOADS))
                    if i < len(WIN_LOADS):
                        c0, c1 = WIN_LOADS[i]
                        dst = wslot[s][:, 0:KD * (c1 - c0)].rearrange("p (k c) -> p k c", k=KD)
                        src = w_in[l].rearrange("(k p) c -> p k c", p=P)[:, :, c0:c1]
                    else:
                        c0, c1 = WOUT_LOADS[i - len(WIN_LOADS)]
                        dst = wslot[s][:, 0:KD * (c1 - c0)].rearrange("p (k c) -> p k c", k=KD)
                        src = w_out[l].rearrange("(k p) c -> p k c", p=P)[:, :, c0:c1]
                    sp.dma_start(dst, src).then_inc(loaded[s].sem, 16)
                    if l == 0 and i == 0:
                        sp.dma_start(C[:, P:], consts[:, P:]).then_inc(inputs, 16)
                        sp.dma_start(rt_w[:, :, :], router.rearrange("(k p) e -> p k e", p=P)).then_inc(inputs, 16)
                wait(sp, out_ok, l, len(WOUT_LOADS) - 1)
                src, done = (moe, FFN_BLOCKS) if l else (ffn, 0)
                turns, rest = (ROUND_TURNS, 0) if l else divmod(FFN_BLOCKS, SLOTS)
                if l:
                    sp.dma_start(ring[:, tail + 2 * D:tail + 2 * D + ROUTE_N], route_consts).then_inc(route_in, 16)
                for s in range(SLOTS):
                    sp.dma_start(slot[s], src[s]).then_inc(block_loaded[s], 16)
                with sp.Fori(1, turns) as i:
                    for s in range(SLOTS):
                        load(s, src, i, done + SLOTS * (i - 1) + s + 1)
                for s in range(rest):
                    sp.wait_ge(hid_used, done + SLOTS * (turns - 1) + s + 1)
                    sp.dma_start(slot[s], src[turns * SLOTS + s]).then_inc(block_loaded[s], 16)
            sp.dma_start(lnf, ln_final).then_inc(lnf_in, 16)
            sp.wait_ge(more_ok, 1)
            overflow = sp.value_load(more[0:1, 0:1], min_val=0, max_val=1)
            with sp.If(overflow > 0):
                with sp.Fori(1, -(-NT // CAP)) as r:
                    with sp.Fori(0, ROUND_TURNS) as i:
                        for s in range(SLOTS):
                            load(s, moe, i, FFN_BLOCKS + SLOTS * (r * ROUND_TURNS + i - 1) + s + 1)
            for t, (t0, n) in enumerate(TILES):
                wait(sp, final_ok, 0, t)
                sp.dma_start(y_out[t0:t0 + n, :], X[0:n, t, :]).then_inc(y_stored, 16)
            sp.wait_ge(y_stored, 48)

        @block.gpsimd
        def _(pool):
            spreads = [0]
            pool.wait_ge(x_loaded, 48)
            for l in range(DEPTH):
                if l:
                    wait(pool, gT_ok, l - 1, 0)
                    wait(pool, SS_ok, l - 1, 1)
                pool.dma_start(cvs[:, :, :], conv_state[l]).then_inc(seq_states.sem, 16)
                pool.dma_start(shs[:, :, :], shift_state[l]).then_inc(seq_states.sem, 16)
                pool.dma_start(w2a2[:, :], rw_w2a2[l]).then_inc(lora_loaded.sem, 16)
                pool.dma_start(g2[:, :, :], rw_g2[l]).then_inc(lora_loaded.sem, 16)
                pool.dma_start(w0[:, :], rw_w0[l:l + 1, :]).then_inc(lora_loaded.sem, 16)
                if l:
                    wait(pool, rt_state_out, l - 1, 0)
                pool.dma_start(SSr[:, :, :], rt_state[l]).then_inc(rt_state_in.sem, 16)
                if l:
                    wait(pool, ss_out, l - 1, 1)
                pool.dma_start(SS[:, :, :, :], dn_state[l]).then_inc(ss_in.sem, 16)
                wait(pool, cvo_ok, l, 0)
                pool.dma_start(conv_out[l], cvo[:, 0, :, :]).then_inc(stored.sem, 16)
                wait(pool, sho_ok, l, 0)
                pool.dma_start(shift_out[l], sho[:, 0, :, :]).then_inc(stored.sem, 16)
                for y, (pp, ssx) in enumerate(((p_dn, s_dn), (p_rw, s_rw))):
                    wait(pool, U_ok, l, y * 5 + 4)
                    if y:
                        wait(pool, natb_ok, l, 2)
                    for p in range(3):
                        if p == 2:
                            b, turn = fills[(l, y, "SS", 0)]
                            pool.wait_ge(bank_full[b], turn + 1)
                        rows = [(0, U[0:32, 2 * p, :]), (1, U[0:32, 2 * p + 1, :])]
                        if y:
                            rows += [(2, nat[0:32, 2, 2 * p, :]), (3, nat[0:32, 2, 2 * p + 1, :])]
                        for k, src in rows:
                            spread(nc.gpsimd, spread_at(y, p, k), src).then_inc(spread_seq, 1)
                            spreads[0] += 1
                        pool.wait_ge(spread_seq, spreads[0])
                        nc.gpsimd.engine_nop().then_inc(UX_ok.sem, 1)
                    if y:
                        b, turn = fills[(l, y, "SS", 2)]
                        pool.wait_ge(bank_full[b], turn + 1)
                        wait(pool, rtk_ok, l, 2)
                        for h in range(RT_H):
                            spread(nc.gpsimd, UX[0:32, h, :, :], sg[0:32, 2, P + h * HD:P + (h + 1) * HD]).then_inc(rtX_ok.sem, 1)
                    wait(pool, S_ok, l, 4 * y + 3)
                    pool.dma_start(pp[l], S[:, y, :, :]).then_inc(stored.sem, 16)
                    wait(pool, SS_ok, l, y)
                    pool.dma_start(ssx[l], SS[:, :, :, :]).then_inc(ss_out.sem, 16)
                    if y == 0:
                        wait(pool, ss_out, l, 0)
                        pool.dma_start(SS[:, :, :, :], rw_state[l]).then_inc(ss_in.sem, 16)
                wait(pool, rtSp_ok, l, 0)
                pool.dma_start(p_rt[l], Sr[:, l, :]).then_inc(stored.sem, 16)
                wait(pool, rtS_ok, l, 0)
                pool.dma_start(s_rt[l], SSr[:, :, :]).then_inc(rt_state_out.sem, 16)
            wait(pool, stored, DEPTH - 1, 4)
            wait(pool, ss_out, DEPTH - 1, 1)
            wait(pool, rt_state_out, DEPTH - 1, 0)


def rows_to(a, rows=P):
    return np.swapaxes(a.reshape(a.shape[:-1] + (-1, rows)), -1, -2)


def kernel(**inp):
    import concourse.bacc as _bacc
    from concourse.bass_utils import run_bass_kernel_spmd as _run

    a = {k: np.asarray(v) for k, v in inp.items()}
    L = DEPTH
    f32 = np.float32

    def padded(x, n):
        out = np.zeros(x.shape[:-1] + (n,), x.dtype)
        out[..., :x.shape[-1]] = x
        return out

    cols = {
        "ln_mix": rows_to(a["ln_mix"]), "ln_ffn": rows_to(a["ln_ffn"]),
        "conv": np.ascontiguousarray(a["dn_conv"].reshape(L, CONV_W, 9, P).transpose(0, 3, 2, 1)).reshape(L, P, 36),
        "dn_norm": np.concatenate([a["dn_norm"]] * 2, 1)[:, :, None],
        "mu": rows_to(padded(a["rw_mu"], 12 * P)), "a0": rows_to(a["rw_a0"]), "kk": rows_to(a["rw_kk"]),
        "ka": rows_to(a["rw_ka"]), "rk": rows_to(a["rw_rk"].reshape(L, -1)), "ln_g": rows_to(a["rw_ln_g"]),
        "ln_b": rows_to(a["rw_ln_b"]), "rt_ln": rows_to(a["rt_ln"]),
        "a_log": np.repeat(a["dn_a_log"][:, None], P, 1), "dt": np.repeat(a["dn_dt_bias"][:, None], P, 1),
    }
    g2 = np.zeros((L, P, 2, 384), f32)
    g2[:, :, 0] = a["rw_g2"][:, :P]
    g2[:, :32, 1] = a["rw_g2"][:, P:]

    def blocks(w1, w3, w2):
        e, d, f = w1.shape
        up = lambda w: w.reshape(e, KD, P, f // FB, FB).transpose(0, 3, 2, 1, 4).reshape(e * f // FB, P, KD * FB)
        down = w2.reshape(e * f // FB, P, D)
        return np.concatenate([up(w1), up(w3), down], 2)

    shift = padded(a["state_rw_shift"], 12 * P).reshape(L, NB, 12, P).transpose(0, 3, 2, 1)
    arrays = {
        "x_in": np.concatenate([a["x_prompt"].reshape(SEQ, D), a["x_sample"].reshape(NB * DS, D)]),
        "consts": constants(),
        "route_consts": route_constants(),
        "pcol": np.concatenate([cols[k] for k, _ in PCOLS], 2),
        "rw_w2a2": np.concatenate([a["rw_w2"], a["rw_a2"]], 1),
        "rw_g2": g2, "rw_w0": a["rw_w0"], "ln_final": np.repeat(a["ln_final"][None], P, 0),
        "router": a["moe_router"][0], "w_in": a["w_in"], "w_out": a["w_out"],
        "ffn": blocks(a["ffn_w1"], a["ffn_w3"], a["ffn_w2"]),
        "moe": blocks(a["moe_w1"][0], a["moe_w3"][0], a["moe_w2"][0]),
        "conv_state": a["state_dn_conv"].reshape(L, NB, PADC, 9, P).transpose(0, 4, 3, 1, 2).reshape(L, P, 9, 24),
        "shift_state": shift,
        "dn_state": a["state_dn"].reshape(L, NB, 3, P, HD).transpose(0, 3, 2, 1, 4),
        "rw_state": a["state_rw"].transpose(0, 1, 2, 4, 3).reshape(L, NB, 3, P, HD).transpose(0, 3, 2, 1, 4),
        "rt_state": a["state_rt"].reshape(L, NB, P, HD).transpose(0, 2, 1, 3),
    }
    outs = {"y_out": (NT, D), "conv_out": (L, P, 9, 27), "shift_out": (L, P, 12, 9), "p_dn": (L, P, 3, HD),
            "p_rw": (L, P, 3, HD), "p_rt": (L, P, HD), "s_dn": (L, P, 3, NB, HD), "s_rw": (L, P, 3, NB, HD),
            "s_rt": (L, P, NB, HD)}
    nc = _bacc.Bacc("TRN2", target_bir_lowering=False, num_devices=1)
    args, given = {}, {}
    for name, x in arrays.items():
        given[name + "_dram"] = np.ascontiguousarray(x)
        args[name] = nc.dram_tensor(name + "_dram", x.shape, F32, kind="ExternalInput").ap()
    for name, shape in outs.items():
        args[name] = nc.dram_tensor(name + "_dram", shape, F32, kind="ExternalOutput").ap()
    trunk(nc, **args)
    r = _run(nc, [given], core_ids=[0]).results[0]
    o = {name: r[name + "_dram"] for name in outs}
    conv = o["conv_out"].reshape(L, P, 9, 9, PADC).transpose(3, 0, 4, 2, 1).reshape(9, L, PADC, 9 * P)
    sh = o["shift_out"].transpose(3, 0, 2, 1).reshape(9, L, 12 * P)[:, :, :1440]
    heads = lambda x: x.transpose(0, 2, 1, 3).reshape(L, H, HD, HD)
    sheads = lambda x: x.transpose(0, 3, 2, 1, 4).reshape(L, NB, H, HD, HD)
    res = (o["y_out"][:SEQ].reshape(1, SEQ, D), o["y_out"][SEQ:].reshape(NB, DS, D),
           conv[0][:, None], heads(o["p_dn"])[:, None], sh[0][:, None],
           heads(o["p_rw"]).swapaxes(-1, -2)[:, None], o["p_rt"].reshape(L, 1, RT_H, RT_K, HD),
           conv[1:].transpose(1, 0, 2, 3), sheads(o["s_dn"]), sh[1:].transpose(1, 0, 2),
           sheads(o["s_rw"]).swapaxes(-1, -2), o["s_rt"].transpose(0, 2, 1, 3).reshape(L, NB, RT_H, RT_K, HD))
    return tuple(np.ascontiguousarray(x) for x in res)
```
